# Optimizing a Trainium2 kernel written in Bass

```python
import math
import jax, jax.numpy as jnp
from jax import lax
import numpy as np

D_MODEL = 1024
BATCH = 1
SEQ = 512
DEPTH = 2

HEAD_DIM = 64
A_HEADS = 4
DILATED_PATTERNS = ((128, 1), (512, 4), (2048, 16))
WIN_BLOCK = 64
B_HEADS = 8
MLA_Q_LORA = 384
MLA_KV_LORA = 256
MLA_NOPE = 64
MLA_ROPE = 32
MLA_V = 64
ROPE_THETA = 10000.0
C_HEADS = 4
DIFF_QK = 32
DIFF_V = 64
D_FF = 2816
QUERY_BLOCK = 128
EPS = 1e-6
NEG_INF = -1e30

A_COLS = 3 * A_HEADS * HEAD_DIM
B_COLS = MLA_Q_LORA + MLA_KV_LORA + MLA_ROPE
C_COLS = 2 * (C_HEADS * 2 * DIFF_QK) + C_HEADS * DIFF_V
N_IN = A_COLS + B_COLS + C_COLS
D_MIX = A_HEADS * HEAD_DIM + B_HEADS * MLA_V + C_HEADS * DIFF_V


def rmsnorm(x, gain):
    xf = x.astype(jnp.float32)
    y = xf * lax.rsqrt(jnp.mean(xf * xf, axis=-1, keepdims=True) + EPS)
    return y.astype(x.dtype) * gain

def swiglu(h, w_gate, w_up, w_down):
    return (jax.nn.silu(h @ w_gate) * (h @ w_up)) @ w_down

def alibi_slopes():
    n = A_HEADS + C_HEADS
    s = jnp.asarray([2.0 ** (-8.0 * (i + 1) / n) for i in range(n)], dtype=jnp.float32)
    return s[0::2], s[1::2]

def rope(t, pos):
    half = t.shape[-1] // 2
    inv = ROPE_THETA ** (-jnp.arange(half, dtype=jnp.float32) / half)
    ang = pos.astype(jnp.float32)[..., None, None] * inv
    cos, sin = jnp.cos(ang), jnp.sin(ang)
    tf = t.astype(jnp.float32)
    t1, t2 = tf[..., :half], tf[..., half:]
    return jnp.concatenate([t1 * cos - t2 * sin, t2 * cos + t1 * sin], axis=-1).astype(t.dtype)

def dilated_branch(q, k, v, pos, slopes, dilation, radius):
    B, S, H, E = q.shape
    L = S // dilation

    def to_res(t):
        return t.reshape(B, L, dilation, H, E).transpose(0, 2, 3, 1, 4)

    qr, kr, vr = to_res(q), to_res(k), to_res(v)
    pr = pos.reshape(B, L, dilation).transpose(0, 2, 1)
    nb = -(-L // WIN_BLOCK)
    Lp = nb * WIN_BLOCK
    K = WIN_BLOCK + 2 * radius
    qr = jnp.pad(qr, ((0, 0), (0, 0), (0, 0), (0, Lp - L), (0, 0)))
    kpad = ((0, 0), (0, 0), (0, 0), (radius, radius + Lp - L), (0, 0))
    kr, vr = jnp.pad(kr, kpad), jnp.pad(vr, kpad)
    pq = jnp.pad(pr, ((0, 0), (0, 0), (0, Lp - L)))
    pk = jnp.pad(pr, ((0, 0), (0, 0), (radius, radius + Lp - L)))
    slab = jnp.arange(nb)[:, None] * WIN_BLOCK + jnp.arange(K)[None, :]
    ks = jnp.take(kr, slab, axis=3)
    vs = jnp.take(vr, slab, axis=3)
    pks = jnp.take(pk, slab, axis=2)
    qb = qr.reshape(B, dilation, H, nb, WIN_BLOCK, E)
    pqb = pq.reshape(B, dilation, nb, WIN_BLOCK)
    off = jnp.arange(K)[None, :] - radius - jnp.arange(WIN_BLOCK)[:, None]
    kabs = slab - radius
    valid = (jnp.abs(off) <= radius)[None] & ((kabs >= 0) & (kabs < L))[:, None, :]
    sc = jnp.einsum('bdhnqe,bdhnke->bdhnqk', qb, ks).astype(jnp.float32) * (E ** -0.5)
    dist = jnp.abs(pqb[..., :, None] - pks[..., None, :]).astype(jnp.float32)
    sc = sc - slopes[None, None, :, None, None, None] * dist[:, :, None]
    sc = jnp.where(valid, sc, NEG_INF)
    m = jnp.max(sc, axis=-1)
    p = jnp.exp(sc - m[..., None])
    s = jnp.sum(p, axis=-1)
    o = jnp.einsum('bdhnqk,bdhnke->bdhnqe', p, vs.astype(jnp.float32)) / s[..., None]
    o = o.reshape(B, dilation, H, Lp, E)[:, :, :, :L].transpose(0, 3, 1, 2, 4).reshape(B, S, H, E)
    m = m.reshape(B, dilation, H, Lp)[..., :L].transpose(0, 3, 1, 2).reshape(B, S, H)
    s = s.reshape(B, dilation, H, Lp)[..., :L].transpose(0, 3, 1, 2).reshape(B, S, H)
    return o, m, s

def dilated_attention(q, k, v, pos, slopes):
    outs = [dilated_branch(q, k, v, pos, slopes, d, w // 2 // d) for (w, d) in DILATED_PATTERNS]
    m_all = jnp.max(jnp.stack([m for (_, m, _) in outs]), axis=0)
    wts = [s * jnp.exp(m - m_all) for (_, m, s) in outs]
    num = sum(w[..., None] * o for w, (o, _, _) in zip(wts, outs))
    return num / sum(wts)[..., None]

def mla_attention(q, k, v):
    B, H, S, Dk = q.shape
    nq = S // QUERY_BLOCK
    scale = Dk ** -0.5
    qb = q.reshape(B, H, nq, QUERY_BLOCK, Dk).transpose(2, 0, 1, 3, 4)
    vf = v.astype(jnp.float32)

    def one(qi):
        sc = jnp.einsum('bhqe,bhke->bhqk', qi, k).astype(jnp.float32) * scale
        return jnp.einsum('bhqk,bhkv->bhqv', jax.nn.softmax(sc, axis=-1), vf)

    o = lax.map(one, qb)
    return o.transpose(1, 0, 3, 2, 4).reshape(B, S, H, v.shape[-1])

def diff_attention(q, k, v, pos, slopes, lam):
    B, H, _, S, E = q.shape
    nq = S // QUERY_BLOCK
    scale = E ** -0.5
    qb = q.reshape(B, H, 2, nq, QUERY_BLOCK, E).transpose(3, 0, 1, 2, 4, 5)
    pqb = pos.reshape(B, nq, QUERY_BLOCK).transpose(1, 0, 2)
    vf = v.astype(jnp.float32)

    def one(args):
        qi, pi = args
        sc = jnp.einsum('bhcqe,bhcke->bhcqk', qi, k).astype(jnp.float32) * scale
        dist = jnp.abs(pi[:, :, None] - pos[:, None, :]).astype(jnp.float32)
        sc = sc - slopes[None, :, None, None, None] * dist[:, None, None]
        a = jax.nn.softmax(sc, axis=-1)
        return jnp.einsum('bhqk,bhkv->bhqv', a[:, :, 0] - lam * a[:, :, 1], vf)

    o = lax.map(one, (qb, pqb))
    return o.transpose(1, 0, 3, 2, 4).reshape(B, S, H, v.shape[-1])

def token_mixing(h, pos, w_in, mla_q_norm, mla_w_uq, mla_kv_norm, mla_w_ukv,
                 lq1, lk1, lq2, lk2, diff_head_norm, w_out, layer_idx):
    B, S, _ = h.shape
    slopes_a, slopes_c = alibi_slopes()
    proj = h @ w_in
    a_part, b_part, c_part = jnp.split(proj, [A_COLS, A_COLS + B_COLS], axis=-1)

    qa, ka, va = [t.reshape(B, S, A_HEADS, HEAD_DIM) for t in jnp.split(a_part, 3, axis=-1)]
    out_a = dilated_attention(qa, ka, va, pos, slopes_a).astype(h.dtype)

    c_q, c_kv, k_pe = jnp.split(b_part, [MLA_Q_LORA, MLA_Q_LORA + MLA_KV_LORA], axis=-1)
    qfull = (rmsnorm(c_q, mla_q_norm) @ mla_w_uq).reshape(B, S, B_HEADS, MLA_NOPE + MLA_ROPE)
    q_b = jnp.concatenate([qfull[..., :MLA_NOPE], rope(qfull[..., MLA_NOPE:], pos)], axis=-1)
    kv = (rmsnorm(c_kv, mla_kv_norm) @ mla_w_ukv).reshape(B, S, B_HEADS, MLA_NOPE + MLA_V)
    k_rot = jnp.broadcast_to(rope(k_pe[:, :, None, :], pos), (B, S, B_HEADS, MLA_ROPE))
    k_b = jnp.concatenate([kv[..., :MLA_NOPE], k_rot], axis=-1)
    v_b = kv[..., MLA_NOPE:]
    out_b = mla_attention(q_b.transpose(0, 2, 1, 3), k_b.transpose(0, 2, 1, 3),
                          v_b.transpose(0, 2, 1, 3)).astype(h.dtype)

    nqk = C_HEADS * 2 * DIFF_QK
    q_c, k_c, v_c = jnp.split(c_part, [nqk, 2 * nqk], axis=-1)
    q_c = q_c.reshape(B, S, C_HEADS, 2, DIFF_QK).transpose(0, 2, 3, 1, 4)
    k_c = k_c.reshape(B, S, C_HEADS, 2, DIFF_QK).transpose(0, 2, 3, 1, 4)
    v_c = v_c.reshape(B, S, C_HEADS, DIFF_V).transpose(0, 2, 1, 3)
    lam_init = 0.8 - 0.6 * math.exp(-0.3 * layer_idx)
    lam = (jnp.exp(jnp.sum(lq1.astype(jnp.float32) * lk1.astype(jnp.float32)))
           - jnp.exp(jnp.sum(lq2.astype(jnp.float32) * lk2.astype(jnp.float32))) + lam_init)
    o_c = diff_attention(q_c, k_c, v_c, pos, slopes_c, lam).astype(h.dtype)
    out_c = rmsnorm(o_c, diff_head_norm) * (1.0 - lam_init)

    mixed = jnp.concatenate([out_a.reshape(B, S, -1), out_b.reshape(B, S, -1),
                             out_c.reshape(B, S, -1)], axis=-1)
    return mixed @ w_out

def first_inputs(seed: int = 0) -> dict:
    key = jax.random.key(seed)
    ks = iter(jax.random.split(key, 32))
    f32 = jnp.float32

    def dense(shape, fan_in):
        return jax.random.normal(next(ks), shape, f32) * (fan_in ** -0.5)

    def gain(shape):
        return 1.0 + 0.02 * jax.random.normal(next(ks), shape, f32)

    return {
        "x": jax.random.normal(next(ks), (BATCH, SEQ, D_MODEL), f32),
        "positions": jnp.broadcast_to(jnp.arange(SEQ, dtype=jnp.int32), (BATCH, SEQ)),
        "ffn1_norm": gain((DEPTH, D_MODEL)),
        "ffn1_w_gate": dense((DEPTH, D_MODEL, D_FF), D_MODEL),
        "ffn1_w_up": dense((DEPTH, D_MODEL, D_FF), D_MODEL),
        "ffn1_w_down": dense((DEPTH, D_FF, D_MODEL), D_FF),
        "mix_norm": gain((DEPTH, D_MODEL)),
        "w_in": dense((DEPTH, D_MODEL, N_IN), D_MODEL),
        "mla_q_norm": gain((DEPTH, MLA_Q_LORA)),
        "mla_w_uq": dense((DEPTH, MLA_Q_LORA, B_HEADS * (MLA_NOPE + MLA_ROPE)), MLA_Q_LORA),
        "mla_kv_norm": gain((DEPTH, MLA_KV_LORA)),
        "mla_w_ukv": dense((DEPTH, MLA_KV_LORA, B_HEADS * (MLA_NOPE + MLA_V)), MLA_KV_LORA),
        "diff_lambda_q1": 0.1 * jax.random.normal(next(ks), (DEPTH, DIFF_QK), f32),
        "diff_lambda_k1": 0.1 * jax.random.normal(next(ks), (DEPTH, DIFF_QK), f32),
        "diff_lambda_q2": 0.1 * jax.random.normal(next(ks), (DEPTH, DIFF_QK), f32),
        "diff_lambda_k2": 0.1 * jax.random.normal(next(ks), (DEPTH, DIFF_QK), f32),
        "diff_head_norm": gain((DEPTH, DIFF_V)),
        "w_out": dense((DEPTH, D_MIX, D_MODEL), D_MIX),
        "ffn2_norm": gain((DEPTH, D_MODEL)),
        "ffn2_w_gate": dense((DEPTH, D_MODEL, D_FF), D_MODEL),
        "ffn2_w_up": dense((DEPTH, D_MODEL, D_FF), D_MODEL),
        "ffn2_w_down": dense((DEPTH, D_FF, D_MODEL), D_FF),
        "final_norm": gain((D_MODEL,)),
    }

def first_block(x, positions, ffn1_norm, ffn1_w_gate, ffn1_w_up, ffn1_w_down, mix_norm, w_in,
              mla_q_norm, mla_w_uq, mla_kv_norm, mla_w_ukv, diff_lambda_q1, diff_lambda_k1,
              diff_lambda_q2, diff_lambda_k2, diff_head_norm, w_out, ffn2_norm, ffn2_w_gate,
              ffn2_w_up, ffn2_w_down, final_norm):
    for l in range(DEPTH):
        x = x + 0.5 * swiglu(rmsnorm(x, ffn1_norm[l]), ffn1_w_gate[l], ffn1_w_up[l], ffn1_w_down[l])
        x = x + token_mixing(rmsnorm(x, mix_norm[l]), positions, w_in[l], mla_q_norm[l], mla_w_uq[l],
                             mla_kv_norm[l], mla_w_ukv[l], diff_lambda_q1[l], diff_lambda_k1[l],
                             diff_lambda_q2[l], diff_lambda_k2[l], diff_head_norm[l], w_out[l], l)
        x = x + 0.5 * swiglu(rmsnorm(x, ffn2_norm[l]), ffn2_w_gate[l], ffn2_w_up[l], ffn2_w_down[l])
    return rmsnorm(x, final_norm)


DEPTH_2 = 1

PLE_DIM = 256
NORM_EPS = 1e-6
S5_WIDTH = 512
S5_GROUP = 16
S5_GROUPS = S5_WIDTH // S5_GROUP
S5_STATE = 64
S5_DT_MIN = 1e-3
S5_DT_MAX = 1e-1
LRU_WIDTH = 1280
LRU_HEADS = 10
LRU_HEAD_DIM = LRU_WIDTH // LRU_HEADS
LRU_C = 8.0
CONV_WIDTH = 4
IN_SPLITS = (
    S5_WIDTH,
    2 * S5_WIDTH,
    2 * S5_WIDTH + LRU_WIDTH,
    2 * S5_WIDTH + 2 * LRU_WIDTH,
    2 * S5_WIDTH + 2 * LRU_WIDTH + D_MODEL,
)
IN_COLS = 2 * S5_WIDTH + 2 * LRU_WIDTH + 2 * D_MODEL


def rms_norm(x, g):
    xf = x.astype(jnp.float32)
    y = xf * lax.rsqrt(jnp.mean(xf * xf, axis=-1, keepdims=True) + NORM_EPS)
    return (y * g.astype(jnp.float32)).astype(x.dtype)

def _linear_combine(e1, e2):
    a1, b1 = e1
    a2, b2 = e2
    return (a1 * a2, a2 * b1 + b2)

def s5_ssm(u, a_re, a_im, log_dt, b_re, b_im, c_re, c_im, d_skip):
    f32 = jnp.float32
    bsz, seqlen, _ = u.shape
    uf = u.astype(f32)
    ug = uf.reshape(bsz, seqlen, S5_GROUPS, S5_GROUP)
    lam = lax.complex(a_re.astype(f32), a_im.astype(f32))
    dt = jnp.exp(log_dt.astype(f32))[:, None]
    a_bar = jnp.exp(lam * dt)
    zoh = (a_bar - 1.0) / lam
    b = lax.complex(b_re.astype(f32), b_im.astype(f32))
    b_bar = zoh[..., None] * b
    bu = lax.complex(jnp.einsum('blgc,gnc->lbgn', ug, jnp.real(b_bar)),
                     jnp.einsum('blgc,gnc->lbgn', ug, jnp.imag(b_bar)))
    a_seq = jnp.broadcast_to(a_bar[None, None], (seqlen, 1, S5_GROUPS, S5_STATE))
    _, states = lax.associative_scan(_linear_combine, (a_seq, bu), axis=0)
    y = (jnp.einsum('lbgn,gcn->blgc', jnp.real(states), c_re.astype(f32))
         - jnp.einsum('lbgn,gcn->blgc', jnp.imag(states), c_im.astype(f32)))
    y = y.reshape(bsz, seqlen, S5_WIDTH) + d_skip.astype(f32) * uf
    return y.astype(u.dtype)

def causal_depthwise_conv(x, w, b):
    y = lax.conv_general_dilated(
        x, w[:, None, :].astype(x.dtype), window_strides=(1,),
        padding=[(CONV_WIDTH - 1, 0)],
        dimension_numbers=('NWC', 'WIO', 'NWC'),
        feature_group_count=x.shape[-1])
    return y + b

def rg_lru(x, w_a, b_a, w_x, b_x, lam):
    f32 = jnp.float32
    bsz, seqlen, _ = x.shape
    xf = x.astype(f32)
    xh = xf.reshape(bsz, seqlen, LRU_HEADS, LRU_HEAD_DIM)
    r = jax.nn.sigmoid(jnp.einsum('blhi,hij->blhj', xh, w_a.astype(f32)).reshape(bsz, seqlen, LRU_WIDTH)
                       + b_a.astype(f32))
    i = jax.nn.sigmoid(jnp.einsum('blhi,hij->blhj', xh, w_x.astype(f32)).reshape(bsz, seqlen, LRU_WIDTH)
                       + b_x.astype(f32))
    log_a = -LRU_C * r * jax.nn.softplus(-lam.astype(f32))
    a = jnp.exp(log_a)
    mult = jnp.sqrt(-jnp.expm1(2.0 * log_a))
    _, h = lax.associative_scan(_linear_combine, (a, mult * (i * xf)), axis=1)
    return h.astype(x.dtype)

def second_inputs(seed: int = 0) -> dict:
    key = jax.random.key(seed)
    ks = jax.random.split(key, 32)
    f32 = jnp.float32

    def nrm(k, shape, scale):
        return jax.random.normal(k, shape, f32) * scale

    L, D, G, N, C, HD = DEPTH_2, D_MODEL, S5_GROUPS, S5_STATE, S5_GROUP, LRU_HEAD_DIM
    x = nrm(ks[0], (BATCH, SEQ, D), 1.0)
    p = nrm(ks[1], (DEPTH_2, BATCH, SEQ, PLE_DIM), 1.0)
    g_pre = 1.0 + nrm(ks[2], (L, D), 0.05)
    w_in = nrm(ks[3], (L, D, IN_COLS), D ** -0.5)
    s5_a_re = -0.5 + nrm(ks[4], (L, G, N), 0.01)
    s5_a_im = math.pi * jnp.arange(N, dtype=f32)[None, None, :] + nrm(ks[5], (L, G, N), 0.01)
    s5_log_dt = jax.random.uniform(ks[6], (L, G), f32, math.log(S5_DT_MIN), math.log(S5_DT_MAX))
    s5_b_re = nrm(ks[7], (L, G, N, C), C ** -0.5)
    s5_b_im = nrm(ks[8], (L, G, N, C), C ** -0.5)
    s5_c_re = nrm(ks[9], (L, G, C, N), N ** -0.5)
    s5_c_im = nrm(ks[10], (L, G, C, N), N ** -0.5)
    s5_d = nrm(ks[11], (L, S5_WIDTH), 1.0)
    w_glu = nrm(ks[12], (L, S5_WIDTH, 2 * S5_WIDTH), S5_WIDTH ** -0.5)
    w_bs = nrm(ks[13], (L, S5_WIDTH, D), S5_WIDTH ** -0.5)
    conv_w = nrm(ks[14], (L, CONV_WIDTH, LRU_WIDTH), CONV_WIDTH ** -0.5)
    conv_b = nrm(ks[15], (L, LRU_WIDTH), 0.01)
    lru_w_a = nrm(ks[16], (L, LRU_HEADS, HD, HD), HD ** -0.5)
    lru_b_a = nrm(ks[17], (L, LRU_WIDTH), 0.01)
    lru_w_x = nrm(ks[18], (L, LRU_HEADS, HD, HD), HD ** -0.5)
    lru_b_x = nrm(ks[19], (L, LRU_WIDTH), 0.01)
    a_c = jax.random.uniform(ks[20], (L, LRU_WIDTH), f32, 0.9, 0.999)
    sig = a_c ** (1.0 / LRU_C)
    lru_lambda = jnp.log(sig) - jnp.log1p(-sig)
    w_bl = nrm(ks[21], (L, LRU_WIDTH, D), LRU_WIDTH ** -0.5)
    w_out = nrm(ks[22], (L, D, D), D ** -0.5)
    g_post = 1.0 + nrm(ks[23], (L, D), 0.05)
    w_ple = nrm(ks[24], (L, PLE_DIM, D), PLE_DIM ** -0.5)
    w_ple_gate = nrm(ks[25], (L, D, D), D ** -0.5)
    return {
        'x': x, 'p': p, 'g_pre': g_pre, 'w_in': w_in,
        's5_a_re': s5_a_re, 's5_a_im': s5_a_im, 's5_log_dt': s5_log_dt,
        's5_b_re': s5_b_re, 's5_b_im': s5_b_im, 's5_c_re': s5_c_re, 's5_c_im': s5_c_im,
        's5_d': s5_d, 'w_glu': w_glu, 'w_bs': w_bs,
        'conv_w': conv_w, 'conv_b': conv_b,
        'lru_w_a': lru_w_a, 'lru_b_a': lru_b_a, 'lru_w_x': lru_w_x, 'lru_b_x': lru_b_x,
        'lru_lambda': lru_lambda, 'w_bl': w_bl, 'w_out': w_out, 'g_post': g_post,
        'w_ple': w_ple, 'w_ple_gate': w_ple_gate,
    }

def second_block(x, p, g_pre, w_in, s5_a_re, s5_a_im, s5_log_dt, s5_b_re, s5_b_im,
              s5_c_re, s5_c_im, s5_d, w_glu, w_bs, conv_w, conv_b,
              lru_w_a, lru_b_a, lru_w_x, lru_b_x, lru_lambda, w_bl, w_out, g_post,
              w_ple, w_ple_gate):
    for i in range(DEPTH_2):
        h = rms_norm(x, g_pre[i])
        proj = h @ w_in[i]
        s5_x, s5_g, lru_x, lru_g, gate_s, gate_l = jnp.split(proj, IN_SPLITS, axis=-1)

        y_s = s5_ssm(s5_x, s5_a_re[i], s5_a_im[i], s5_log_dt[i], s5_b_re[i], s5_b_im[i],
                     s5_c_re[i], s5_c_im[i], s5_d[i])
        glu_a, glu_b = jnp.split(jax.nn.gelu(y_s) @ w_glu[i], 2, axis=-1)
        y_s = glu_a * jax.nn.sigmoid(glu_b) * jax.nn.silu(s5_g)
        z_s = y_s @ w_bs[i]

        c = causal_depthwise_conv(lru_x, conv_w[i], conv_b[i])
        y_l = rg_lru(c, lru_w_a[i], lru_b_a[i], lru_w_x[i], lru_b_x[i], lru_lambda[i])
        z_l = (y_l * jax.nn.silu(lru_g)) @ w_bl[i]

        merged = jax.nn.sigmoid(gate_s) * z_s + jax.nn.sigmoid(gate_l) * z_l
        x = x + rms_norm(merged @ w_out[i], g_post[i])

        x = x + (p[i] @ w_ple[i]) * jax.nn.sigmoid(x @ w_ple_gate[i])
    return x


def setup_inputs(seed=0):
    out = dict(first_inputs(seed))
    for name, value in second_inputs(seed + 1).items():
        if name != "x":
            out[name + "_2"] = value
    return out


def reference(
    x, positions, ffn1_norm, ffn1_w_gate, ffn1_w_up, ffn1_w_down, mix_norm, w_in, mla_q_norm,
    mla_w_uq, mla_kv_norm, mla_w_ukv, diff_lambda_q1, diff_lambda_k1, diff_lambda_q2,
    diff_lambda_k2, diff_head_norm, w_out, ffn2_norm, ffn2_w_gate, ffn2_w_up, ffn2_w_down,
    final_norm, p_2, g_pre_2, w_in_2, s5_a_re_2, s5_a_im_2, s5_log_dt_2, s5_b_re_2, s5_b_im_2,
    s5_c_re_2, s5_c_im_2, s5_d_2, w_glu_2, w_bs_2, conv_w_2, conv_b_2, lru_w_a_2, lru_b_a_2,
    lru_w_x_2, lru_b_x_2, lru_lambda_2, w_bl_2, w_out_2, g_post_2, w_ple_2, w_ple_gate_2,
):
    x = first_block(
        x, positions, ffn1_norm, ffn1_w_gate, ffn1_w_up, ffn1_w_down, mix_norm, w_in,
        mla_q_norm, mla_w_uq, mla_kv_norm, mla_w_ukv, diff_lambda_q1, diff_lambda_k1,
        diff_lambda_q2, diff_lambda_k2, diff_head_norm, w_out, ffn2_norm, ffn2_w_gate,
        ffn2_w_up, ffn2_w_down, final_norm,
    )
    return second_block(
        x, p_2, g_pre_2, w_in_2, s5_a_re_2, s5_a_im_2, s5_log_dt_2, s5_b_re_2, s5_b_im_2,
        s5_c_re_2, s5_c_im_2, s5_d_2, w_glu_2, w_bs_2, conv_w_2, conv_b_2, lru_w_a_2, lru_b_a_2,
        lru_w_x_2, lru_b_x_2, lru_lambda_2, w_bl_2, w_out_2, g_post_2, w_ple_2, w_ple_gate_2,
    )


_drawn_inputs = setup_inputs


def setup_inputs(seed=0):
    import zlib

    import numpy as np

    out = dict(_drawn_inputs(seed))
    spreads = {}
    factors = {'ffn1_norm': 3.595,
     'mla_q_norm': 8.0,
     'mla_kv_norm': 8.0,
     'diff_lambda_k2': 3.095,
     'diff_head_norm': 3.249,
     'ffn2_norm': 4.875,
     's5_a_re_2': 64.0,
     's5_b_re_2': 2.918,
     's5_b_im_2': 2.981,
     's5_c_re_2': 2.914,
     's5_c_im_2': 2.802,
     'lru_b_a_2': 46.61,
     'lru_b_x_2': 26.309}
    for name, (base, spread) in spreads.items():
        noise = np.random.default_rng([zlib.crc32(name.encode()), seed]).standard_normal(out[name].shape)
        drawn = base * np.exp(spread * noise) if base else spread * noise
        out[name] = __import__('jax').numpy.asarray(drawn.astype(out[name].dtype))
    for name, factor in factors.items():
        out[name] = (out[name] * factor).astype(out[name].dtype)
    return out
```

```python
from contextlib import ExitStack
import math

import numpy as np

import concourse.bass as bass
from concourse import mybir

F32 = mybir.dt.float32
F32R = mybir.dt.float32r
I32 = mybir.dt.int32
ACT = mybir.ActivationFunctionType
ALU = mybir.AluOpType
AX = mybir.AxisListType

P = 128
T = 512
D = 1024
NM = D // P
DEPTH = 2
D_FF = 2816
NF = D_FF // P
NT = T // P
HEADS_A, HEADS_B, HEADS_C = 4, 8, 4
NOPE, ROPE, V_DIM, DIFF_QK = 64, 32, 64, 32
Q_LORA, KV_LORA = 384, 256
A_COLS = 3 * HEADS_A * 64
B_COLS = Q_LORA + KV_LORA + ROPE
EPS = 1e-6
MAPS_C = 2 * HEADS_C
FAR = 1e30

BLOCKS = 16
SLOT = BLOCKS * P
ORD = [4, 5, 6, 7, 0, 1, 2, 3]
SS_BANK = ORD[0]

UP_SLOTS = NF
DOWN_SLOTS = NF // 2
FFN_SLOTS = UP_SLOTS + DOWN_SLOTS
MIX_SLOTS = 16
LAYER_SLOTS = 2 * FFN_SLOTS + MIX_SLOTS
MIX_AT = FFN_SLOTS
FFN2_AT = FFN_SLOTS + MIX_SLOTS

SQ_LAYER = 3 * NM + 2

TILES = [1] * (FFN_SLOTS - 1) + [NM] + [2] * 7 + [1, 4, 4, 4, 8] + [2] * 4 + [1] * (FFN_SLOTS - 1) + [NM]
EARLIER = [sum(n - 1 for n in TILES[:s]) for s in range(LAYER_SLOTS + 1)]

UNITS = ([("c", h, c, q) for h in range(HEADS_C) for q in range(NT) for c in range(2)]
         + [("b", h, 0, q) for h in range(HEADS_B) for q in range(NT)]
         + [("a", h, 0, q) for h in range(HEADS_A) for q in range(NT)])
BIASED = [u for u, (kind, *_) in enumerate(UNITS) if kind != "b"]
TURNS = [u for u, (kind, _, c, _) in enumerate(UNITS) if kind != "c" or c == 1]
HEADS = [UNITS[TURNS[NT * g]][:2] for g in range(len(TURNS) // NT)]
PAIR_TILE = [6, 7, 2, 3, 4, 5, 0, 1]
SLOPES = [2.0 ** (-8.0 * (i + 1) / (HEADS_A + HEADS_C)) for i in range(HEADS_A + HEADS_C)]
SCALE = {"a": 64 ** -0.5, "b": (NOPE + ROPE) ** -0.5, "c": DIFF_QK ** -0.5}
LAM_INIT = [0.8 - 0.6 * math.exp(-0.3 * layer) for layer in range(DEPTH)]
DVE_STEPS = 136
MAGIC = 1.5 * 2.0 ** 23
TURN_HI = 6.28125
TURN_LO = 2 * math.pi - 6.28125
PI_DOWN = 3.1415925
OC_NORM_AT = 37
LOW_RANK_GAINS = 8 * NM
C_GAINS = LOW_RANK_GAINS + 5 * DEPTH
PI = math.pi
D_DECAY, D_ANGLE, D_LAM, D_TABLES = 2, 6, 8, 34


S5_TILES, STATES, S5_PAIRS = 4, 64, 16
LRU_TILES, CONV = 10, 4
PAD = CONV - 1
PLE_TILES = 2
U_AT, LRU_X_AT, LRU_G_AT, S5_G_AT, GATE_L_AT, LRU_OUT_AT = 0, 2, 7, 12, 14, 18
GATE_S_AT, GLU_AT, S5_OUT_AT, OUT_AT, PLE_AT, PLE_GATE_AT, SLOTS_2 = 23, 27, 29, 31, 35, 36, 40
D_SKIP, CONV_W, CONV_B, B_A, B_X, LAM, G_POST = 0, 4, 44, 54, 64, 74, 84
S5_FROM = 4
S5_STEPS = S5_PAIRS + 3
LRU_FROM = 2 * GATE_L_AT
LRU_STEPS = LRU_TILES + 2
PLE_BANKS = [5, 6, 7, 0, 1, 2, 3, 4]
TURN = 6.283185


class Signal:

    def __init__(self, sem, per_layer=0):
        self.sem, self.per_layer = sem, per_layer

    def at(self, layer, k):
        return layer * self.per_layer + k if self.per_layer else k


def build(nc, a):
    ctx = ExitStack()
    with ctx:
        def sb(name, shape, dt=F32, where=ctx):
            return where.enter_context(nc.sbuf_tensor(name, shape, dt))

        def signal(name, per_layer=0):
            return Signal(ctx.enter_context(nc.semaphore(name)), per_layer)

        x = sb("x", [P, NM, T])
        raw = [sb(f"raw{i}", [P, SLOT]) for i in range(2)]
        sq = sb("sq", [P, 2, T])
        tmp = sb("tmp", [P, 2, T])
        bias_ring = sb("bias_ring", [P, 4, T])
        mats = sb("mats", [P, 4, P])
        cols = sb("cols", [P, a["cols"].shape[1]])
        cols2 = sb("cols2", [P, a["cols2"].shape[1]])
        lru_s = sb("lru_s", [P, 4, LRU_TILES])
        gains = sb("gains", [P, a["gains"].shape[1]])
        lam_s = sb("lam_s", [P, 8])
        nlam = sb("nlam", [P, DEPTH])
        gain_c = sb("gain_c", [P, DEPTH])
        wide = sb("wide", [P, 2, T])
        dist = bias_ring
        mneg = sb("mneg", [P, 4])
        rsum = sb("rsum", [P, 4])
        rinv = sb("rinv", [P, 8])
        atmp, rstd = sq[:, 0, :], sq[:, 1, :]
        sil = tmp
        ident, ones, ones64, spread = (mats[:, i, :] for i in range(4))
        eps = cols[:, 0:1]

        with ExitStack() as own:
            w_hi = sb("w_hi", [P, 2, SLOT], F32R, own)
            w_lo = sb("w_lo", [P, 2, SLOT], F32R, own)
        own = ctx.enter_context(ExitStack())
        pt = sb("pt", [P, 2, NT, T], F32, own)
        probs = sb("probs", [P, 4, T], F32, own)
        negs = sb("negs", [P, 4, T], F32, own)
        with ExitStack() as own:
            h_hi = sb("h_hi", [P, NM, T], F32R, own)
            h_lo = sb("h_lo", [P, NM, T], F32R, own)
        own = ctx.enter_context(ExitStack())
        mix_hi = sb("mix_hi", [P, NM, T], F32R, own)
        mix_lo = sb("mix_lo", [P, NM, T], F32R, own)
        with ExitStack() as own:
            a_hi = sb("a_hi", [P, NF, T], F32R, own)
            a_lo = sb("a_lo", [P, NF, T], F32R, own)
        with ExitStack() as own:
            pos_i = sb("pos_i", [P, T], I32, own)
            pos_r = sb("pos_r", [P, T], F32, own)
            pcol_i = sb("pcol_i", [P, NT], I32, own)
            pcol = sb("pcol", [P, NT], F32, own)
            rot = sb("rot", [P, 4, T], F32, own)
            table2 = sb("table2", [P, 2, T], F32, own)
            lamv = sb("lamv", [P, DEPTH, 4, DIFF_QK], F32, own)
            used = 2 * T + 2 * NT + 6 * T + DEPTH * 4 * DIFF_QK
            sb("unused", [P, 2 * NF * T - used - (2 * T - P)], F32, own)
            reach = sb("reach", [P, 2 * T - P], F32, own)
        own = ctx.enter_context(ExitStack())
        qk = sb("qk", [P, 8, T], F32, own)
        cn_hi = sb("cn_hi", [P, 5, T], F32R, own)
        cn_lo = sb("cn_lo", [P, 5, T], F32R, own)
        v_ac = sb("v_ac", [P, NT, T], F32, own)
        v_b = sb("v_b", [P, NT, T], F32, own)
        cs = sb("cs", [P, 2, T], F32, own)
        q_b = sb("q_b", [P, HEADS_B, T], F32, own)
        k_b = sb("k_b", [P, HEADS_B, T], F32, own)
        c_raw, k_prod = q_b[:, 0:5, :], q_b[:, 5, :]
        c_sq, c_rstd = k_b[:, 0:5, :], k_b[:, 5:7, :]

        own.close()

        def region(size, *parts):
            got = []
            for part in parts:
                with ExitStack() as own:
                    got += [sb(name, shape, dt, own) for name, shape, dt in part]
                    used = sum(int(np.prod(shape[1:])) for _, shape, _ in part)
            keep = ctx.enter_context(ExitStack())
            sb("held_by_" + got[0].name, [P, size], F32, keep)
            assert used <= size
            return got

        s5p, s5w, tidx, s5b, s5c_in, s5c, gl = region(
            NM * T, [("s5p", [P, 3, S5_PAIRS], F32), ("s5w", [P, 24, S5_PAIRS], F32), ("tidx", [P, T], F32),
                     ("s5b", [P, S5_TILES, 2, P], F32), ("s5c_in", [P, 2, S5_PAIRS * 32], F32),
                     ("s5c", [P, 2, S5_PAIRS * 32], F32)],
            [("gl", [P, NM, T], F32)])
        u, p_hi, p_lo = region(S5_TILES * T, [("u", [P, S5_TILES, T], F32)],
                               [("p_hi", [P, PLE_TILES, T], F32R), ("p_lo", [P, PLE_TILES, T], F32R)])
        lrux, yl_hi, yl_lo, g_hi, g_lo = region(
            LRU_TILES * (T + 4), [("lrux", [P, LRU_TILES, T + 4], F32)],
            [("yl_hi", [P, 2, T], F32R), ("yl_lo", [P, 2, T], F32R)],
            [("g_hi", [P, S5_TILES, T], F32R), ("g_lo", [P, S5_TILES, T], F32R)])
        slg, ys_hi, ys_lo = region(LRU_TILES * T, [("slg", [P, LRU_TILES, T], F32)],
                                   [("ys_hi", [P, S5_TILES, T], F32R), ("ys_lo", [P, S5_TILES, T], F32R)])
        s5t, w_lru, lt, gs = region(
            10 * T, [("s5t", [P, 10, T], F32)],
            [("w_lru", [P, 2 * LRU_TILES, P], F32), ("lt", [P, 5, T], F32)], [("gs", [P, NM, T], F32)])
        s5h_re = [sq[:, n, :] for n in range(2)]
        cos_sin = [s5t[:, 8:10, :], wide]
        ssg = bias_ring
        lru_t = [[lt[:, n, :] for n in range(5)],
                 [tmp[:, 0, :], tmp[:, 1, :], sq[:, 0, :], sq[:, 1, :], wide[:, 0, :]]]

        ps = ctx.enter_context(nc.psum_tensor("ps", [P, 8, T], F32))
        bias_d = nc.dram_tensor("bias_d", (HEADS_A + HEADS_C, NT, P, T), F32).ap()
        cs_d = nc.dram_tensor("cs_d", (P, 2, T), F32).ap()

        inputs_in = signal("inputs_in")
        pos_in = signal("pos_in")
        x_in = signal("x_in")
        raw_in = [signal(f"raw_in{i}") for i in range(2)]
        hi_split = signal("hi_split", LAYER_SLOTS)
        lo_split = signal("lo_split", LAYER_SLOTS)
        slot_used = signal("slot_used", LAYER_SLOTS)
        tile_done = signal("tile_done", EARLIER[LAYER_SLOTS])
        x_done = signal("x_done", 3 * NM)
        squared = signal("squared", SQ_LAYER)
        summed = signal("summed", SQ_LAYER)
        rooted = signal("rooted", 3)
        inverted = signal("inverted", 3)
        h_scaled = signal("h_scaled", 3 * NM)
        h_hi_done = signal("h_hi_done", 3 * NM)
        h_done = signal("h_done", 3 * NM)
        silued = signal("silued", 2 * NF)
        a_prod = signal("a_prod", 2 * NF)
        a_hi_done = signal("a_hi_done", 2 * NF)
        a_done = signal("a_done", 2 * NF)

        act_evac = signal("act_evac", 7 + 2 + 8)
        dve_evac = signal("dve_evac", 7 + 2 + HEADS_B + NT)
        c_squared = signal("c_squared", 5)
        c_summed = signal("c_summed", 2)
        c_rooted = signal("c_rooted", 2)
        c_done = signal("c_done", 5)
        k_turned = signal("k_turned", 1)
        k_spread = signal("k_spread", 2)
        cs_in = signal("cs_in", 16)
        bias_in = [signal(f"bias_in{i}", 16 * (len(BIASED) // 4)) for i in range(4)]
        score_done = signal("score_done", len(UNITS))
        max_done = signal("max_done", len(UNITS))
        exp_done = signal("exp_done", len(UNITS))
        p_done = signal("p_done", len(TURNS))
        turned = signal("turned", len(TURNS))
        pt_act = signal("pt_act", len(TURNS) // 2)
        pt_dve = signal("pt_dve", len(TURNS) // 2)
        pv_done = signal("pv_done", len(HEADS))
        pv_taken = signal("pv_taken", len(HEADS) // 2)
        oc_rooted = signal("oc_rooted", 2)
        oc_mixed = signal("oc_mixed", 2)
        dist_done = signal("dist_done")
        bias_made = signal("bias_made")
        bias_out = [signal(f"bias_out{i}") for i in range(2)]
        cs_made = signal("cs_made")
        cs_out = signal("cs_out")
        dve_step = signal("dve_step", DVE_STEPS)
        act_step = signal("act_step")
        dve_pro = signal("dve_pro")
        pro_step = signal("pro_step")
        fin = signal("fin")
        out_sent = signal("out_sent")

        pool_met = signal("pool_met")
        dve_met = signal("dve_met")

        cols2_in = signal("cols2_in")
        s5_in = signal("s5_in")
        w_lru_in = signal("w_lru_in")
        p_in = signal("p_in")
        x_again = signal("x_again")
        tile2_done = signal("tile2_done")
        evac2 = signal("evac2")
        d_small = signal("d_small")
        a_small = signal("a_small")
        s5_ready = signal("s5_ready")
        table_d = signal("table_d")
        table_a = signal("table_a")
        bu_done = signal("bu_done")
        pre_done = signal("pre_done")
        pre_sum = signal("pre_sum")
        scan_done = signal("scan_done")
        post_d = signal("post_d")
        post_p = signal("post_p")
        h_re_done = signal("h_re_done")
        h_im_done = signal("h_im_done")
        s5_out = signal("s5_out")
        s5_y = signal("s5_y")
        pads_done = signal("pads_done")
        conv_step = signal("conv_step")
        conv_done = signal("conv_done")
        ri_done = signal("ri_done")
        lru_a = signal("lru_a")
        lru_ic = signal("lru_ic")
        lru_mid = signal("lru_mid")
        lru_root = signal("lru_root")
        lru_b = signal("lru_b")
        lru_scan = signal("lru_scan")
        lru_y = signal("lru_y")
        yl_hi_done = signal("yl_hi_done")
        yl_done = signal("yl_done")
        yl_used = signal("yl_used")
        z_taken = signal("z_taken")
        gs_done = signal("gs_done")
        gelued = signal("gelued")
        g_hi_done = signal("g_hi_done")
        g_done = signal("g_done")
        glu_sig = signal("glu_sig")
        glu_prod = signal("glu_prod")
        glu_step = signal("glu_step")
        ys_done = signal("ys_done")
        bs_taken = signal("bs_taken")
        merge_step = signal("merge_step")
        merged = signal("merged")
        o_copied = signal("o_copied")
        o_step = signal("o_step")
        xs_done = signal("xs_done")
        p_split = signal("p_split")
        ple_evac = signal("ple_evac")
        gate_sig = signal("gate_sig")
        gate_step = signal("gate_step")

        block = ctx.enter_context(nc.Block())

        def first_products():
            step = lru = 0
            for s in range(LRU_OUT_AT):
                yield "slot", s
                for i in range(2):
                    n = 2 * s + i
                    yield "tile", n
                    if n >= S5_FROM and step < S5_STEPS:
                        yield "s5", step
                        step += 1
                    if n >= LRU_FROM:
                        yield "lru", lru
                        lru += 1
            while lru < LRU_STEPS:
                yield "lru", lru
                lru += 1

        def wait_tile2(eng, s, i, n=2, before=0):
            if i == n - 1:
                wait(eng, slot_used, DEPTH, s + 1)
            else:
                eng.wait_ge(tile2_done.sem, before + i + 1)

        per_slot = [1] * LRU_OUT_AT + [0] * 4 + [7] + [1] * 4 + [3] * 4 + [1] * 4 + [7] + [1] * 4
        before2 = [sum(per_slot[:s]) for s in range(SLOTS_2 + 1)]

        def wait(eng, sig, layer, k):
            eng.wait_ge(sig.sem, sig.at(layer, k))

        def wait_tile(eng, layer, s, i):
            if i == TILES[s] - 1:
                wait(eng, slot_used, layer, s + 1)
            else:
                wait(eng, tile_done, layer, EARLIER[s] + i + 1)

        @block.sync
        def _(sp):
            sp.dma_start(x[:], a["x"]).then_inc(x_in.sem, 16)
            sp.dma_start(cols2[:], a["cols2"]).then_inc(cols2_in.sem, 16)
            for dst, name in ((cols, "cols"), (mats, "mats"), (gains, "gains"), (lamv, "lamv")):
                sp.dma_start(dst[:], a[name]).then_inc(inputs_in.sem, 16)
            for i in range(2):
                sp.dma_start(raw[i][:], a["stream"][i]).then_inc(raw_in[i].sem, 16)
            with sp.Fori(1, a["stream"].shape[0] // 2) as j:
                for i in range(2):
                    sp.wait_ge(lo_split.sem, 2 * j - 1 + i)
                    sp.dma_start(raw[i][:], a["stream"][2 * j + i]).then_inc(raw_in[i].sem, 16)
            for m in range(NM):
                sp.wait_ge(fin.sem, m + 1)
                sp.dma_start(a["out"][:, m, :], x[:, m, :]).then_inc(out_sent.sem, 16)
            sp.wait_ge(out_sent.sem, 16 * NM)

        @block.gpsimd
        def _(pool):
            pool.dma_start(pos_i[:], a["pos"].partition_broadcast(P)).then_inc(pos_in.sem, 16)
            pool.dma_start(pcol_i[:], a["pos_col"]).then_inc(pos_in.sem, 16)
            pool.dma_start(reach[:], a["reach"]).then_inc(pos_in.sem, 16)
            pool.wait_ge(cs_made.sem, 1)
            pool.dma_start(cs_d, table2[:]).then_inc(cs_out.sem, 16)
            n = made = 0
            for table in range(HEADS_A + HEADS_C):
                is_a = table < HEADS_A
                slope = SLOPES[2 * table] if is_a else SLOPES[2 * (table - HEADS_A) + 1]
                for q in range(NT):
                    pool.wait_ge(dist_done.sem, q + 1)
                    if n >= 2:
                        pool.wait_ge(bias_out[n % 2].sem, 16 * (n // 2))
                    pool.tensor_scalar(wide[:, n % 2, :], dist[:, q, :], slope, 0.0, ALU.mult, ALU.add
                                       ).then_inc(bias_made.sem, 1)
                    made += 1
                    pool.wait_ge(bias_made.sem, made)
                    if is_a:
                        pool.wait_ge(pos_in.sem, 48)
                        lo = T - P - P * q
                        pool.tensor_tensor(wide[:, n % 2, :], wide[:, n % 2, :], reach[:, lo:lo + T], ALU.add
                                           ).then_inc(bias_made.sem, 1)
                        made += 1
                        pool.wait_ge(bias_made.sem, made)
                    pool.dma_start(bias_d[table, q], wide[:, n % 2, :]).then_inc(bias_out[n % 2].sem, 16)
                    n += 1
            for i in range(2):
                pool.wait_ge(bias_out[i].sem, 16 * (n // 2))
            pool.wait_ge(cs_out.sem, 16)
            with pool.Fori(0, DEPTH) as layer:
                wait(pool, x_done, layer, NM)
                pool.sem_inc(pool_met.sem, 1)
                pool.dma_start(cs[:], cs_d).then_inc(cs_in.sem, 16)
                for n, u in enumerate(BIASED):
                    kind, head, _, q = UNITS[u]
                    if n >= 4:
                        wait(pool, max_done, layer, BIASED[n - 4] + 1)
                        pool.sem_inc(pool_met.sem, 1)
                    pool.dma_start(bias_ring[:, n % 4, :], bias_d[head + (HEADS_A if kind == "c" else 0), q]
                                   ).then_inc(bias_in[n % 4].sem, 16)
                wait(pool, max_done, layer, len(UNITS))

            wait(pool, x_done, DEPTH, 0)
            for dst, name in ((s5p, "s5p"), (tidx, "tidx"), (s5b, "s5b"), (s5c_in, "s5c")):
                pool.dma_start(dst[:], a[name]).then_inc(s5_in.sem, 16)

            def s5_step(p):
                if p < S5_PAIRS:
                    t = 4 * (p % 2)
                    pool.wait_ge(pre_done.sem, 4 * (p + 1))
                    pool.tensor_tensor(s5t[:, t, :], s5t[:, t, :], s5t[:, t + 1, :], ALU.add).then_inc(pre_sum.sem, 1)
                    pool.tensor_tensor(s5t[:, t + 2, :], s5t[:, t + 2, :], s5t[:, t + 3, :], ALU.subtract
                                       ).then_inc(pre_sum.sem, 1)
                p -= 1
                if 0 <= p < S5_PAIRS:
                    t = 4 * (p % 2)
                    cos, sin = (cos_sin[p % 2][:, n, :] for n in range(2))
                    pool.wait_ge(scan_done.sem, 2 * (p + 1))
                    pool.tensor_tensor(s5t[:, t, :], s5t[:, t + 1, :], sin, ALU.mult).then_inc(post_p.sem, 1)
                    pool.tensor_tensor(s5t[:, t + 2, :], s5t[:, t + 3, :], cos, ALU.mult).then_inc(post_p.sem, 1)
                    pool.wait_ge(post_p.sem, 2 * (p + 1))
                    pool.tensor_tensor(s5t[:, t, :], s5t[:, t, :], s5t[:, t + 2, :], ALU.add).then_inc(h_im_done.sem, 1)

            def lru_step(q):
                if q < LRU_TILES:
                    c, _, i_, _, _ = lru_t[q % 2]
                    pool.wait_ge(lru_a.sem, 4 * q + 2)
                    pool.tensor_tensor(i_, i_, c, ALU.mult).then_inc(lru_ic.sem, 1)
                q -= 1
                if 0 <= q < LRU_TILES:
                    _, _, i_, _, root = lru_t[q % 2]
                    pool.wait_ge(lru_ic.sem, q + 1)
                    pool.wait_ge(lru_root.sem, q + 1)
                    pool.tensor_tensor(i_, i_, root, ALU.mult).then_inc(lru_b.sem, 1)

            for kind, n in first_products():
                if kind == "s5":
                    s5_step(n)
                if kind == "s5" and n == S5_STEPS - 1:
                    pool.wait_ge(s5_out.sem, S5_PAIRS)
                    pool.dma_start(w_lru[:], a["w_lru"]).then_inc(w_lru_in.sem, 16)
                if kind == "lru":
                    lru_step(n)
            pool.wait_ge(lru_y.sem, LRU_TILES)
            pool.dma_start(wide[:], a["p"]).then_inc(p_in.sem, 16)

        @block.tensor
        def _(pe):
            def three(out, w, xs, start, stop):
                (wh, wl), (xh, xl) = w, xs
                pe.matmul(out, wh, xh, start=start, stop=False)
                pe.matmul(out, wh, xl, start=False, stop=False)
                return pe.matmul(out, wl, xh, start=False, stop=stop)

            def weights(buf, b, n=1):
                return (w_hi[:, buf, b * P:(b + n) * P], w_lo[:, buf, b * P:(b + n) * P])

            def hid(m, lo=0, hi=T):
                return (h_hi[:, m, lo:hi], h_lo[:, m, lo:hi])

            def sum_squares(layer, before, idx, mat=None, bank=SS_BANK, alone=False):
                wait(pe, squared, layer, before + idx + 1)
                pe.matmul(ps[:, bank, :], ones if mat is None else mat, sq[:, idx % 2, :],
                          start=alone or idx == 0, stop=alone or idx == NM - 1).then_inc(summed.sem, 1)

            def up_slots(layer, f, at):
                with pe.Fori(0, UP_SLOTS // 2) as j:
                    for i in range(2):
                        c, buf = 2 * j + i, (at + i) % 2
                        pe.wait_ge(lo_split.sem, lo_split.at(layer, at + 1) + c)
                        pe.wait_ge(a_done.sem, a_done.at(layer, f * NF) + c)
                        for k in range(NM):
                            wait(pe, h_done, layer, 2 * f * NM + k + 1)
                            for half in range(2):
                                last = three(ps[:, 2 * i + half, :], weights(buf, 2 * k + half), hid(k),
                                             k == 0, k == NM - 1)
                        last.then_inc(slot_used.sem, 1)

            def down_slot(layer, f, at, j, i, first=False, final=False):
                buf = (at + i) % 2
                pe.wait_ge(lo_split.sem, lo_split.at(layer, at + 1) + j)
                pe.wait_ge(a_done.sem, a_done.at(layer, f * NF + 3) + 2 * j)
                before = (1 if f == 0 else 2) * NM + (0 if f == 0 else 2 + NM)
                for idx, m in enumerate(ORD):
                    if first and m == 0:
                        wait(pe, a_done, layer, (f + 1) * NF + 1)
                    for n in range(2):
                        mm = three(ps[:, m, :], weights(buf, 2 * idx + n),
                                   (a_hi[:, 2 * j + n, :], a_lo[:, 2 * j + n, :]),
                                   first and n == 0, final and n == 1)
                    if final and idx < NM - 1:
                        mm.then_inc(tile_done.sem, 1)
                    if idx == NM - 1:
                        mm.then_inc(slot_used.sem, 1)
                    if final and idx >= 2:
                        sum_squares(layer, before, idx - 2)
                if final:
                    for idx in (NM - 2, NM - 1):
                        sum_squares(layer, before, idx)

            def ffn(layer, f, at):
                up_slots(layer, f, at)
                at += UP_SLOTS
                down_slot(layer, f, at, 0, 0, first=True)
                with pe.Fori(0, DOWN_SLOTS // 2 - 1) as j:
                    for i in range(2):
                        down_slot(layer, f, at, 2 * j + 1 + i, 1 + i)
                down_slot(layer, f, at, DOWN_SLOTS - 2, 1)
                down_slot(layer, f, at, DOWN_SLOTS - 1, 0, final=True)

            def in_products(layer):
                for s in range(7):
                    wait(pe, lo_split, layer, MIX_AT + s + 1)
                    for i in range(2):
                        t = 2 * s + i
                        if t >= 4:
                            wait(pe, (dve_evac, act_evac)[i], layer, s - 1)
                        for k in range(NM):
                            wait(pe, h_done, layer, NM + k + 1)
                            mm = three(ps[:, t % 4, :], weights((MIX_AT + s) % 2, i * NM + k), hid(k),
                                       k == 0, k == NM - 1)
                        mm.then_inc((tile_done, slot_used)[i].sem, 1)
                    if s == 1:
                        wait(pe, dve_evac, layer, 1)
                        pe.matmul(ps[:, 7, :], spread[0:64, :], k_prod[0:64, :], start=True, stop=True
                                  ).then_inc(k_turned.sem, 1)
                    if s == 4:
                        for i in range(5):
                            wait(pe, c_squared, layer, i + 1)
                            mm = pe.matmul(ps[:, 5 if i < 3 else 6, :], ones, c_sq[:, i, :],
                                           start=i in (0, 3), stop=i in (2, 4))
                            if i in (2, 4):
                                mm.then_inc(c_summed.sem, 1)
                wait(pe, dve_evac, layer, 7)
                wait(pe, act_evac, layer, 7)
                for s in (7, 8):
                    wait(pe, lo_split, layer, MIX_AT + s + 1)
                    for t in range(NT):
                        for k in range(4):
                            kk = 4 * (s - 7) + k
                            mm = three(ps[:, t, :], hid(kk, t * P, (t + 1) * P),
                                       weights((MIX_AT + s) % 2, 4 * k, 4), kk == 0, kk == NM - 1)
                        if s == 8 and t < NT - 1:
                            mm.then_inc(tile_done.sem, 1)
                    mm.then_inc(slot_used.sem, 1)
                for s in (9, 10):
                    wait(pe, lo_split, layer, MIX_AT + s + 1)
                    wait(pe, c_done, layer, 5)
                    for i in range(4):
                        if s == 9:
                            wait(pe, (dve_evac, act_evac)[i % 2], layer, 8 + i // 2)
                        else:
                            wait(pe, dve_evac, layer, 10 + i)
                        for k in range(3):
                            mm = three(ps[:, i, :], weights((MIX_AT + s) % 2, 3 * i + k),
                                       (cn_hi[:, k, :], cn_lo[:, k, :]), k == 0, k == 2)
                        mm.then_inc((tile_done if i < 3 else slot_used).sem, 1)
                wait(pe, lo_split, layer, MIX_AT + 12)
                for i in range(4):
                    wait(pe, dve_evac, layer, 14 + i)
                    for k in range(2):
                        mm = three(ps[:, i, :], weights((MIX_AT + 11) % 2, 2 * i + k),
                                   (cn_hi[:, 3 + k, :], cn_lo[:, 3 + k, :]), k == 0, k == 1)
                    mm.then_inc(tile_done.sem, 1)
                wait(pe, c_rooted, layer, 2)
                wait(pe, k_spread, layer, 2)
                for t in range(NT):
                    for k in range(2):
                        mm = three(ps[:, 4 + t, :], (cn_hi[:, 3 + k, t * P:(t + 1) * P], cn_lo[:, 3 + k, t * P:(t + 1) * P]),
                                   weights((MIX_AT + 11) % 2, 8 + 4 * k, 4), k == 0, k == 1)
                    mm.then_inc((tile_done if t < 3 else slot_used).sem, 1)

            def score(layer, u):
                kind, head, c, q = UNITS[u]
                if u == 0:
                    wait(pe, act_evac, layer, 17)
                    wait(pe, dve_evac, layer, 17)
                if u >= 4:
                    wait(pe, exp_done, layer, u - 3)
                if kind == "b":
                    query, key, lo, n = q_b[:, head, :], k_b[:, head, :], 0, P
                elif kind == "a":
                    query, key, lo, n = qk[:, 2 * (head // 2), :], qk[:, 2 * (head // 2) + 1, :], 64 * (head % 2), 64
                else:
                    m = 2 * head + c
                    query, key, lo, n = qk[:, 4 + 2 * (m // 4), :], qk[:, 5 + 2 * (m // 4), :], 32 * (m % 4), 32
                pe.matmul(ps[:, u % 4, :], query[lo:lo + n, q * P:(q + 1) * P], key[lo:lo + n, :],
                          start=True, stop=True).then_inc(score_done.sem, 1)

            def turn(layer, v):
                wait(pe, p_done, layer, v + 1)
                if v >= 2:
                    wait(pe, (pt_act, pt_dve)[v % 2], layer, v // 2)
                for k in range(NT):
                    mm = pe.transpose(ps[:, 4 + v % 2, k * P:(k + 1) * P], probs[:, TURNS[v] % 4, k * P:(k + 1) * P],
                                      ident)
                mm.then_inc(turned.sem, 1)

            def attend(layer, g):
                kind, head = HEADS[g]
                if g in (4, 6):
                    wait(pe, oc_rooted, layer, g // 2 - 1)
                if g >= 4:
                    wait(pe, pv_taken, layer, g // 2 - 1)
                wait(pe, pt_act, layer, 2 * g + 2)
                wait(pe, pt_dve, layer, 2 * g + 2)
                if g == 0:
                    wait(pe, dve_evac, layer, 21)
                v, col = (v_b, 64 * head) if kind == "b" else (v_ac, 64 * head + (256 if kind == "c" else 0))
                half = 64 * (g % 2)
                for k in range(NT):
                    mm = pe.matmul(ps[half:half + 64, 6 + (g // 2) % 2, :], v[:, k, col:col + 64], pt[:, g % 2, k, :],
                                   start=k == 0, stop=k == NT - 1)
                mm.then_inc(pv_done.sem, 1)

            def attention(layer):
                for u in range(len(UNITS) + 4):
                    if u < len(UNITS):
                        score(layer, u)
                    if u - 3 in TURNS:
                        turn(layer, TURNS.index(u - 3))
                    if u - 4 in TURNS and TURNS.index(u - 4) % NT == NT - 1:
                        attend(layer, TURNS.index(u - 4) // NT)
                    if u == OC_NORM_AT + 1:
                        for i in range(2):
                            sum_squares(layer, 2 * NM, i, mat=ones64, bank=6 + i, alone=True)

            def out_products(layer):
                wait(pe, pv_taken, layer, 8)
                wait(pe, oc_mixed, layer, 2)
                for s in range(12, 16):
                    wait(pe, lo_split, layer, MIX_AT + s + 1)
                    for i in range(2):
                        idx = 2 * (s - 12) + i
                        for k in range(NM):
                            mm = three(ps[:, ORD[idx], :], weights((MIX_AT + s) % 2, i * NM + k),
                                       (mix_hi[:, k, :], mix_lo[:, k, :]), k == 0, k == NM - 1)
                        mm.then_inc((tile_done, slot_used)[i].sem, 1)
                        if idx >= 2:
                            sum_squares(layer, 2 * NM + 2, idx - 2)
                for idx in (NM - 2, NM - 1):
                    sum_squares(layer, 2 * NM + 2, idx)

            pe.wait_ge(inputs_in.sem, 64)
            for idx in range(NM):
                sum_squares(0, 0, idx)
            with pe.Fori(0, DEPTH) as layer:
                ffn(layer, 0, 0)
                in_products(layer)
                attention(layer)
                out_products(layer)
                ffn(layer, 1, FFN2_AT)

            for idx in range(NM):
                sum_squares(DEPTH, NM, idx)

            def tile2(s, i, bank, ins, n_k, blocks_at, signal_to, begin=0):
                for k in range(n_k):
                    mm = three(ps[:, bank, :], weights(s % 2, blocks_at + k), ins(k), k == 0, k == n_k - 1)
                mm.then_inc(signal_to.sem, 1)

            def slot2(s):
                wait(pe, lo_split, DEPTH, s + 1)

            def s5_step(p):
                if p < S5_PAIRS:
                    lo, tile = 32 * (p % 4), p // 4
                    if p % 4 == 0:
                        pe.wait_ge(evac2.sem, tile + 1)
                    if p == 0:
                        wait(pe, rooted, DEPTH, 2)
                        pe.wait_ge(s5_in.sem, 64)
                    if p >= 1:
                        pe.wait_ge(pre_done.sem, 4 * p)
                    for ri in range(2):
                        mm = pe.matmul(ps[:, 4 + ri, :], s5b[lo:lo + 32, tile, ri, :], u[lo:lo + 32, tile, :],
                                       start=True, stop=True)
                    mm.then_inc(bu_done.sem, 1)
                p -= 2
                if 0 <= p < S5_PAIRS:
                    lo, tile = 32 * (p % 4), p // 4
                    if p % 4 == 0 and tile >= 2:
                        pe.wait_ge(s5_y.sem, tile - 1)
                    if p == 0:
                        pe.wait_ge(s5_ready.sem, 1)
                    t = 4 * (p % 2)
                    pe.wait_ge(h_re_done.sem, p + 1)
                    pe.matmul(ps[lo:lo + 32, 6 + tile % 2, :], s5c[:, 0, 32 * p:32 * p + 32], s5h_re[p % 2],
                              start=True, stop=False)
                    pe.wait_ge(h_im_done.sem, p + 1)
                    pe.matmul(ps[lo:lo + 32, 6 + tile % 2, :], s5c[:, 1, 32 * p:32 * p + 32], s5t[:, t, :],
                              start=False, stop=True).then_inc(s5_out.sem, 1)

            def lru_step(q):
                if q >= LRU_TILES:
                    return
                bank = 4 + 2 * (q % 2)
                if q == 0:
                    pe.wait_ge(w_lru_in.sem, 16)
                    pe.wait_ge(s5_y.sem, S5_TILES)
                if q >= 2:
                    pe.wait_ge(lru_a.sem, 4 * (q - 2) + 2)
                pe.wait_ge(conv_done.sem, q + 1)
                for n in range(2):
                    mm = pe.matmul(ps[:, bank + n, :], w_lru[:, 2 * q + n, :], lru_t[q % 2][0], start=True, stop=True)
                mm.then_inc(ri_done.sem, 1)

            for kind, n in first_products():
                if kind == "slot":
                    slot2(n)
                elif kind == "s5":
                    s5_step(n)
                elif kind == "lru":
                    lru_step(n)
                else:
                    if n >= 4:
                        pe.wait_ge(evac2.sem, n - 3)
                    if n < 2:
                        for k in range(NM):
                            wait(pe, h_done, DEPTH, NM + k + 1)
                    tile2(n // 2, n % 2, n % 4, hid, NM, NM * (n % 2), (tile2_done, slot_used)[n % 2])
            pe.wait_ge(evac2.sem, 2 * LRU_OUT_AT)
            pe.wait_ge(lru_a.sem, 4 * (LRU_TILES - 1) + 2)
            for k in range(LRU_TILES):
                s = LRU_OUT_AT + k // 2
                slot2(s)
                pe.wait_ge(yl_done.sem, k + 1)
                for m in range(NM):
                    mm = three(ps[:, m, :], weights(s % 2, NM * (k % 2) + m), (yl_hi[:, k % 2, :], yl_lo[:, k % 2, :]),
                               k == 0, k == LRU_TILES - 1)
                    if k == LRU_TILES - 1 and m < NM - 1:
                        mm.then_inc(tile2_done.sem, 1)
                mm.then_inc((yl_used, slot_used)[k % 2].sem, 1)
            for m in range(NM):
                s = GATE_S_AT + m // 2
                if m % 2 == 0:
                    slot2(s)
                if m < 4:
                    pe.wait_ge(z_taken.sem, m + 1)
                else:
                    pe.wait_ge(gs_done.sem, m - 3)
                tile2(s, m % 2, m % 4, hid, NM, NM * (m % 2), (tile2_done, slot_used)[m % 2])
            pe.wait_ge(z_taken.sem, NM)
            for n in range(2 * S5_TILES):
                s = GLU_AT + n // 4
                if n % 4 == 0:
                    slot2(s)
                    pe.wait_ge(g_done.sem, S5_TILES)
                if n >= 4 and n % 2 == 0:
                    pe.wait_ge(glu_prod.sem, n // 2 - 1)
                tile2(s, n % 4, 4 + n % 4, lambda k: (g_hi[:, k, :], g_lo[:, k, :]), S5_TILES, 4 * (n % 4),
                      slot_used if n % 4 == 3 else tile2_done)
            for m in range(NM):
                s = S5_OUT_AT + m // 4
                if m % 4 == 0:
                    slot2(s)
                if m == 0:
                    pe.wait_ge(ys_done.sem, S5_TILES)
                    pe.wait_ge(gs_done.sem, NM)
                if m >= 4:
                    pe.wait_ge(bs_taken.sem, m - 3)
                tile2(s, m % 4, m % 4, lambda k: (ys_hi[:, k, :], ys_lo[:, k, :]), S5_TILES, 4 * (m % 4),
                      slot_used if m % 4 == 3 else tile2_done)
            pe.wait_ge(merged.sem, NM)
            for idx, m in enumerate(ORD):
                s = OUT_AT + idx // 2
                if idx % 2 == 0:
                    slot2(s)
                tile2(s, idx % 2, m, lambda k: (mix_hi[:, k, :], mix_lo[:, k, :]), NM, NM * (idx % 2),
                      (tile2_done, slot_used)[idx % 2])
                if idx >= 2:
                    sum_squares(DEPTH, 2 * NM, idx - 2)
            for idx in (NM - 2, NM - 1):
                sum_squares(DEPTH, 2 * NM, idx)
            slot2(PLE_AT)
            pe.wait_ge(p_split.sem, 2 * PLE_TILES)
            for m in range(NM):
                mm_bank = PLE_BANKS[m]
                if m == NM - 1:
                    wait(pe, rooted, DEPTH, 3)
                for k in range(PLE_TILES):
                    mm = three(ps[:, mm_bank, :], weights(PLE_AT % 2, 2 * m + k), (p_hi[:, k, :], p_lo[:, k, :]),
                               k == 0, k == 1)
                mm.then_inc((tile2_done if m < NM - 1 else slot_used).sem, 1)
            for m in range(NM):
                s = PLE_GATE_AT + m // 2
                if m % 2 == 0:
                    slot2(s)
                pe.wait_ge(ple_evac.sem, m + 1)
                for k in range(NM):
                    if m == 0:
                        pe.wait_ge(xs_done.sem, k + 1)
                    mm = three(ps[:, PLE_BANKS[m], :], weights(s % 2, NM * (m % 2) + k), hid(k), k == 0, k == NM - 1)
                mm.then_inc((tile2_done, slot_used)[m % 2].sem, 1)

        @block.scalar
        def _(act):
            def split(layer, s, more=0):
                buf = s % 2
                act.wait_ge(raw_in[buf].sem, (layer * (LAYER_SLOTS // 2) + s // 2 + 1) * 16 + more * 8)
                act.wait_ge(slot_used.sem, slot_used.at(layer, s - 1) + more)
                act.activation(w_hi[:, buf, :], raw[buf][:], ACT.Copy).then_inc(hi_split.sem, 1)

            def square(layer, before, idx, src):
                if idx >= 2:
                    wait(act, summed, layer, before + idx - 1)
                act.activation(sq[:, idx % 2, :], src, ACT.Square).then_inc(squared.sem, 1)

            def root(layer, before, n):
                wait(act, summed, layer, before + NM)
                act.activation(rstd, ps[:, SS_BANK, :], ACT.Sqrt, bias=eps, scale=1.0 / D).then_inc(rooted.sem, 1)

            def norm(layer, before, n, stage, s):
                for idx, m in enumerate(ORD):
                    wait(act, x_done, layer, stage * NM + idx + 1)
                    square(layer, before, idx, x[:, m, :])
                root(layer, before, n)

            def ffn(layer, f, at):
                with act.Fori(0, UP_SLOTS // 2) as j:
                    for i in range(2):
                        c = 2 * j + i
                        split(layer, at + i + 1, 2 * j)
                        act.wait_ge(slot_used.sem, slot_used.at(layer, at + 1) + c)
                        act.wait_ge(a_done.sem, a_done.at(layer, f * NF) + c)
                        act.activation(sil[:, i, :], ps[:, 2 * i, :], ACT.Silu).then_inc(silued.sem, 1)
                at += UP_SLOTS
                with act.Fori(0, DOWN_SLOTS // 2) as j:
                    for i in range(2):
                        split(layer, at + i + 1, 2 * j)
                split(layer, at + DOWN_SLOTS)
                norm(layer, NM if f == 0 else 3 * NM + 2, 0, 2 * f, 0)

            def in_products(layer):
                for s in range(7):
                    split(layer, MIX_AT + s + 1)
                    t = 2 * s + 1
                    wait_tile(act, layer, MIX_AT + s, 1)
                    dst = c_raw[:, t - 1, :] if t < 6 else qk[:, t - 6, :]
                    act.activation(dst, ps[:, t % 4, :], ACT.Copy).then_inc(act_evac.sem, 1)
                    if s == 3:
                        wait(act, dve_evac, layer, 3)
                        wait(act, act_evac, layer, 3)
                        for i in range(5):
                            act.activation(c_sq[:, i, :], c_raw[:, i, :], ACT.Square).then_inc(c_squared.sem, 1)
                    if s == 5:
                        for i, width in enumerate((Q_LORA, KV_LORA)):
                            wait(act, c_summed, layer, i + 1)
                            act.activation(c_rstd[:, i, :], ps[:, 5 + i, :], ACT.Sqrt, bias=eps, scale=1.0 / width
                                           ).then_inc(c_rooted.sem, 1)
                split(layer, MIX_AT + 8)
                split(layer, MIX_AT + 9)
                for t in (1, 3):
                    wait_tile(act, layer, MIX_AT + 8, t)
                    act.activation(v_ac[:, t, :], ps[:, t, :], ACT.Copy).then_inc(act_evac.sem, 1)
                split(layer, MIX_AT + 10)
                wait(act, c_done, layer, 5)
                wait(act, k_turned, layer, 1)
                for half in range(2):
                    lo = 64 * (1 - half)
                    dst = k_b[lo:lo + 64, :, :].rearrange("p (h two) t -> p h two t", two=2)[:, :, half, :]
                    act.activation(dst, ps[lo:lo + 64, 7, :].unsqueeze(1).to_broadcast([64, HEADS_B // 2, T]), ACT.Copy
                                   ).then_inc(k_spread.sem, 1)
                split(layer, MIX_AT + 11)
                for i in range(4):
                    wait_tile(act, layer, MIX_AT + 11, i)
                    for half in range(2):
                        act.activation(k_b[64 * half:64 * half + 64, 2 * i + half, :],
                                       ps[64 * half:64 * half + 64, i, :], ACT.Copy).then_inc(act_evac.sem, 1)

            def exps(layer, u):
                kind = UNITS[u][0]
                wait(act, max_done, layer, u + 1)
                if u >= 4:
                    if u - 4 in TURNS:
                        wait(act, turned, layer, TURNS.index(u - 4) + 1)
                    else:
                        wait(act, p_done, layer, TURNS.index(u - 3) + 1)
                src = ps[:, u % 4, :] if kind == "b" else negs[:, u % 4, :]
                act.activation(probs[:, u % 4, :], src, ACT.Exp, bias=mneg[:, u % 4:u % 4 + 1], scale=-1.0,
                               accum_out=rsum[:, u % 4:u % 4 + 1]).then_inc(exp_done.sem, 1)

            def turned_out(layer, v):
                wait(act, turned, layer, v + 1)
                if v >= 2 * NT:
                    wait(act, pv_done, layer, v // NT - 1)
                q = v % NT
                act.activation(pt[:, (v // NT) % 2, :, q * P:(q + 1) * P],
                               ps[:, 4 + v % 2, :].rearrange("p (k n) -> p k n", k=NT), ACT.Copy
                               ).then_inc(pt_act.sem, 1)

            def attention(layer):
                for u in range(len(UNITS) + 4):
                    if u < len(UNITS):
                        exps(layer, u)
                    v = TURNS.index(u - 4) if u - 4 in TURNS else 1
                    if v % 2 == 0:
                        turned_out(layer, v)
                    if u == OC_NORM_AT:
                        for i in range(2):
                            wait(act, pv_taken, layer, i + 1)
                            square(layer, 2 * NM, i, tmp[:, i, :])
                    if u == OC_NORM_AT + 1:
                        for i in range(2):
                            wait(act, summed, layer, 2 * NM + i + 1)
                            act.activation(sq[:, i, :], ps[:, 6 + i, :], ACT.Sqrt, bias=eps, scale=1.0 / V_DIM
                                           ).then_inc(oc_rooted.sem, 1)

            def out_products(layer):
                wait(act, pv_done, layer, len(HEADS))
                split(layer, MIX_AT + 12)
                for s in range(12, 16):
                    split(layer, MIX_AT + s + 1)
                    for i in range(2):
                        idx = 2 * (s - 12) + i
                        wait(act, x_done, layer, NM + idx + 1)
                        square(layer, 2 * NM + 2, idx, x[:, ORD[idx], :])
                root(layer, 2 * NM + 2, 1)

            act.wait_ge(x_in.sem, 16)
            act.wait_ge(raw_in[0].sem, 16)
            act.activation(w_hi[:, 0, :], raw[0][:], ACT.Copy).then_inc(hi_split.sem, 1)
            for idx, m in enumerate(ORD):
                square(0, 0, idx, x[:, m, :])
            act.wait_ge(inputs_in.sem, 64)
            root(0, 0, 0)
            act.wait_ge(dve_pro.sem, 1)
            act.activation(lam_s[:, 4:6], lam_s[:, 0:2], ACT.Exp).then_inc(act_step.sem, 1)
            act.activation(lam_s[:, 6:8], lam_s[:, 2:4], ACT.Exp).then_inc(act_step.sem, 1)
            act.wait_ge(dve_pro.sem, 2)
            act.activation(rot[:, 0, :], rot[:, 2, :], ACT.Sin).then_inc(act_step.sem, 1)
            act.activation(rot[:, 3, :], rot[:, 2, :], ACT.Abs).then_inc(act_step.sem, 1)
            act.wait_ge(act_step.sem, 4)
            act.activation(rot[:, 1, :], rot[:, 3, :], ACT.Sin, bias=cols[:, 1:2], scale=-1.0).then_inc(act_step.sem, 1)
            with act.Fori(0, DEPTH) as layer:
                ffn(layer, 0, 0)
                in_products(layer)
                attention(layer)
                out_products(layer)
                ffn(layer, 1, FFN2_AT)

            def split2(s):
                if s < SLOTS_2:
                    split(DEPTH, s)

            small = [0]

            def small_step(ins):
                small[0] += 1
                ins.then_inc(a_small.sem, 1)
                act.wait_ge(a_small.sem, small[0])

            for idx, m in enumerate(ORD):
                wait(act, x_again, 0, NM)
                square(DEPTH, NM, idx, x[:, m, :])
            wait(act, summed, DEPTH, 2 * NM)
            act.activation(rstd, ps[:, SS_BANK, :], ACT.Sqrt, bias=eps, scale=1.0 / D).then_inc(rooted.sem, 1)
            act.wait_ge(s5_in.sem, 64)
            small_step(act.activation(s5w[:, 0, :], s5p[:, 2, :], ACT.Exp))
            act.wait_ge(d_small.sem, D_DECAY)
            small_step(act.activation(s5w[:, 3, :], s5w[:, 2, :], ACT.Exp))
            act.wait_ge(d_small.sem, D_ANGLE)
            small_step(act.activation(s5w[:, 6, :], s5w[:, 5, :], ACT.Sin, scale=TURN))
            small_step(act.activation(s5w[:, 7, :], s5w[:, 5, :], ACT.Abs))
            small_step(act.activation(s5w[:, 7, :], s5w[:, 7, :], ACT.Sin, scale=-TURN, bias=cols[:, 1:2]))
            act.wait_ge(d_small.sem, D_LAM)
            small_step(act.activation(lru_s[:, 1, :], lru_s[:, 0, :], ACT.Exp, scale=-1.0))
            act.wait_ge(d_small.sem, D_LAM + 1)
            small_step(act.activation(lru_s[:, 1, :], lru_s[:, 1, :], ACT.Ln))

            def evac(n):
                src = ps[:, n % 4, :]
                wait_tile2(act, n // 2, n % 2, before=before2[n // 2])
                s = n // 2
                if s < LRU_X_AT:
                    dst, func = u[:, n, :], ACT.Copy
                elif s < LRU_G_AT:
                    dst, func = lrux[:, n - 2 * LRU_X_AT, PAD:PAD + T], ACT.Copy
                elif s < S5_G_AT:
                    dst, func = slg[:, n - 2 * LRU_G_AT, :], ACT.Silu
                elif s < GATE_L_AT:
                    dst, func = ssg[:, n - 2 * S5_G_AT, :], ACT.Silu
                else:
                    dst, func = gl[:, n - 2 * GATE_L_AT, :], ACT.Sigmoid
                if n == 2 * GATE_L_AT:
                    act.wait_ge(s5_out.sem, S5_PAIRS)
                    act.wait_ge(scan_done.sem, 2 * S5_PAIRS)
                act.activation(dst, src, func).then_inc(evac2.sem, 1)

            def tables(p):
                if p >= S5_PAIRS:
                    return
                cos, sin = (cos_sin[p % 2][:, n, :] for n in range(2))
                act.wait_ge(table_d.sem, 3 * (p + 1))
                if p >= 2:
                    act.wait_ge(post_d.sem, 2 * (p - 1))
                    act.wait_ge(post_p.sem, 2 * (p - 1))
                act.activation(sin, tmp[:, 0, :], ACT.Sin, scale=TURN).then_inc(table_a.sem, 1)
                act.activation(cos, tmp[:, 0, :], ACT.Abs).then_inc(table_a.sem, 1)
                act.wait_ge(table_a.sem, 3 * p + 2)
                act.activation(cos, cos, ACT.Sin, scale=-TURN, bias=cols[:, 1:2]).then_inc(table_a.sem, 1)

            def lru_step(q):
                if q < LRU_TILES:
                    _, r, i_, a_, _ = lru_t[q % 2]
                    bank = 4 + 2 * (q % 2)
                    act.wait_ge(ri_done.sem, q + 1)
                    if q >= 2:
                        act.wait_ge(lru_scan.sem, q - 1)
                        act.wait_ge(lru_mid.sem, 3 * (q - 1))
                    act.activation(r, ps[:, bank, :], ACT.Sigmoid, bias=cols2[:, B_A + q:B_A + q + 1]
                                   ).then_inc(lru_a.sem, 1)
                    act.activation(i_, ps[:, bank + 1, :], ACT.Sigmoid, bias=cols2[:, B_X + q:B_X + q + 1]
                                   ).then_inc(lru_a.sem, 1)
                    act.wait_ge(lru_a.sem, 4 * q + 1)
                    act.activation(a_, r, ACT.Exp, scale=lru_s[:, 3, q:q + 1]).then_inc(lru_a.sem, 1)
                    act.wait_ge(lru_a.sem, 4 * q + 3)
                    act.activation(r, r, ACT.Tanh, scale=lru_s[:, 2, q:q + 1]).then_inc(lru_a.sem, 1)
                q -= 1
                if 0 <= q < LRU_TILES:
                    root = lru_t[q % 2][4]
                    act.wait_ge(lru_mid.sem, 3 * (q + 1))
                    act.activation(root, root, ACT.Sqrt, scale=2.0).then_inc(lru_root.sem, 1)

            act.wait_ge(d_small.sem, D_TABLES)
            for kind, n in first_products():
                if kind == "slot":
                    split2(n + 1)
                    if n == S5_FROM // 2 - 1:
                        tables(0)
                elif kind == "s5":
                    tables(n + 1)
                elif kind == "lru":
                    lru_step(n)
                else:
                    evac(n)
            for s in range(LRU_OUT_AT, GATE_S_AT):
                split2(s + 1)
            for n in range(S5_TILES):
                act.activation(u[:, n, :], u[:, n, :], ACT.Gelu_apprx_tanh).then_inc(gelued.sem, 1)
            for m in range(NM):
                if m % 2 == 0:
                    split2(GATE_S_AT + m // 2 + 1)
                wait_tile2(act, GATE_S_AT + m // 2, m % 2, before=before2[GATE_S_AT + m // 2])
                act.activation(gs[:, m, :], ps[:, m % 4, :], ACT.Sigmoid).then_inc(gs_done.sem, 1)
            for n in range(S5_TILES):
                s = GLU_AT + n // 2
                if n % 2 == 0:
                    split2(s + 1)
                wait_tile2(act, s, 2 * (n % 2) + 1, n=4, before=before2[s])
                if n >= 2:
                    act.wait_ge(ys_done.sem, n - 1)
                act.activation(tmp[:, n % 2, :], ps[:, 5 + 2 * (n % 2), :], ACT.Sigmoid).then_inc(glu_sig.sem, 1)
            split2(S5_OUT_AT + 1)
            split2(S5_OUT_AT + 2)
            for idx, m in enumerate(ORD):
                s = OUT_AT + idx // 2
                if idx % 2 == 0:
                    split2(s + 1)
                wait_tile2(act, s, idx % 2, before=before2[s])
                if idx == 0:
                    act.wait_ge(merged.sem, NM)
                act.activation(gs[:, m, :], ps[:, m, :], ACT.Copy).then_inc(o_copied.sem, 1)
                square(DEPTH, 2 * NM, idx, ps[:, m, :])
            split2(PLE_AT + 1)
            wait(act, summed, DEPTH, 3 * NM)
            act.activation(rstd, ps[:, SS_BANK, :], ACT.Sqrt, bias=eps, scale=1.0 / D).then_inc(rooted.sem, 1)
            for m in range(NM):
                wait_tile2(act, PLE_AT, m, n=NM, before=before2[PLE_AT])
                act.activation(gl[:, m, :], ps[:, PLE_BANKS[m], :], ACT.Copy).then_inc(ple_evac.sem, 1)
            for m in range(NM):
                s = PLE_GATE_AT + m // 2
                if m % 2 == 0:
                    split2(s + 1)
                wait_tile2(act, s, m % 2, before=before2[s])
                if m >= 2:
                    act.wait_ge(gate_step.sem, m - 1)
                act.activation(sq[:, m % 2, :], ps[:, PLE_BANKS[m], :], ACT.Sigmoid).then_inc(gate_sig.sem, 1)

        @block.vector
        def _(dve):
            steps = [0]

            def split(layer, s, more=0):
                buf = s % 2
                dve.wait_ge(hi_split.sem, hi_split.at(layer, s + 1) + more)
                dve.tensor_tensor(w_lo[:, buf, :], raw[buf][:], w_hi[:, buf, :].bitcast(F32), ALU.subtract
                                  ).then_inc(lo_split.sem, 1)

            def step(layer, ins):
                steps[0] += 1
                ins.then_inc(dve_step.sem, 1)
                wait(dve, dve_step, layer, steps[0])

            def scale_h(layer, stage):
                norm_no = 3 * layer + stage
                wait(dve, rooted, layer, stage + 1)
                dve.reciprocal(rstd, rstd).then_inc(inverted.sem, 1)
                wait(dve, inverted, layer, stage + 1)
                for m in range(NM):
                    n = stage * NM + m + 1
                    dve.scalar_tensor_tensor(out=tmp[:, m % 2, :], in0=x[:, m, :],
                                             scalar=gains[:, bass.ds(norm_no * NM + m, 1)], in1=rstd,
                                             op0=ALU.mult, op1=ALU.mult).then_inc(h_scaled.sem, 1)
                    wait(dve, h_scaled, layer, n)
                    dve.tensor_copy(h_hi[:, m, :], tmp[:, m % 2, :]).then_inc(h_hi_done.sem, 1)
                    wait(dve, h_hi_done, layer, n)
                    dve.tensor_tensor(h_lo[:, m, :], tmp[:, m % 2, :], h_hi[:, m, :].bitcast(F32), ALU.subtract
                                      ).then_inc(h_done.sem, 1)

            def ffn(layer, f, at):
                with dve.Fori(0, UP_SLOTS // 2) as j:
                    for i in range(2):
                        c = 2 * j + i
                        split(layer, at + i + 1, 2 * j)
                        dve.wait_ge(silued.sem, silued.at(layer, f * NF + 1) + c)
                        dve.wait_ge(bias_made.sem, 2 * c)
                        dve.wait_ge(a_done.sem, a_done.at(layer, f * NF + 1) + c)
                        dve.tensor_tensor(atmp, sil[:, i, :], ps[:, 2 * i + 1, :], ALU.mult).then_inc(a_prod.sem, 1)
                        dve.wait_ge(a_prod.sem, a_prod.at(layer, f * NF + 1) + c)
                        dve.tensor_copy(a_hi[:, c, :], atmp).then_inc(a_hi_done.sem, 1)
                        dve.wait_ge(a_hi_done.sem, a_hi_done.at(layer, f * NF + 1) + c)
                        dve.tensor_tensor(a_lo[:, c, :], atmp, a_hi[:, c, :].bitcast(F32), ALU.subtract
                                          ).then_inc(a_done.sem, 1)
                at += UP_SLOTS
                with dve.Fori(0, DOWN_SLOTS // 2) as j:
                    for i in range(2):
                        split(layer, at + i + 1, 2 * j)
                split(layer, at + DOWN_SLOTS)
                for idx, m in enumerate(ORD):
                    wait_tile(dve, layer, at + DOWN_SLOTS - 1, idx)
                    dve.scalar_tensor_tensor(out=x[:, m, :], in0=ps[:, m, :], scalar=0.5, in1=x[:, m, :],
                                             op0=ALU.mult, op1=ALU.add).then_inc(x_done.sem, 1)
                scale_h(layer, 1 if f == 0 else 3)

            def in_products(layer):
                for s in range(7):
                    split(layer, MIX_AT + s + 1)
                    t = 2 * s
                    wait_tile(dve, layer, MIX_AT + s, 0)
                    bank = ps[:, t % 4, :]
                    if t == 0:
                        wait(dve, cs_in, layer, 16)
                        ins = dve.tensor_tensor(k_prod[0:64, :], bank[0:64, :], cs[0:64, 1, :], ALU.mult)
                    elif t < 6:
                        ins = dve.tensor_copy(c_raw[:, t - 1, :], bank)
                    else:
                        ins = dve.tensor_scalar(qk[:, t - 6, :], bank, -SCALE["a" if t < 10 else "c"], None, ALU.mult)
                    ins.then_inc(dve_evac.sem, 1)
                for i in range(2):
                    wait(dve, c_rooted, layer, i + 1)
                    step(layer, dve.reciprocal(c_rstd[:, i, :], c_rstd[:, i, :]))
                for i in range(5):
                    step(layer, dve.scalar_tensor_tensor(
                        out=tmp[:, i % 2, :], in0=c_raw[:, i, :],
                        scalar=gains[:, bass.ds(LOW_RANK_GAINS + 5 * layer + i, 1)],
                        in1=c_rstd[:, 0 if i < 3 else 1, :], op0=ALU.mult, op1=ALU.mult))
                    step(layer, dve.tensor_copy(cn_hi[:, i, :], tmp[:, i % 2, :]))
                    dve.tensor_tensor(cn_lo[:, i, :], tmp[:, i % 2, :], cn_hi[:, i, :].bitcast(F32), ALU.subtract
                                      ).then_inc(c_done.sem, 1)
                split(layer, MIX_AT + 8)
                split(layer, MIX_AT + 9)
                for t in (0, 2):
                    wait_tile(dve, layer, MIX_AT + 8, t)
                    dve.tensor_copy(v_ac[:, t, :], ps[:, t, :]).then_inc(dve_evac.sem, 1)
                for s in (9, 10):
                    split(layer, MIX_AT + s + 1)
                    for i in range(4):
                        wait_tile(dve, layer, MIX_AT + s, i)
                        head = 4 * (s - 9) + i
                        dve.scalar_tensor_tensor(out=q_b[:, head, :], in0=ps[:, i, :], scalar=-SCALE["b"],
                                                 in1=cs[:, head % 2, :], op0=ALU.mult, op1=ALU.mult
                                                 ).then_inc(dve_evac.sem, 1)
                for t in range(NT):
                    wait_tile(dve, layer, MIX_AT + 11, 4 + t)
                    dve.tensor_copy(v_b[:, t, :], ps[:, 4 + t, :]).then_inc(dve_evac.sem, 1)

            def maxes(layer, u):
                wait(dve, score_done, layer, u + 1)
                if u >= 4:
                    wait(dve, exp_done, layer, u - 3)
                if UNITS[u][0] == "b":
                    dve.tensor_reduce(mneg[:, u % 4:u % 4 + 1], ps[:, u % 4, :], AX.X, ALU.min
                                      ).then_inc(max_done.sem, 1)
                    return
                n = BIASED.index(u)
                wait(dve, bias_in[n % 4], layer, 16 * (n // 4 + 1))
                dve.sem_inc(dve_met.sem, 1)
                dve.tensor_tensor_reduce(out=negs[:, u % 4, :], in0=bias_ring[:, n % 4, :], in1=ps[:, u % 4, :],
                                         scale=1.0, scalar=3e38, op0=ALU.add, op1=ALU.min,
                                         accum_out=mneg[:, u % 4:u % 4 + 1]).then_inc(max_done.sem, 1)

            def normalise(layer, u):
                kind, _, c, _ = UNITS[u]
                wait(dve, exp_done, layer, u + 1)
                r = rinv[:, u % 4:u % 4 + 1]
                p = probs[:, u % 4, :]
                step(layer, dve.reciprocal(r, rsum[:, u % 4:u % 4 + 1]))
                if kind != "c":
                    dve.tensor_scalar(p, p, r, None, ALU.mult).then_inc(p_done.sem, 1)
                elif c == 0:
                    step(layer, dve.tensor_scalar(p, p, r, None, ALU.mult))
                else:
                    rl = rinv[:, 4 + u % 4:5 + u % 4]
                    step(layer, dve.tensor_scalar(rl, r, nlam[:, bass.ds(layer, 1)], None, ALU.mult))
                    dve.scalar_tensor_tensor(out=p, in0=p, scalar=rl, in1=probs[:, (u - 1) % 4, :],
                                             op0=ALU.mult, op1=ALU.add).then_inc(p_done.sem, 1)

            def turned_out(layer, v):
                wait(dve, turned, layer, v + 1)
                if v >= 2 * NT:
                    wait(dve, pv_done, layer, v // NT - 1)
                q = v % NT
                dve.tensor_copy(pt[:, (v // NT) % 2, :, q * P:(q + 1) * P],
                                ps[:, 4 + v % 2, :].rearrange("p (k n) -> p k n", k=NT)).then_inc(pt_dve.sem, 1)

            def pair_out(layer, pair):
                wait(dve, pv_done, layer, 2 * pair + 2)
                bank = ps[:, 6 + pair % 2, :]
                if pair < 2:
                    dve.tensor_copy(tmp[:, pair, :], bank).then_inc(pv_taken.sem, 1)
                    return
                tile = PAIR_TILE[pair]
                step(layer, dve.tensor_copy(mix_hi[:, tile, :], bank))
                dve.tensor_tensor(mix_lo[:, tile, :], bank, mix_hi[:, tile, :].bitcast(F32), ALU.subtract
                                  ).then_inc(pv_taken.sem, 1)

            def attention(layer):
                for u in range(len(UNITS) + 6):
                    if u < len(UNITS):
                        maxes(layer, u)
                    if 1 <= u <= len(UNITS):
                        normalise(layer, u - 1)
                    v = TURNS.index(u - 4) if u - 4 in TURNS else 0
                    if v % 2 == 1:
                        turned_out(layer, v)
                    v = TURNS.index(u - 5) if u - 5 in TURNS else 0
                    if v % (2 * NT) == 2 * NT - 1:
                        pair_out(layer, v // (2 * NT))
                    if u == OC_NORM_AT + 3:
                        for i in range(2):
                            wait(dve, oc_rooted, layer, i + 1)
                            step(layer, dve.reciprocal(sq[:, i, :], sq[:, i, :]))
                            step(layer, dve.scalar_tensor_tensor(
                                out=tmp[:, i, :], in0=tmp[:, i, :], scalar=gain_c[:, bass.ds(layer, 1)],
                                in1=sq[:, i, :], op0=ALU.mult, op1=ALU.mult))
                            step(layer, dve.tensor_copy(mix_hi[:, 6 + i, :], tmp[:, i, :]))
                            dve.tensor_tensor(mix_lo[:, 6 + i, :], tmp[:, i, :], mix_hi[:, 6 + i, :].bitcast(F32),
                                              ALU.subtract).then_inc(oc_mixed.sem, 1)

            def out_products(layer):
                split(layer, MIX_AT + 12)
                for s in range(12, 16):
                    split(layer, MIX_AT + s + 1)
                    for i in range(2):
                        m = ORD[2 * (s - 12) + i]
                        wait_tile(dve, layer, MIX_AT + s, i)
                        dve.tensor_tensor(x[:, m, :], ps[:, m, :], x[:, m, :], ALU.add).then_inc(x_done.sem, 1)
                scale_h(layer, 2)

            n_pro = [0]

            def pro(ins):
                n_pro[0] += 1
                ins.then_inc(pro_step.sem, 1)
                dve.wait_ge(pro_step.sem, n_pro[0])

            dve.memset(mneg[:], 0.0).then_inc(a_done.sem, 1)
            split(0, 0)
            dve.wait_ge(inputs_in.sem, 64)
            for l in range(DEPTH):
                for i in range(2):
                    pro(dve.tensor_tensor(tmp[:, 0, 0:DIFF_QK], lamv[:, l, 2 * i, :], lamv[:, l, 2 * i + 1, :], ALU.mult))
                    pro(dve.tensor_reduce(lam_s[:, 2 * i + l:2 * i + l + 1], tmp[:, 0, 0:DIFF_QK], AX.X, ALU.add))
            dve.memset(rsum[:], 0.0).then_inc(dve_pro.sem, 1)
            dve.wait_ge(pos_in.sem, 48)
            pro(dve.tensor_copy(pos_r[:], pos_i[:]))
            pro(dve.tensor_copy(pcol[:], pcol_i[:]))
            for q in range(NT):
                pro(dve.tensor_scalar(rot[:, 0, :], pos_r[:], pcol[:, q:q + 1], None, ALU.subtract))
                dve.scalar_tensor_tensor(out=dist[:, q, :], in0=rot[:, 0, :], scalar=-1.0, in1=rot[:, 0, :],
                                         op0=ALU.mult, op1=ALU.max).then_inc(dist_done.sem, 1)
                dve.wait_ge(dist_done.sem, q + 1)
            pro(dve.tensor_scalar(rot[:, 0, :], pos_r[:], cols[:, 2:3], None, ALU.mult))
            pro(dve.tensor_scalar(rot[:, 1, :], rot[:, 0, :], 1.0 / (2 * PI), MAGIC, ALU.mult, ALU.add))
            pro(dve.tensor_scalar(rot[:, 1, :], rot[:, 1, :], MAGIC, None, ALU.subtract))
            pro(dve.scalar_tensor_tensor(out=rot[:, 2, :], in0=rot[:, 1, :], scalar=-TURN_HI, in1=rot[:, 0, :],
                                         op0=ALU.mult, op1=ALU.add))
            pro(dve.scalar_tensor_tensor(out=rot[:, 2, :], in0=rot[:, 1, :], scalar=-TURN_LO, in1=rot[:, 2, :],
                                         op0=ALU.mult, op1=ALU.add))
            dve.tensor_scalar(rot[:, 2, :], rot[:, 2, :], PI_DOWN, -PI_DOWN, ALU.min, ALU.max).then_inc(dve_pro.sem, 1)
            dve.wait_ge(act_step.sem, 2)
            pro(dve.tensor_tensor(nlam[:], lam_s[:, 6:8], lam_s[:, 4:6], ALU.subtract))
            pro(dve.tensor_tensor(nlam[:], nlam[:], cols[:, 9:11], ALU.subtract))
            pro(dve.tensor_tensor(gain_c[:], gains[:, C_GAINS:C_GAINS + 2], cols[:, 11:13], ALU.mult))
            dve.wait_ge(act_step.sem, 5)
            for i in range(2):
                mc, ms, mo = (cols[:, 3 + 3 * i + n:4 + 3 * i + n] for n in range(3))
                pro(dve.tensor_scalar(table2[:, i, :], rot[:, 1, :], mc, mo, ALU.mult, ALU.add))
                pro(dve.scalar_tensor_tensor(out=table2[:, i, :], in0=rot[:, 0, :], scalar=ms, in1=table2[:, i, :],
                                             op0=ALU.mult, op1=ALU.add))
            dve.memset(rsum[:], 0.0).then_inc(cs_made.sem, 1)
            scale_h(0, 0)
            dve.wait_ge(cs_out.sem, 16)
            with dve.Fori(0, DEPTH) as layer:
                ffn(layer, 0, 0)
                in_products(layer)
                attention(layer)
                out_products(layer)
                ffn(layer, 1, FFN2_AT)
            assert steps[0] == DVE_STEPS

            def split2(s):
                if s < SLOTS_2:
                    split(DEPTH, s)

            small = [0]

            def small_step(ins):
                small[0] += 1
                ins.then_inc(d_small.sem, 1)
                dve.wait_ge(d_small.sem, small[0])
                return small[0]

            for m in range(NM):
                wait(dve, h_done, DEPTH, m + 1)
                dve.tensor_tensor(x[:, m, :], h_hi[:, m, :].bitcast(F32), h_lo[:, m, :].bitcast(F32), ALU.add
                                  ).then_inc(x_again.sem, 1)
            dve.wait_ge(x_again.sem, NM)
            dve.memset(lrux[:, :, 0:PAD], 0.0).then_inc(pads_done.sem, 1)
            scale_h(DEPTH, 1)
            sw = [s5w[:, n, :] for n in range(24)]
            re, im, dt, decay, turn, sin, cos = s5p[:, 0, :], s5p[:, 1, :], sw[0], sw[3], sw[5], sw[6], sw[7]
            dve.wait_ge(s5_in.sem, 64)
            dve.wait_ge(a_small.sem, 1)
            small_step(dve.tensor_tensor(sw[1], im, dt, ALU.mult))
            assert small_step(dve.tensor_tensor(sw[2], re, dt, ALU.mult)) == D_DECAY
            small_step(dve.tensor_scalar(sw[1], sw[1], 1.0 / (2 * PI), None, ALU.mult))
            small_step(dve.tensor_scalar(sw[4], sw[1], MAGIC, None, ALU.add))
            small_step(dve.tensor_scalar(sw[4], sw[4], MAGIC, None, ALU.subtract))
            assert small_step(dve.tensor_tensor(turn, sw[1], sw[4], ALU.subtract)) == D_ANGLE
            dve.wait_ge(cols2_in.sem, 16)
            lam = cols2[:, LAM:LAM + LRU_TILES]
            small_step(dve.tensor_scalar(lru_s[:, 2, :], lam, -1.0, None, ALU.mult))
            assert small_step(dve.tensor_tensor(lru_s[:, 0, :], lam, lru_s[:, 2, :], ALU.max)) == D_LAM
            dve.wait_ge(a_small.sem, 6)
            small_step(dve.tensor_scalar(lru_s[:, 1, :], lru_s[:, 1, :], 1.0, None, ALU.add))
            small_step(dve.tensor_tensor(sw[8], decay, cos, ALU.mult))
            small_step(dve.tensor_scalar(sw[8], sw[8], -1.0, None, ALU.add))
            small_step(dve.tensor_tensor(sw[9], decay, sin, ALU.mult))
            small_step(dve.tensor_tensor(sw[10], re, re, ALU.mult))
            small_step(dve.tensor_tensor(sw[11], im, im, ALU.mult))
            small_step(dve.tensor_tensor(sw[10], sw[10], sw[11], ALU.add))
            small_step(dve.reciprocal(sw[10], sw[10]))
            for dst, (x0, y0), (x1, y1), op in ((12, (8, re), (9, im), ALU.add), (13, (9, re), (8, im), ALU.subtract)):
                small_step(dve.tensor_tensor(sw[14], sw[x0], y0, ALU.mult))
                small_step(dve.tensor_tensor(sw[15], sw[x1], y1, ALU.mult))
                small_step(dve.tensor_tensor(sw[14], sw[14], sw[15], op))
                small_step(dve.tensor_tensor(sw[dst], sw[14], sw[10], ALU.mult))
            z_re, z_im = (sw[n].unsqueeze(2).to_broadcast([P, S5_PAIRS, 32]) for n in (12, 13))
            c_re, c_im = (s5c_in[:, n, :].rearrange("p (g c) -> p g c", c=32) for n in range(2))
            t0, t1 = (s5t[:, n, :].rearrange("p (g c) -> p g c", c=32) for n in range(2))
            small_step(dve.tensor_tensor(t0, c_re, z_re, ALU.mult))
            small_step(dve.tensor_tensor(t1, c_im, z_im, ALU.mult))
            small_step(dve.tensor_tensor(s5c[:, 0, :], s5t[:, 0, :], s5t[:, 1, :], ALU.subtract))
            small_step(dve.tensor_tensor(t0, c_re, z_im, ALU.mult))
            small_step(dve.tensor_tensor(t1, c_im, z_re, ALU.mult))
            small_step(dve.scalar_tensor_tensor(out=s5c[:, 1, :], in0=s5t[:, 0, :], scalar=-1.0, in1=s5t[:, 1, :],
                                                op0=ALU.mult, op1=ALU.subtract))
            dve.wait_ge(a_small.sem, 7)
            small_step(dve.tensor_scalar(lru_s[:, 2, :], lru_s[:, 2, :], 0.0, None, ALU.max))
            small_step(dve.tensor_tensor(lru_s[:, 2, :], lru_s[:, 2, :], lru_s[:, 1, :], ALU.add))
            small_step(dve.tensor_scalar(lru_s[:, 2, :], lru_s[:, 2, :], 8.0, None, ALU.mult))
            assert small_step(dve.tensor_scalar(lru_s[:, 3, :], lru_s[:, 2, :], -1.0, None, ALU.mult)) == D_TABLES
            dve.memset(rsum[:], 0.0).then_inc(s5_ready.sem, 1)

            def tables(p):
                if p >= S5_PAIRS:
                    return
                f, per_step = tmp[:, 0, :], turn[:, p:p + 1]
                if p >= 1:
                    dve.wait_ge(table_a.sem, 3 * p)
                dve.tensor_scalar(f, tidx[:], per_step, MAGIC, ALU.mult, ALU.add).then_inc(table_d.sem, 1)
                dve.wait_ge(table_d.sem, 3 * p + 1)
                dve.tensor_scalar(f, f, MAGIC, None, ALU.subtract).then_inc(table_d.sem, 1)
                dve.wait_ge(table_d.sem, 3 * p + 2)
                dve.scalar_tensor_tensor(out=f, in0=tidx[:], scalar=per_step, in1=f, op0=ALU.mult, op1=ALU.subtract
                                         ).then_inc(table_d.sem, 1)

            def s5_step(p):
                tables(p + 1)
                if p < S5_PAIRS:
                    t = 4 * (p % 2)
                    cos_, sin_ = (cos_sin[p % 2][:, n, :] for n in range(2))
                    dve.wait_ge(bu_done.sem, p + 1)
                    dve.wait_ge(table_a.sem, 3 * (p + 1))
                    if p >= 2:
                        dve.wait_ge(s5_out.sem, p - 1)
                        dve.wait_ge(h_re_done.sem, p - 1)
                    for n, (bank, by) in enumerate(((4, cos_), (5, sin_), (5, cos_), (4, sin_))):
                        dve.tensor_tensor(s5t[:, t + n, :], ps[:, bank, :], by, ALU.mult).then_inc(pre_done.sem, 1)
                p -= 1
                if 0 <= p < S5_PAIRS:
                    t = 4 * (p % 2)
                    cos_, sin_ = (cos_sin[p % 2][:, n, :] for n in range(2))
                    dve.wait_ge(pre_sum.sem, 2 * (p + 1))
                    for n in range(2):
                        dve.tensor_tensor_scan(s5t[:, t + 2 * n + 1, :], decay[:, p:p + 1].to_broadcast([P, T]),
                                               s5t[:, t + 2 * n, :], 0.0, ALU.mult, ALU.add).then_inc(scan_done.sem, 1)
                    dve.wait_ge(scan_done.sem, 2 * (p + 1))
                    dve.tensor_tensor(s5h_re[p % 2], s5t[:, t + 1, :], cos_, ALU.mult).then_inc(post_d.sem, 1)
                    dve.tensor_tensor(tmp[:, 1, :], s5t[:, t + 3, :], sin_, ALU.mult).then_inc(post_d.sem, 1)
                    dve.wait_ge(post_d.sem, 2 * (p + 1))
                    dve.tensor_tensor(s5h_re[p % 2], s5h_re[p % 2], tmp[:, 1, :], ALU.subtract
                                      ).then_inc(h_re_done.sem, 1)
                    dve.wait_ge(h_re_done.sem, p + 1)
                if p % 4 == 1 and p >= 5:
                    s5_result(p // 4 - 1)

            def s5_result(tile):
                dve.wait_ge(s5_out.sem, 4 * (tile + 1))
                dve.scalar_tensor_tensor(out=u[:, tile, :], in0=u[:, tile, :],
                                         scalar=cols2[:, D_SKIP + tile:D_SKIP + tile + 1],
                                         in1=ps[:, 6 + tile % 2, :], op0=ALU.mult, op1=ALU.add).then_inc(s5_y.sem, 1)

            def lru_step(q):
                if q < LRU_TILES:
                    c = lru_t[q % 2][0]
                    if q == 0:
                        dve.wait_ge(pads_done.sem, 1)
                        dve.wait_ge(s5_out.sem, S5_PAIRS)
                    if q >= 2:
                        dve.wait_ge(lru_ic.sem, q - 1)
                        dve.wait_ge(ri_done.sem, q - 1)
                    dve.wait_ge(evac2.sem, 2 * LRU_X_AT + q + 1)
                    w = [cols2[:, CONV_W + LRU_TILES * n + q:CONV_W + LRU_TILES * n + q + 1] for n in range(CONV)]
                    dve.tensor_scalar(c, lrux[:, q, 0:T], w[0], cols2[:, CONV_B + q:CONV_B + q + 1], ALU.mult, ALU.add
                                      ).then_inc(conv_step.sem, 1)
                    for n in range(1, CONV):
                        dve.wait_ge(conv_step.sem, 3 * q + n)
                        dve.scalar_tensor_tensor(out=c, in0=lrux[:, q, n:n + T], scalar=w[n], in1=c,
                                                 op0=ALU.mult, op1=ALU.add
                                                 ).then_inc((conv_step if n < CONV - 1 else conv_done).sem, 1)
                if 0 <= q - 1 < LRU_TILES:
                    q1 = q - 1
                    _, th, _, _, root = lru_t[q1 % 2]
                    dve.wait_ge(lru_a.sem, 4 * (q1 + 1))
                    if q1 >= 2:
                        dve.wait_ge(lru_y.sem, q1 - 1)
                    dve.tensor_scalar(root, th, 1.0, None, ALU.add).then_inc(lru_mid.sem, 1)
                    dve.wait_ge(lru_mid.sem, 3 * q1 + 1)
                    dve.reciprocal(root, root).then_inc(lru_mid.sem, 1)
                    dve.wait_ge(lru_mid.sem, 3 * q1 + 2)
                    dve.tensor_tensor(root, root, th, ALU.mult).then_inc(lru_mid.sem, 1)
                if 0 <= q - 2 < LRU_TILES:
                    q2 = q - 2
                    _, _, i_, a_, y = lru_t[q2 % 2]
                    dve.wait_ge(lru_b.sem, q2 + 1)
                    dve.tensor_tensor_scan(y, a_, i_, 0.0, ALU.mult, ALU.add).then_inc(lru_scan.sem, 1)
                    dve.wait_ge(lru_scan.sem, q2 + 1)
                    dve.wait_ge(evac2.sem, 2 * LRU_G_AT + q2 + 1)
                    dve.tensor_tensor(slg[:, q2, :], y, slg[:, q2, :], ALU.mult).then_inc(lru_y.sem, 1)

            for kind, n in first_products():
                if kind == "slot":
                    split2(n + 1)
                    if n == S5_FROM // 2 - 1:
                        tables(0)
                elif kind == "s5":
                    s5_step(n)
                elif kind == "lru":
                    lru_step(n)
            for k in range(LRU_TILES):
                if k == 0:
                    dve.wait_ge(lru_y.sem, LRU_TILES)
                if k >= 2:
                    if k % 2 == 0:
                        dve.wait_ge(yl_used.sem, k // 2)
                    else:
                        wait(dve, slot_used, DEPTH, LRU_OUT_AT + k // 2)
                dve.tensor_copy(yl_hi[:, k % 2, :], slg[:, k, :]).then_inc(yl_hi_done.sem, 1)
                dve.wait_ge(yl_hi_done.sem, k + 1)
                dve.tensor_tensor(yl_lo[:, k % 2, :], slg[:, k, :], yl_hi[:, k % 2, :].bitcast(F32), ALU.subtract
                                  ).then_inc(yl_done.sem, 1)
                if k % 2 == 1:
                    split2(LRU_OUT_AT + k // 2 + 1)
            for m in range(NM):
                wait_tile2(dve, GATE_S_AT - 1, m, n=NM, before=before2[GATE_S_AT - 1])
                dve.tensor_tensor(gl[:, m, :], ps[:, m, :], gl[:, m, :], ALU.mult).then_inc(z_taken.sem, 1)
            for s in range(GATE_S_AT, GLU_AT - 1):
                split2(s + 1)
                if s == GATE_S_AT:
                    for n in range(S5_TILES):
                        dve.wait_ge(gelued.sem, n + 1)
                        dve.tensor_copy(g_hi[:, n, :], u[:, n, :]).then_inc(g_hi_done.sem, 1)
                        dve.wait_ge(g_hi_done.sem, n + 1)
                        dve.tensor_tensor(g_lo[:, n, :], u[:, n, :], g_hi[:, n, :].bitcast(F32), ALU.subtract
                                          ).then_inc(g_done.sem, 1)
                if s == GATE_S_AT + 1:
                    dve.wait_ge(p_in.sem, 16)
                    dve.wait_ge(g_done.sem, S5_TILES)
                    for n in range(PLE_TILES):
                        dve.tensor_copy(p_hi[:, n, :], wide[:, n, :]).then_inc(p_split.sem, 1)
                        dve.wait_ge(p_split.sem, 2 * n + 1)
                        dve.tensor_tensor(p_lo[:, n, :], wide[:, n, :], p_hi[:, n, :].bitcast(F32), ALU.subtract
                                          ).then_inc(p_split.sem, 1)
            split2(GLU_AT)
            for n in range(S5_TILES):
                if n % 2 == 0:
                    split2(GLU_AT + n // 2 + 1)
                t = tmp[:, n % 2, :]
                dve.wait_ge(glu_sig.sem, n + 1)
                dve.tensor_tensor(t, ps[:, 4 + 2 * (n % 2), :], t, ALU.mult).then_inc(glu_prod.sem, 1)
                dve.wait_ge(glu_prod.sem, n + 1)
                dve.tensor_tensor(t, t, ssg[:, n, :], ALU.mult).then_inc(glu_step.sem, 1)
                dve.wait_ge(glu_step.sem, 2 * n + 1)
                dve.tensor_copy(ys_hi[:, n, :], t).then_inc(glu_step.sem, 1)
                dve.wait_ge(glu_step.sem, 2 * n + 2)
                dve.tensor_tensor(ys_lo[:, n, :], t, ys_hi[:, n, :].bitcast(F32), ALU.subtract).then_inc(ys_done.sem, 1)
            for m in range(NM):
                s = S5_OUT_AT + m // 4
                if m % 4 == 0:
                    split2(s + 1)
                wait_tile2(dve, s, m % 4, n=4, before=before2[s])
                dve.tensor_tensor(gs[:, m, :], ps[:, m % 4, :], gs[:, m, :], ALU.mult).then_inc(bs_taken.sem, 1)
                dve.wait_ge(bs_taken.sem, m + 1)
                dve.tensor_tensor(gl[:, m, :], gl[:, m, :], gs[:, m, :], ALU.add).then_inc(merge_step.sem, 1)
                dve.wait_ge(merge_step.sem, 2 * m + 1)
                dve.tensor_copy(mix_hi[:, m, :], gl[:, m, :]).then_inc(merge_step.sem, 1)
                dve.wait_ge(merge_step.sem, 2 * m + 2)
                dve.tensor_tensor(mix_lo[:, m, :], gl[:, m, :], mix_hi[:, m, :].bitcast(F32), ALU.subtract
                                  ).then_inc(merged.sem, 1)
            for s in range(OUT_AT, OUT_AT + 4):
                split2(s + 1)
            split2(PLE_AT + 1)
            wait(dve, rooted, DEPTH, 3)
            dve.reciprocal(rstd, rstd).then_inc(inverted.sem, 1)
            wait(dve, inverted, DEPTH, 3)
            for m in range(NM):
                t = tmp[:, m % 2, :]
                dve.scalar_tensor_tensor(out=t, in0=gs[:, m, :], scalar=cols2[:, G_POST + m:G_POST + m + 1], in1=rstd,
                                         op0=ALU.mult, op1=ALU.mult).then_inc(o_step.sem, 1)
                dve.wait_ge(o_step.sem, 3 * m + 1)
                dve.tensor_tensor(x[:, m, :], x[:, m, :], t, ALU.add).then_inc(o_step.sem, 1)
                dve.wait_ge(o_step.sem, 3 * m + 2)
                dve.tensor_copy(h_hi[:, m, :], x[:, m, :]).then_inc(o_step.sem, 1)
                dve.wait_ge(o_step.sem, 3 * m + 3)
                dve.tensor_tensor(h_lo[:, m, :], x[:, m, :], h_hi[:, m, :].bitcast(F32), ALU.subtract
                                  ).then_inc(xs_done.sem, 1)
            for m in range(NM):
                s = PLE_GATE_AT + m // 2
                if m % 2 == 0:
                    split2(s + 1)
                dve.wait_ge(gate_sig.sem, m + 1)
                dve.wait_ge(ple_evac.sem, m + 1)
                dve.tensor_tensor(gl[:, m, :], gl[:, m, :], sq[:, m % 2, :], ALU.mult).then_inc(gate_step.sem, 1)
                dve.wait_ge(gate_step.sem, m + 1)
                dve.tensor_tensor(x[:, m, :], x[:, m, :], gl[:, m, :], ALU.add).then_inc(fin.sem, 1)


def _blocks(w):
    k, m = w.shape
    return w.reshape(k // P, P, m // P, P).transpose(0, 2, 1, 3)


def _slot(blocks):
    out = np.zeros((P, SLOT), np.float32)
    n = len(blocks)
    out[:, :n * P] = np.asarray(blocks).transpose(1, 0, 2).reshape(P, n * P)
    return out


def _ffn_slots(gate, up, down):
    g, u, d = _blocks(gate), _blocks(up), _blocks(down)
    for c in range(NF):
        yield _slot([w[k, c] for k in range(NM) for w in (g, u)])
    for j in range(DOWN_SLOTS):
        yield _slot([d[2 * j + n, m] for m in ORD for n in range(2)])


def _mixer_slots(w_in, w_uq, w_ukv, w_out):
    cols = np.arange(w_in.shape[1] + 1)
    a0, b0, c0 = 0, A_COLS, A_COLS + B_COLS
    kpe = b0 + Q_LORA + KV_LORA
    swap = list(range(16, 32)) + list(range(16))
    w_pad = np.concatenate([w_in, np.zeros((D, 1), np.float32)], axis=1)
    zero = [w_in.shape[1]] * 64
    tile = lambda at: list(range(at, at + P))
    tiles = [[kpe + i for i in range(32)] + [kpe + i for i in swap] + zero]
    tiles += [tile(b0 + P * i) for i in range(5)]
    for i in range(2):
        tiles += [tile(a0 + P * i), tile(a0 + 256 + P * i)]
    for i in range(2):
        tiles += [tile(c0 + P * i), tile(c0 + 256 + P * i)]
    b = [_blocks(w_pad[:, t])[:, 0] for t in tiles]
    for s in range(7):
        yield _slot(list(b[2 * s]) + list(b[2 * s + 1]))
    v = _blocks(w_in[:, list(range(a0 + 512, a0 + 768)) + list(range(c0 + 512, c0 + 768))])
    for s in range(2):
        yield _slot([v[4 * s + k, n] for k in range(4) for n in range(4)])
    heads = []
    for h in range(HEADS_B):
        q = h * (NOPE + ROPE)
        nope, rope = [q + i for i in range(NOPE)], [q + NOPE + i for i in range(ROPE)]
        swapped = [q + NOPE + i for i in swap]
        heads.append(_blocks(w_uq[:, nope + rope + swapped if h % 2 == 0 else rope + swapped + nope])[:, 0])
    for s in range(2):
        yield _slot([heads[4 * s + i][k] for i in range(4) for k in range(3)])
    keys = _blocks(w_ukv[:, [h * 128 + i for h in range(HEADS_B) for i in range(64)]])
    vals = _blocks(w_ukv[:, [h * 128 + 64 + i for h in range(HEADS_B) for i in range(64)]])
    yield _slot([keys[k, i] for i in range(4) for k in range(2)] + [vals[k, n] for k in range(2) for n in range(4)])
    o = _blocks(w_out)
    for j in range(4):
        yield _slot([o[k, ORD[2 * j + i]] for i in range(2) for k in range(NM)])


def _second_slots(g):
    w_in = _blocks(g["w_in_2"][0])
    x_s, g_s, x_l = range(0, 4), range(4, 8), range(8, 18)
    g_l, gate_s, gate_l = range(18, 28), range(28, 36), range(36, 44)

    def pairs(w, tiles):
        tiles = list(tiles)
        return [_slot([w[k, t] for t in tiles[i:i + 2] for k in range(NM)]) for i in range(0, len(tiles), 2)]

    out = []
    for tiles in (x_s, x_l, g_l, g_s, gate_l):
        out += pairs(w_in, tiles)
    w_bl, w_glu, w_bs = _blocks(g["w_bl_2"][0]), _blocks(g["w_glu_2"][0]), _blocks(g["w_bs_2"][0])
    out += [_slot([w_bl[2 * s + n, m] for n in range(2) for m in range(NM)]) for s in range(LRU_TILES // 2)]
    out += pairs(w_in, gate_s)
    out += [_slot([w_glu[k, t] for i in (0, 1) for t in (2 * s + i, 4 + 2 * s + i) for k in range(4)]) for s in range(2)]
    out += [_slot([w_bs[k, 4 * s + i] for i in range(4) for k in range(4)]) for s in range(2)]
    out += pairs(_blocks(g["w_out_2"][0]), ORD)
    w_ple = _blocks(g["w_ple_2"][0])
    out += [_slot([w_ple[k, m] for m in range(NM) for k in range(2)])]
    out += pairs(_blocks(g["w_ple_gate_2"][0]), range(NM))
    assert len(out) == SLOTS_2
    return out


def _s5_arrays(g):
    by_state = lambda v: v.reshape(S5_PAIRS, 2 * STATES).T
    log_dt = np.repeat(g["s5_log_dt_2"][0][:, None], STATES, axis=1)
    s5p = np.stack([by_state(v) for v in (g["s5_a_re_2"][0], g["s5_a_im_2"][0], log_dt)], axis=1)
    s5b = np.zeros((P, S5_TILES, 2, P), np.float32)
    s5c = np.zeros((P, 2, S5_PAIRS, 32), np.float32)
    for ri, part in enumerate(("re", "im")):
        b, c = g[f"s5_b_{part}_2"][0], g[f"s5_c_{part}_2"][0]
        for group in range(2 * S5_PAIRS):
            pair, n = divmod(group, 2)
            row = 32 * (pair % 4) + 16 * n
            s5b[row:row + 16, pair // 4, ri, 64 * n:64 * n + 64] = b[group].T
            s5c[64 * n:64 * n + 64, ri, pair, 16 * n:16 * n + 16] = c[group].T
    return s5p, s5b, s5c.reshape(P, 2, S5_PAIRS * 32)


def _columns(v):
    return v.reshape(-1, P).T


def _constants():
    cols = np.zeros((P, 16), np.float32)
    p = np.arange(P)
    cols[:, 0] = EPS
    cols[:, 1] = PI / 2
    half = ROPE // 2
    inv = (np.float32(10000.0) ** (-np.arange(half, dtype=np.float32) / np.float32(half))).astype(np.float32)
    cols[:, 2] = inv[p % half]
    sign = np.where(p % 32 < 16, -1.0, 1.0)
    for i, group in enumerate(((2, 2, 0, 1), (0, 1, 2, 2))):
        kind = np.array(group)[p // 32]
        cols[:, 3 + 3 * i] = kind == 0
        cols[:, 4 + 3 * i] = (kind == 1) * sign
        cols[:, 5 + 3 * i] = kind == 2
    cols[:, 9:11] = LAM_INIT
    cols[:, 11:13] = 1.0 - np.array(LAM_INIT)
    mats = np.zeros((P, 4, P), np.float32)
    mats[:, 0] = np.eye(P)
    mats[:, 1] = 1.0
    mats[:, 2] = p[:, None] // 64 == p[None, :] // 64
    mats[:, 3] = p[:, None] % 32 == p[None, :] % 32
    d = np.abs(p[:, None] - np.arange(2 * T - P)[None, :] + (T - P))
    count = (d <= 64).astype(int) + ((d % 4 == 0) & (d <= 256)) + ((d % 16 == 0) & (d <= 1024))
    reach = np.where(count > 0, -np.log(np.maximum(count, 1)), FAR).astype(np.float32)
    return cols, mats, reach


def kernel(**inputs):
    import concourse.bacc as bacc
    from concourse.bass_utils import run_bass_kernel_spmd

    g = {k: np.ascontiguousarray(v) for k, v in inputs.items()}
    slots = []
    for l in range(DEPTH):
        slots += _ffn_slots(g["ffn1_w_gate"][l], g["ffn1_w_up"][l], g["ffn1_w_down"][l])
        slots += _mixer_slots(g["w_in"][l], g["mla_w_uq"][l], g["mla_w_ukv"][l], g["w_out"][l])
        slots += _ffn_slots(g["ffn2_w_gate"][l], g["ffn2_w_up"][l], g["ffn2_w_down"][l])
    slots += _second_slots(g)
    cols, mats, reach = _constants()
    gains = [_columns(v) for l in range(DEPTH) for v in (g["ffn1_norm"][l], g["mix_norm"][l], g["ffn2_norm"][l])]
    gains += [_columns(g["final_norm"]), _columns(g["g_pre_2"][0])]
    for l in range(DEPTH):
        gains += [_columns(g["mla_q_norm"][l]), _columns(g["mla_kv_norm"][l])]
    gains += [np.tile(g["diff_head_norm"][l], 2)[:, None] for l in range(DEPTH)]
    s5p, s5b, s5c = _s5_arrays(g)
    lam = np.stack([g["diff_lambda_" + n] for n in ("q1", "k1", "q2", "k2")], axis=1)
    arrays = {
        "x": g["x"][0].T.reshape(NM, P, T).transpose(1, 0, 2),
        "stream": np.stack(slots),
        "cols": cols, "mats": mats, "reach": reach,
        "gains": np.concatenate(gains, axis=1),
        "lamv": np.broadcast_to(lam[None], (P,) + lam.shape),
        "s5p": s5p, "s5b": s5b, "s5c": s5c,
        "tidx": np.broadcast_to(np.arange(T, dtype=np.float32) - T // 2, (P, T)),
        "w_lru": np.stack([g["lru_w_a_2"][0], g["lru_w_x_2"][0]], axis=1).reshape(2 * LRU_TILES, P, P).transpose(1, 0, 2),
        "p": g["p_2"][0, 0].T.reshape(PLE_TILES, P, T).transpose(1, 0, 2),
        "cols2": np.concatenate([_columns(v) for v in (
            g["s5_d_2"][0], *g["conv_w_2"][0], g["conv_b_2"][0], g["lru_b_a_2"][0], g["lru_b_x_2"][0],
            g["lru_lambda_2"][0], g["g_post_2"][0])], axis=1),
        "pos": g["positions"][0], "pos_col": g["positions"][0].reshape(NT, P).T,
    }
    arrays = {k: np.ascontiguousarray(v) for k, v in arrays.items()}
    nc = bacc.Bacc("TRN2", target_bir_lowering=False, num_devices=1)
    aps = {k: nc.dram_tensor("in_" + k, v.shape, mybir.dt.from_np(v.dtype), kind="ExternalInput").ap()
           for k, v in arrays.items()}
    aps["out"] = nc.dram_tensor("out", (P, NM, T), F32, kind="ExternalOutput").ap()
    build(nc, aps)
    r = run_bass_kernel_spmd(nc, [{"in_" + k: v for k, v in arrays.items()}], core_ids=[0])
    return r.results[0]["out"].transpose(1, 0, 2).reshape(1, D, T).transpose(0, 2, 1)
```

```python
from contextlib import ExitStack
import math

import numpy as np

import concourse.bass as bass
from concourse import mybir

F32 = mybir.dt.float32
F32R = mybir.dt.float32r
I32 = mybir.dt.int32
ACT = mybir.ActivationFunctionType
ALU = mybir.AluOpType
AX = mybir.AxisListType

P = 128
T = 512
D = 1024
NM = D // P
DEPTH = 2
D_FF = 2816
NF = D_FF // P
NT = T // P
HEADS_A, HEADS_B, HEADS_C = 4, 8, 4
NOPE, ROPE, V_DIM, DIFF_QK = 64, 32, 64, 32
Q_LORA, KV_LORA = 384, 256
A_COLS = 3 * HEADS_A * 64
B_COLS = Q_LORA + KV_LORA + ROPE
EPS = 1e-6
FAR = 1e30

BLOCKS = 16
SLOT = BLOCKS * P
ORD = [4, 5, 6, 7, 0, 1, 2, 3]
SS_BANK = ORD[0]

UP_SLOTS = NF
DOWN_SLOTS = NF // 2
FFN_SLOTS = UP_SLOTS + DOWN_SLOTS
MIX_SLOTS = 16
LAYER_SLOTS = 2 * FFN_SLOTS + MIX_SLOTS
MIX_AT = FFN_SLOTS
FFN2_AT = FFN_SLOTS + MIX_SLOTS

SQ_LAYER = 3 * NM + 2
SUM_LAYER = 5
GATHERED = 6

TILES = [1] * (FFN_SLOTS - 1) + [NM] + [2] * 7 + [1, 4, 4, 4, 8] + [2] * 4 + [1] * (FFN_SLOTS - 1) + [NM]
EARLIER = [sum(n - 1 for n in TILES[:s]) for s in range(LAYER_SLOTS + 1)]

UNITS = ([("c", h, c, q) for h in range(HEADS_C) for q in range(NT) for c in range(2)]
         + [("b", h, 0, q) for h in range(HEADS_B) for q in range(NT)]
         + [("a", h, 0, q) for h in range(HEADS_A) for q in range(NT)])
BIASED = [u for u, (kind, *_) in enumerate(UNITS) if kind != "b"]
TURNS = [u for u, (kind, _, c, _) in enumerate(UNITS) if kind != "c" or c == 1]
HEADS = [UNITS[TURNS[NT * g]][:2] for g in range(len(TURNS) // NT)]
PAIR_TILE = [6, 7, 2, 3, 4, 5, 0, 1]
SLOPES = [2.0 ** (-8.0 * (i + 1) / (HEADS_A + HEADS_C)) for i in range(HEADS_A + HEADS_C)]
SCALE = {"a": 64 ** -0.5, "b": (NOPE + ROPE) ** -0.5, "c": DIFF_QK ** -0.5}
LAM_INIT = [0.8 - 0.6 * math.exp(-0.3 * layer) for layer in range(DEPTH)]
DVE_STEPS = 126
MAGIC = 1.5 * 2.0 ** 23
TURN_HI = 6.28125
TURN_LO = 2 * math.pi - 6.28125
PI_DOWN = 3.1415925
OC_NORM_AT = 38
LOW_RANK_GAINS = 8 * NM
C_GAINS = LOW_RANK_GAINS + 5 * DEPTH
PI = math.pi
D_DECAY, D_ANGLE, D_LAM, D_TABLES = 2, 6, 8, 35


S5_TILES, STATES, S5_PAIRS = 4, 64, 16
LRU_TILES, CONV = 10, 4
PAD = CONV - 1
PLE_TILES = 2
U_AT, LRU_G_AT, S5_G_AT, LRU_X_AT, GATE_L_AT, LRU_OUT_AT = 0, 2, 7, 9, 14, 18
GATE_S_AT, GLU_AT, S5_OUT_AT, OUT_AT, PLE_AT, PLE_GATE_AT, SLOTS_2 = 23, 27, 29, 31, 35, 36, 40
D_SKIP, CONV_W, CONV_B, B_A, B_X, LAM, G_POST = 0, 4, 44, 54, 64, 74, 84
S5_FROM = 4
S5_STEPS = S5_PAIRS + 3
LRU_FROM = S5_FROM + S5_STEPS + 1
LRU_STEPS = LRU_TILES + 2
PLE_BANKS = [5, 6, 7, 0, 1, 2, 3, 4]
TURN = 6.283185


class Signal:

    def __init__(self, sem, per_layer=0, start=0):
        self.sem, self.per_layer, self.start = sem, per_layer, start

    def at(self, layer, k):
        k += self.start
        return layer * self.per_layer + k if self.per_layer else k


def build(nc, a):
    ctx = ExitStack()
    with ctx:
        def sb(name, shape, dt=F32, where=ctx):
            return where.enter_context(nc.sbuf_tensor(name, shape, dt))

        def signal(name, per_layer=0, start=0):
            return Signal(ctx.enter_context(nc.semaphore(name)), per_layer, start)

        x = sb("x", [P, NM, T])
        raw = [sb(f"raw{i}", [P, SLOT]) for i in range(2)]
        sq = sb("sq", [P, 2, T])
        tmp = sb("tmp", [P, 2, T])
        bias_ring = sb("bias_ring", [P, 4, T])
        mats = sb("mats", [P, 4, P])
        cols = sb("cols", [P, a["cols"].shape[1]])
        cols2 = sb("cols2", [P, a["cols2"].shape[1]])
        lru_s = sb("lru_s", [P, 4, LRU_TILES])
        gains = sb("gains", [P, a["gains"].shape[1]])
        lam_s = sb("lam_s", [P, 8])
        nlam = sb("nlam", [P, DEPTH])
        gain_c = sb("gain_c", [P, DEPTH])
        wide = sb("wide", [P, 2, T])
        dist = bias_ring
        mneg = sb("mneg", [P, 4])
        rsum = sb("rsum", [P, 4])
        rinv = sb("rinv", [P, 8])
        atmp, rstd = sq[:, 0, :], sq[:, 1, :]
        sil = tmp
        ident, ones, ones64, spread = (mats[:, i, :] for i in range(4))
        eps = cols[:, 0:1]

        with ExitStack() as own:
            w_hi = sb("w_hi", [P, 2, SLOT], F32R, own)
            w_lo = sb("w_lo", [P, 2, SLOT], F32R, own)
        own = ctx.enter_context(ExitStack())
        pt = sb("pt", [P, 2, NT, T], F32, own)
        probs = sb("probs", [P, 4, T], F32, own)
        negs = sb("negs", [P, 4, T], F32, own)
        with ExitStack() as own:
            h_hi = sb("h_hi", [P, NM, T], F32R, own)
            h_lo = sb("h_lo", [P, NM, T], F32R, own)
        own = ctx.enter_context(ExitStack())
        mix_hi = sb("mix_hi", [P, NM, T], F32R, own)
        mix_lo = sb("mix_lo", [P, NM, T], F32R, own)
        with ExitStack() as own:
            a_hi = sb("a_hi", [P, NF, T], F32R, own)
            a_lo = sb("a_lo", [P, NF, T], F32R, own)
        with ExitStack() as own:
            pos_i = sb("pos_i", [P, T], I32, own)
            pos_r = sb("pos_r", [P, T], F32, own)
            pcol_i = sb("pcol_i", [P, NT], I32, own)
            pcol = sb("pcol", [P, NT], F32, own)
            rot = sb("rot", [P, 4, T], F32, own)
            table2 = sb("table2", [P, 2, T], F32, own)
            lamv = sb("lamv", [P, DEPTH, 4, DIFF_QK], F32, own)
            used = 2 * T + 2 * NT + 6 * T + DEPTH * 4 * DIFF_QK
            sb("unused", [P, 2 * NF * T - used - (2 * T - P)], F32, own)
            reach = sb("reach", [P, 2 * T - P], F32, own)
        own = ctx.enter_context(ExitStack())
        qk = sb("qk", [P, 8, T], F32, own)
        cn_hi = sb("cn_hi", [P, 5, T], F32R, own)
        cn_lo = sb("cn_lo", [P, 5, T], F32R, own)
        v_ac = sb("v_ac", [P, NT, T], F32, own)
        v_b = sb("v_b", [P, NT, T], F32, own)
        cs = sb("cs", [P, 2, T], F32, own)
        q_b = sb("q_b", [P, HEADS_B, T], F32, own)
        k_b = sb("k_b", [P, HEADS_B, T], F32, own)
        c_raw, k_prod = q_b[:, 0:5, :], q_b[:, 5, :]
        c_sq, c_rstd = k_b[:, 0:5, :], k_b[:, 5:7, :]

        own.close()

        def region(size, *parts):
            got = []
            for part in parts:
                with ExitStack() as own:
                    got += [sb(name, shape, dt, own) for name, shape, dt in part]
                    used = sum(int(np.prod(shape[1:])) for _, shape, _ in part)
            keep = ctx.enter_context(ExitStack())
            sb("held_by_" + got[0].name, [P, size], F32, keep)
            assert used <= size
            return got

        s5p, s5w, tidx, s5b, s5c_in, s5c, gl = region(
            NM * T, [("s5p", [P, 3, S5_PAIRS], F32), ("s5w", [P, 24, S5_PAIRS], F32), ("tidx", [P, T], F32),
                     ("s5b", [P, S5_TILES, 2, P], F32), ("s5c_in", [P, 2, S5_PAIRS * 32], F32),
                     ("s5c", [P, 2, S5_PAIRS * 32], F32)],
            [("gl", [P, NM, T], F32)])
        u, p_hi, p_lo = region(S5_TILES * T, [("u", [P, S5_TILES, T], F32)],
                               [("p_hi", [P, PLE_TILES, T], F32R), ("p_lo", [P, PLE_TILES, T], F32R)])
        lrux, yl_hi, yl_lo, g_hi, g_lo = region(
            LRU_TILES * (T + 4), [("lrux", [P, LRU_TILES, T + 4], F32)],
            [("yl_hi", [P, 2, T], F32R), ("yl_lo", [P, 2, T], F32R)],
            [("g_hi", [P, S5_TILES, T], F32R), ("g_lo", [P, S5_TILES, T], F32R)])
        slg, ys_hi, ys_lo = region(LRU_TILES * T, [("slg", [P, LRU_TILES, T], F32)],
                                   [("ys_hi", [P, S5_TILES, T], F32R), ("ys_lo", [P, S5_TILES, T], F32R)])
        s5t, w_lru, lt, gs = region(
            10 * T, [("s5t", [P, 10, T], F32)],
            [("w_lru", [P, 2 * LRU_TILES, P], F32), ("lt", [P, 5, T], F32)], [("gs", [P, NM, T], F32)])
        s5h_re = [sq[:, n, :] for n in range(2)]
        cos_sin = [s5t[:, 8:10, :], wide]
        ssg = bias_ring
        gathering = wide[:, 0, :]
        turns = lrux[:, LRU_TILES - 1, 4:4 + T]
        lru_t = [[lt[:, n, :] for n in range(3)], [lt[:, 3, :], lt[:, 4, :], wide[:, 0, :]],
                 [tmp[:, 0, :], tmp[:, 1, :], sq[:, 0, :]]]
        lru_r = [lrux[:, q, 0:T] for q in range(LRU_TILES)]

        ps = ctx.enter_context(nc.psum_tensor("ps", [P, 8, T], F32))
        bias_d = nc.dram_tensor("bias_d", (HEADS_A + HEADS_C, NT, P, T), F32).ap()
        cs_d = nc.dram_tensor("cs_d", (P, 2, T), F32).ap()

        cols_in = signal("cols_in")
        mats_in = signal("mats_in")
        pos_in = signal("pos_in")
        reach_in = signal("reach_in")
        x_in = [signal(f"x_in{i}") for i in range(2)]
        raw_in = [signal(f"raw_in{i}") for i in range(2)]
        hi_split = signal("hi_split", LAYER_SLOTS)
        lo_split = signal("lo_split", LAYER_SLOTS)
        slot_used = signal("slot_used", LAYER_SLOTS, start=1)
        tile_done = signal("tile_done", EARLIER[LAYER_SLOTS])
        x_done = signal("x_done", 3 * NM)
        squared = signal("squared", SQ_LAYER)
        gathered = signal("gathered", 3 * (GATHERED - 1))
        summed = signal("summed", SUM_LAYER, start=NM)
        logged = signal("logged", 3)
        inverted = signal("inverted", 3)
        h_scaled = signal("h_scaled", 3 * NM)
        h_hi_done = signal("h_hi_done", 3 * NM)
        h_done = signal("h_done", 3 * NM)
        silued = signal("silued", 2 * NF)
        a_prod = signal("a_prod", 2 * NF)
        a_hi_done = signal("a_hi_done", 2 * NF)
        a_done = signal("a_done", 2 * NF, start=1)

        act_evac = signal("act_evac", 7 + 2 + 8)
        dve_evac = signal("dve_evac", 7 + 2 + HEADS_B + NT)
        c_squared = signal("c_squared", 5)
        c_summed = signal("c_summed", 2)
        c_logged = signal("c_logged", 2)
        c_inverted = signal("c_inverted", 2)
        c_done = signal("c_done", 5)
        k_turned = signal("k_turned", 1)
        k_spread = signal("k_spread", 2)
        cs_in = signal("cs_in", 16)
        bias_in = [signal(f"bias_in{i}", 16 * (len(BIASED) // 4)) for i in range(4)]
        score_done = signal("score_done", len(UNITS))
        max_done = signal("max_done", len(UNITS))
        exp_done = signal("exp_done", len(UNITS))
        p_done = signal("p_done", len(TURNS))
        turned = signal("turned", len(TURNS))
        pt_done = signal("pt_done", len(TURNS))
        pv_done = signal("pv_done", len(HEADS))
        pair_hi = signal("pair_hi", len(HEADS) // 2 - 2)
        pv_taken = signal("pv_taken", len(HEADS) // 2)
        oc_logged = signal("oc_logged", 2)
        oc_inverted = signal("oc_inverted", 2)
        oc_mixed = signal("oc_mixed", 2)
        pos_done = signal("pos_done")
        dist_done = signal("dist_done")
        bias_made = signal("bias_made")
        bias_out = [signal(f"bias_out{i}") for i in range(2)]
        cs_made = signal("cs_made")
        cs_out = signal("cs_out")
        dve_step = signal("dve_step", DVE_STEPS)
        act_step = signal("act_step")
        dve_pro = signal("dve_pro")
        pro_step = signal("pro_step")
        fin = signal("fin")
        out_sent = signal("out_sent")

        pool_met = signal("pool_met")
        dve_met = signal("dve_met")

        cols2_in = signal("cols2_in")
        s5_in = signal("s5_in")
        w_lru_in = signal("w_lru_in")
        p_in = signal("p_in")
        x_again = signal("x_again")
        tile2_done = signal("tile2_done")
        evac2 = signal("evac2")
        d_small = signal("d_small")
        a_small = signal("a_small")
        s5_ready = signal("s5_ready")
        turned_by = signal("turned_by")
        whole_turns = signal("whole_turns")
        table_d = signal("table_d")
        table_a = signal("table_a")
        bu_done = signal("bu_done")
        pre_done = signal("pre_done")
        pre_sum = signal("pre_sum")
        scan_done = signal("scan_done")
        post_d = signal("post_d")
        post_p = signal("post_p")
        h_re_done = signal("h_re_done")
        h_im_done = signal("h_im_done")
        s5_out = signal("s5_out")
        s5_y = signal("s5_y")
        pads_done = signal("pads_done")
        conv_step = signal("conv_step")
        conv_done = signal("conv_done")
        ri_done = signal("ri_done")
        lru_a = signal("lru_a")
        lru_square = signal("lru_square")
        lru_log = signal("lru_log")
        lru_rest = signal("lru_rest")
        lru_root = signal("lru_root")
        lru_rc = signal("lru_rc")
        lru_b = signal("lru_b")
        lru_scan = signal("lru_scan")
        lru_y = signal("lru_y")
        yl_hi_done = signal("yl_hi_done")
        yl_done = signal("yl_done")
        yl_used = signal("yl_used")
        z_taken = signal("z_taken")
        gs_done = signal("gs_done")
        gelued = signal("gelued")
        g_hi_done = signal("g_hi_done")
        g_done = signal("g_done")
        glu_sig = signal("glu_sig")
        glu_prod = signal("glu_prod")
        glu_step = signal("glu_step")
        ys_done = signal("ys_done")
        bs_taken = signal("bs_taken")
        gates_added = signal("gates_added")
        merged_hi = signal("merged_hi")
        merged = signal("merged")
        o_copied = signal("o_copied")
        o_step = signal("o_step")
        o_added = signal("o_added")
        xs_hi_done = signal("xs_hi_done")
        xs_done = signal("xs_done")
        p_split = signal("p_split")
        ple_evac = signal("ple_evac")
        gate_sig = signal("gate_sig")
        gate_step = signal("gate_step")

        block = ctx.enter_context(nc.Block())

        def first_products():
            step = lru = 0
            for s in range(LRU_OUT_AT):
                yield "slot", s
                for i in range(2):
                    n = 2 * s + i
                    yield "tile", n
                    if n >= S5_FROM and step < S5_STEPS:
                        yield "s5", step
                        step += 1
                    if n >= LRU_FROM:
                        yield "lru", lru
                        lru += 1
            while lru < LRU_STEPS:
                yield "lru", lru
                lru += 1

        def wait_tile2(eng, s, i, n=2, before=0):
            if i == n - 1:
                wait(eng, slot_used, DEPTH, s + 1)
            else:
                eng.wait_ge(tile2_done.sem, before + i + 1)

        per_slot = [1] * LRU_OUT_AT + [0] * 4 + [7] + [1] * 4 + [3] * 4 + [1] * 4 + [7] + [1] * 4
        before2 = [sum(per_slot[:s]) for s in range(SLOTS_2 + 1)]

        def wait(eng, sig, layer, k):
            eng.wait_ge(sig.sem, sig.at(layer, k))

        def wait_tile(eng, layer, s, i):
            if i == TILES[s] - 1:
                wait(eng, slot_used, layer, s + 1)
            else:
                wait(eng, tile_done, layer, EARLIER[s] + i + 1)

        @block.sync
        def _(sp):
            sp.dma_start(cols[:], a["cols"]).then_inc(cols_in.sem, 16)
            sp.dma_start(gains[:], a["gains"]).then_inc(cols_in.sem, 16)
            sp.dma_start(lamv[:], a["lamv"]).then_inc(cols_in.sem, 16)
            sp.dma_start(x[:, 4:8, :], a["x"][:, 4:8, :]).then_inc(x_in[0].sem, 16)
            sp.dma_start(mats[:], a["mats"]).then_inc(mats_in.sem, 16)
            sp.dma_start(raw[0][:], a["stream"][0]).then_inc(raw_in[0].sem, 16)
            sp.dma_start(x[:, 0:4, :], a["x"][:, 0:4, :]).then_inc(x_in[1].sem, 16)
            sp.dma_start(raw[1][:], a["stream"][1]).then_inc(raw_in[1].sem, 16)
            sp.dma_start(cols2[:], a["cols2"]).then_inc(cols2_in.sem, 16)
            with sp.Fori(1, a["stream"].shape[0] // 2) as j:
                for i in range(2):
                    sp.wait_ge(lo_split.sem, 2 * j - 1 + i)
                    sp.dma_start(raw[i][:], a["stream"][2 * j + i]).then_inc(raw_in[i].sem, 16)
            for m in range(NM):
                sp.wait_ge(fin.sem, m + 1)
                sp.dma_start(a["out"][:, m, :], x[:, m, :]).then_inc(out_sent.sem, 16)
            sp.wait_ge(out_sent.sem, 16 * NM)

        @block.gpsimd
        def _(pool):
            pool.dma_start(pos_i[:], a["pos"].partition_broadcast(P)).then_inc(pos_in.sem, 16)
            pool.dma_start(pcol_i[:], a["pos_col"]).then_inc(pos_in.sem, 16)
            pool.wait_ge(dist_done.sem, NT)
            pool.dma_start(reach[:], a["reach"]).then_inc(reach_in.sem, 16)
            n = made = 0
            for table in range(HEADS_A + HEADS_C):
                is_a = table < HEADS_A
                slope = SLOPES[2 * table] if is_a else SLOPES[2 * (table - HEADS_A) + 1]
                for q in range(NT):
                    if n == NT:
                        pool.wait_ge(cs_made.sem, 1)
                        pool.dma_start(cs_d, table2[:]).then_inc(cs_out.sem, 16)
                    if n >= 2:
                        pool.wait_ge(bias_out[n % 2].sem, 16 * (n // 2))
                    pool.tensor_scalar(wide[:, n % 2, :], dist[:, q, :], slope, 0.0, ALU.mult, ALU.add
                                       ).then_inc(bias_made.sem, 1)
                    made += 1
                    pool.wait_ge(bias_made.sem, made)
                    if is_a:
                        pool.wait_ge(reach_in.sem, 16)
                        lo = T - P - P * q
                        pool.tensor_tensor(wide[:, n % 2, :], wide[:, n % 2, :], reach[:, lo:lo + T], ALU.add
                                           ).then_inc(bias_made.sem, 1)
                        made += 1
                        pool.wait_ge(bias_made.sem, made)
                    pool.dma_start(bias_d[table, q], wide[:, n % 2, :]).then_inc(bias_out[n % 2].sem, 16)
                    n += 1
            for i in range(2):
                pool.wait_ge(bias_out[i].sem, 16 * (n // 2))
            pool.wait_ge(cs_out.sem, 16)

            def gather(layer, before, n):
                for idx in range(1, GATHERED):
                    wait(pool, squared, layer, before + idx + 1)
                    if idx >= 2:
                        wait(pool, gathered, layer, n * (GATHERED - 1) + idx - 1)
                    pool.tensor_tensor(gathering, sq[:, 0, :] if idx == 1 else gathering, sq[:, idx % 2, :], ALU.add
                                       ).then_inc(gathered.sem, 1)

            with pool.Fori(0, DEPTH) as layer:
                gather(layer, NM, 0)
                wait(pool, x_done, layer, NM)
                pool.sem_inc(pool_met.sem, 1)
                pool.dma_start(cs[:], cs_d).then_inc(cs_in.sem, 16)
                for n, u in enumerate(BIASED):
                    kind, head, _, q = UNITS[u]
                    if n >= 4:
                        wait(pool, max_done, layer, BIASED[n - 4] + 1)
                        pool.sem_inc(pool_met.sem, 1)
                    pool.dma_start(bias_ring[:, n % 4, :], bias_d[head + (HEADS_A if kind == "c" else 0), q]
                                   ).then_inc(bias_in[n % 4].sem, 16)
                wait(pool, max_done, layer, len(UNITS))
                gather(layer, 2 * NM + 2, 1)
                gather(layer, 3 * NM + 2, 2)

            wait(pool, x_done, DEPTH, 0)
            for dst, name in ((s5p, "s5p"), (tidx, "tidx"), (s5b, "s5b"), (s5c_in, "s5c")):
                pool.dma_start(dst[:], a[name]).then_inc(s5_in.sem, 16)

            for m in range(NM):
                wait(pool, h_done, DEPTH, m + 1)
                pool.tensor_tensor(x[:, m, :], h_hi[:, m, :].bitcast(F32), h_lo[:, m, :].bitcast(F32), ALU.add
                                   ).then_inc(x_again.sem, 1)

            def s5_step(p):
                if 0 <= p - 1 < S5_PAIRS:
                    before = p - 1
                    t = 4 * (before % 2)
                    cos, sin = (cos_sin[before % 2][:, n, :] for n in range(2))
                    pool.wait_ge(scan_done.sem, 2 * (before + 1))
                    pool.tensor_tensor(s5t[:, t, :], s5t[:, t + 1, :], sin, ALU.mult).then_inc(post_p.sem, 1)
                    pool.tensor_tensor(s5t[:, t + 2, :], s5t[:, t + 3, :], cos, ALU.mult).then_inc(post_p.sem, 1)
                    pool.wait_ge(post_p.sem, 2 * (before + 1))
                    pool.tensor_tensor(s5t[:, t, :], s5t[:, t, :], s5t[:, t + 2, :], ALU.add).then_inc(h_im_done.sem, 1)
                    pool.wait_ge(post_d.sem, 2 * (before + 1))
                    pool.tensor_tensor(s5h_re[before % 2], s5h_re[before % 2], tmp[:, 1, :], ALU.subtract
                                       ).then_inc(h_re_done.sem, 1)
                if p < S5_PAIRS:
                    t = 4 * (p % 2)
                    pool.wait_ge(pre_done.sem, 4 * (p + 1))
                    pool.tensor_tensor(s5t[:, t, :], s5t[:, t, :], s5t[:, t + 1, :], ALU.add).then_inc(pre_sum.sem, 1)
                    pool.tensor_tensor(s5t[:, t + 2, :], s5t[:, t + 2, :], s5t[:, t + 3, :], ALU.subtract
                                       ).then_inc(pre_sum.sem, 1)

            def lru_step(q):
                if 0 <= q - 1 < LRU_TILES:
                    c = lru_t[(q - 1) % 3][0]
                    pool.wait_ge(lru_root.sem, q)
                    pool.tensor_tensor(c, lru_r[q - 1], c, ALU.mult).then_inc(lru_rc.sem, 1)
                if 0 <= q - 2 < LRU_TILES:
                    pool.wait_ge(lru_scan.sem, q - 1)
                    pool.wait_ge(evac2.sem, 2 * LRU_G_AT + q - 1)
                    pool.tensor_tensor(slg[:, q - 2, :], lru_r[q - 2], slg[:, q - 2, :], ALU.mult).then_inc(lru_y.sem, 1)

            for kind, n in first_products():
                if kind == "s5":
                    s5_step(n)
                if kind == "s5" and n == S5_STEPS - 1:
                    pool.wait_ge(s5_out.sem, S5_PAIRS)
                    pool.dma_start(w_lru[:], a["w_lru"]).then_inc(w_lru_in.sem, 16)
                if kind == "lru":
                    lru_step(n)
            pool.wait_ge(lru_y.sem, LRU_TILES)
            pool.dma_start(wide[:], a["p"]).then_inc(p_in.sem, 16)
            pool.wait_ge(p_split.sem, 2 * PLE_TILES)
            gather(DEPTH, 2 * NM, 0)

        @block.tensor
        def _(pe):
            def three(out, w, xs, start, stop):
                (wh, wl), (xh, xl) = w, xs
                pe.matmul(out, wh, xh, start=start, stop=False)
                pe.matmul(out, wh, xl, start=False, stop=False)
                return pe.matmul(out, wl, xh, start=False, stop=stop)

            def weights(buf, b, n=1):
                return (w_hi[:, buf, b * P:(b + n) * P], w_lo[:, buf, b * P:(b + n) * P])

            def hid(m, lo=0, hi=T):
                return (h_hi[:, m, lo:hi], h_lo[:, m, lo:hi])

            def sum_gathered(layer, before, n):
                wait(pe, gathered, layer, (n + 1) * (GATHERED - 1))
                pe.matmul(ps[:, SS_BANK, :], ones, gathering, start=True, stop=False)
                for idx in range(GATHERED, NM):
                    wait(pe, squared, layer, before + idx + 1)
                    mm = pe.matmul(ps[:, SS_BANK, :], ones, sq[:, idx % 2, :], start=False, stop=idx == NM - 1)
                mm.then_inc(summed.sem, 1)

            def sum_squares(layer, before, idx, mat=None, bank=SS_BANK, alone=False):
                wait(pe, squared, layer, before + idx + 1)
                pe.matmul(ps[:, bank, :], ones if mat is None else mat, sq[:, idx % 2, :],
                          start=alone or idx == 0, stop=alone or idx == NM - 1).then_inc(summed.sem, 1)

            def up_slots(layer, f, at):
                with pe.Fori(0, UP_SLOTS // 2) as j:
                    for i in range(2):
                        c, buf = 2 * j + i, (at + i) % 2
                        pe.wait_ge(lo_split.sem, lo_split.at(layer, at + 1) + c)
                        pe.wait_ge(a_done.sem, a_done.at(layer, f * NF) + c)
                        for k in range(NM):
                            wait(pe, h_done, layer, 2 * f * NM + k + 1)
                            for half in range(2):
                                last = three(ps[:, 2 * i + half, :], weights(buf, 2 * k + half), hid(k),
                                             k == 0, k == NM - 1)
                        last.then_inc(slot_used.sem, 1)

            def down_slot(layer, f, at, j, i, first=False, final=False):
                buf = (at + i) % 2
                pe.wait_ge(lo_split.sem, lo_split.at(layer, at + 1) + j)
                pe.wait_ge(a_done.sem, a_done.at(layer, f * NF + 3) + 2 * j)
                for idx, m in enumerate(ORD):
                    if first and m == 0:
                        wait(pe, a_done, layer, (f + 1) * NF + 1)
                    for n in range(2):
                        mm = three(ps[:, m, :], weights(buf, 2 * idx + n),
                                   (a_hi[:, 2 * j + n, :], a_lo[:, 2 * j + n, :]),
                                   first and n == 0, final and n == 1)
                    if final and idx < NM - 1:
                        mm.then_inc(tile_done.sem, 1)
                    if idx == NM - 1:
                        mm.then_inc(slot_used.sem, 1)
                if final:
                    sum_gathered(layer, NM if f == 0 else 3 * NM + 2, 2 * f)

            def ffn(layer, f, at):
                up_slots(layer, f, at)
                at += UP_SLOTS
                down_slot(layer, f, at, 0, 0, first=True)
                with pe.Fori(0, DOWN_SLOTS // 2 - 1) as j:
                    for i in range(2):
                        down_slot(layer, f, at, 2 * j + 1 + i, 1 + i)
                down_slot(layer, f, at, DOWN_SLOTS - 2, 1)
                down_slot(layer, f, at, DOWN_SLOTS - 1, 0, final=True)

            def first_pair(layer, buf, early):
                for k in range(NM):
                    wait(pe, h_done, layer, NM + k + 1)
                    for i in range(2):
                        mm = three(ps[:, i, :], weights(buf, i * NM + k), hid(k), k == 0, k == NM - 1)
                        if k == NM - 1:
                            mm.then_inc((early, slot_used)[i].sem, 1)

            def in_products(layer):
                wait(pe, lo_split, layer, MIX_AT + 1)
                first_pair(layer, MIX_AT % 2, tile_done)
                for s in range(1, 7):
                    wait(pe, lo_split, layer, MIX_AT + s + 1)
                    for i in range(2):
                        t = 2 * s + i
                        if t >= 4:
                            wait(pe, (dve_evac, act_evac)[i], layer, s - 1)
                        for k in range(NM):
                            mm = three(ps[:, t % 4, :], weights((MIX_AT + s) % 2, i * NM + k), hid(k),
                                       k == 0, k == NM - 1)
                        mm.then_inc((tile_done, slot_used)[i].sem, 1)
                    if s == 1:
                        wait(pe, dve_evac, layer, 1)
                        pe.matmul(ps[:, 7, :], spread[0:64, :], k_prod[0:64, :], start=True, stop=True
                                  ).then_inc(k_turned.sem, 1)
                    if s == 4:
                        for i in range(5):
                            wait(pe, c_squared, layer, i + 1)
                            mm = pe.matmul(ps[:, 5 if i < 3 else 6, :], ones, c_sq[:, i, :],
                                           start=i in (0, 3), stop=i in (2, 4))
                            if i in (2, 4):
                                mm.then_inc(c_summed.sem, 1)
                wait(pe, dve_evac, layer, 7)
                wait(pe, act_evac, layer, 7)
                for s in (7, 8):
                    wait(pe, lo_split, layer, MIX_AT + s + 1)
                    for t in range(NT):
                        for k in range(4):
                            kk = 4 * (s - 7) + k
                            mm = three(ps[:, t, :], hid(kk, t * P, (t + 1) * P),
                                       weights((MIX_AT + s) % 2, 4 * k, 4), kk == 0, kk == NM - 1)
                        if s == 8 and t < NT - 1:
                            mm.then_inc(tile_done.sem, 1)
                    mm.then_inc(slot_used.sem, 1)
                for s in (9, 10):
                    wait(pe, lo_split, layer, MIX_AT + s + 1)
                    wait(pe, c_done, layer, 5)
                    for i in range(4):
                        if s == 9:
                            wait(pe, (dve_evac, act_evac)[i % 2], layer, 8 + i // 2)
                        else:
                            wait(pe, dve_evac, layer, 10 + i)
                        for k in range(3):
                            mm = three(ps[:, i, :], weights((MIX_AT + s) % 2, 3 * i + k),
                                       (cn_hi[:, k, :], cn_lo[:, k, :]), k == 0, k == 2)
                        mm.then_inc((tile_done if i < 3 else slot_used).sem, 1)
                wait(pe, lo_split, layer, MIX_AT + 12)
                for i in range(4):
                    wait(pe, dve_evac, layer, 14 + i)
                    for k in range(2):
                        mm = three(ps[:, i, :], weights((MIX_AT + 11) % 2, 2 * i + k),
                                   (cn_hi[:, 3 + k, :], cn_lo[:, 3 + k, :]), k == 0, k == 1)
                    mm.then_inc(tile_done.sem, 1)
                wait(pe, c_logged, layer, 2)
                wait(pe, k_spread, layer, 2)
                for t in range(NT):
                    for k in range(2):
                        mm = three(ps[:, 4 + t, :], (cn_hi[:, 3 + k, t * P:(t + 1) * P], cn_lo[:, 3 + k, t * P:(t + 1) * P]),
                                   weights((MIX_AT + 11) % 2, 8 + 4 * k, 4), k == 0, k == 1)
                    mm.then_inc((tile_done if t < 3 else slot_used).sem, 1)

            def score(layer, u):
                kind, head, c, q = UNITS[u]
                if u == 0:
                    wait(pe, act_evac, layer, 17)
                    wait(pe, dve_evac, layer, 17)
                if u >= 4:
                    wait(pe, exp_done, layer, u - 3)
                if kind == "b":
                    query, key, lo, n = q_b[:, head, :], k_b[:, head, :], 0, P
                elif kind == "a":
                    query, key, lo, n = qk[:, 2 * (head // 2), :], qk[:, 2 * (head // 2) + 1, :], 64 * (head % 2), 64
                else:
                    m = 2 * head + c
                    query, key, lo, n = qk[:, 4 + 2 * (m // 4), :], qk[:, 5 + 2 * (m // 4), :], 32 * (m % 4), 32
                pe.matmul(ps[:, u % 4, :], query[lo:lo + n, q * P:(q + 1) * P], key[lo:lo + n, :],
                          start=True, stop=True).then_inc(score_done.sem, 1)

            def turn(layer, v):
                wait(pe, p_done, layer, v + 1)
                if v >= 2:
                    wait(pe, pt_done, layer, v - 1)
                for k in range(NT):
                    mm = pe.transpose(ps[:, 4 + v % 2, k * P:(k + 1) * P], probs[:, TURNS[v] % 4, k * P:(k + 1) * P],
                                      ident)
                mm.then_inc(turned.sem, 1)

            def attend(layer, g):
                kind, head = HEADS[g]
                if g in (4, 6):
                    wait(pe, oc_logged, layer, g // 2 - 1)
                if g >= 4:
                    wait(pe, pv_taken, layer, g // 2 - 1)
                wait(pe, pt_done, layer, NT * (g + 1))
                if g == 0:
                    wait(pe, dve_evac, layer, 21)
                v, col = (v_b, 64 * head) if kind == "b" else (v_ac, 64 * head + (256 if kind == "c" else 0))
                half = 64 * (g % 2)
                for k in range(NT):
                    mm = pe.matmul(ps[half:half + 64, 6 + (g // 2) % 2, :], v[:, k, col:col + 64], pt[:, 1 - g % 2, k, :],
                                   start=k == 0, stop=k == NT - 1)
                mm.then_inc(pv_done.sem, 1)

            def attention(layer):
                for u in range(len(UNITS) + 5):
                    if u < len(UNITS):
                        score(layer, u)
                    if u - 3 in TURNS:
                        turn(layer, TURNS.index(u - 3))
                    if u - 5 in TURNS and TURNS.index(u - 5) % NT == NT - 1:
                        attend(layer, TURNS.index(u - 5) // NT)
                    if u == OC_NORM_AT + 1:
                        for i in range(2):
                            sum_squares(layer, 2 * NM, i, mat=ones64, bank=6 + i, alone=True)

            def out_products(layer):
                wait(pe, pv_taken, layer, 7)
                wait(pe, oc_mixed, layer, 2)
                for s in range(12, 16):
                    wait(pe, lo_split, layer, MIX_AT + s + 1)
                    for i in range(2):
                        idx = 2 * (s - 12) + i
                        for n in range(NM):
                            k = (n + PAIR_TILE[-1] + 1) % NM
                            if idx == 0 and n == NM - 1:
                                wait(pe, pv_taken, layer, 8)
                            mm = three(ps[:, ORD[idx], :], weights((MIX_AT + s) % 2, i * NM + k),
                                       (mix_hi[:, k, :], mix_lo[:, k, :]), n == 0, n == NM - 1)
                        mm.then_inc((tile_done, slot_used)[i].sem, 1)
                sum_gathered(layer, 2 * NM + 2, 1)

            pe.sem_inc(slot_used.sem, 1)
            pe.wait_ge(mats_in.sem, 16)
            for idx in range(NM):
                sum_squares(0, 0, idx)
            with pe.Fori(0, DEPTH) as layer:
                ffn(layer, 0, 0)
                in_products(layer)
                attention(layer)
                out_products(layer)
                ffn(layer, 1, FFN2_AT)

            for idx in range(NM):
                sum_squares(DEPTH, NM, idx)

            def tile2(s, i, bank, ins, n_k, blocks_at, signal_to, ready=None):
                for k in range(n_k):
                    if ready is not None:
                        pe.wait_ge(ready.sem, k + 1)
                    mm = three(ps[:, bank, :], weights(s % 2, blocks_at + k), ins(k), k == 0, k == n_k - 1)
                mm.then_inc(signal_to.sem, 1)

            def slot2(s):
                wait(pe, lo_split, DEPTH, s + 1)

            def s5_step(p):
                if p < S5_PAIRS:
                    lo, tile = 32 * (p % 4), p // 4
                    if p % 4 == 0:
                        pe.wait_ge(evac2.sem, tile + 1)
                    if p == 0:
                        wait(pe, logged, DEPTH, 2)
                        pe.wait_ge(s5_in.sem, 64)
                    if p >= 1:
                        pe.wait_ge(pre_done.sem, 4 * p)
                    for ri in range(2):
                        mm = pe.matmul(ps[:, 4 + ri, :], s5b[lo:lo + 32, tile, ri, :], u[lo:lo + 32, tile, :],
                                       start=True, stop=True)
                    mm.then_inc(bu_done.sem, 1)
                p -= 2
                if 0 <= p < S5_PAIRS:
                    lo, tile = 32 * (p % 4), p // 4
                    if p % 4 == 0 and tile >= 2:
                        pe.wait_ge(s5_y.sem, tile - 1)
                    if p == 0:
                        pe.wait_ge(s5_ready.sem, 1)
                    t = 4 * (p % 2)
                    pe.wait_ge(h_re_done.sem, p + 1)
                    pe.matmul(ps[lo:lo + 32, 6 + tile % 2, :], s5c[:, 0, 32 * p:32 * p + 32], s5h_re[p % 2],
                              start=True, stop=False)
                    pe.wait_ge(h_im_done.sem, p + 1)
                    pe.matmul(ps[lo:lo + 32, 6 + tile % 2, :], s5c[:, 1, 32 * p:32 * p + 32], s5t[:, t, :],
                              start=False, stop=True).then_inc(s5_out.sem, 1)

            def lru_step(q):
                if q >= LRU_TILES:
                    return
                bank = 4 + 2 * (q % 2)
                if q == 0:
                    pe.wait_ge(w_lru_in.sem, 16)
                    pe.wait_ge(s5_y.sem, S5_TILES)
                if q >= 2:
                    pe.wait_ge(lru_a.sem, 4 * (q - 2) + 2)
                    pe.wait_ge(lru_rest.sem, q - 1)
                pe.wait_ge(conv_done.sem, q + 1)
                for n in range(2):
                    mm = pe.matmul(ps[:, bank + n, :], w_lru[:, 2 * q + n, :], lru_t[q % 3][0], start=True, stop=True)
                mm.then_inc(ri_done.sem, 1)

            for kind, n in first_products():
                if kind == "slot":
                    slot2(n)
                elif kind == "s5":
                    s5_step(n)
                elif kind == "lru":
                    lru_step(n)
                else:
                    if n >= 4:
                        pe.wait_ge(evac2.sem, n - 3)
                    if n == 0:
                        first_pair(DEPTH, 0, tile2_done)
                    elif n >= 2:
                        tile2(n // 2, n % 2, n % 4, hid, NM, NM * (n % 2), (tile2_done, slot_used)[n % 2])
            for k in range(LRU_TILES):
                s = LRU_OUT_AT + k // 2
                slot2(s)
                pe.wait_ge(yl_done.sem, k + 1)
                for m in range(NM):
                    if k == 0 and m < 4:
                        pe.wait_ge(evac2.sem, 2 * LRU_OUT_AT - 3 + m)
                    elif k == 0 and m % 2 == 0:
                        head = LRU_TILES - 2 + m % 4 // 2
                        pe.wait_ge(lru_a.sem, 4 * head + 2)
                        pe.wait_ge(lru_rest.sem, head + 1)
                    mm = three(ps[:, m, :], weights(s % 2, NM * (k % 2) + m), (yl_hi[:, k % 2, :], yl_lo[:, k % 2, :]),
                               k == 0, k == LRU_TILES - 1)
                    if k == LRU_TILES - 1 and m < NM - 1:
                        mm.then_inc(tile2_done.sem, 1)
                mm.then_inc((yl_used, slot_used)[k % 2].sem, 1)
            for m in range(NM):
                s = GATE_S_AT + m // 2
                if m % 2 == 0:
                    slot2(s)
                if m < 4:
                    pe.wait_ge(z_taken.sem, m + 1)
                else:
                    pe.wait_ge(gs_done.sem, m - 3)
                tile2(s, m % 2, m % 4, hid, NM, NM * (m % 2), (tile2_done, slot_used)[m % 2])
            pe.wait_ge(z_taken.sem, NM)
            for n in range(2 * S5_TILES):
                s = GLU_AT + n // 4
                if n % 4 == 0:
                    slot2(s)
                    pe.wait_ge(g_done.sem, S5_TILES)
                if n >= 4 and n % 2 == 0:
                    pe.wait_ge(glu_prod.sem, n // 2 - 1)
                tile2(s, n % 4, 4 + n % 4, lambda k: (g_hi[:, k, :], g_lo[:, k, :]), S5_TILES, 4 * (n % 4),
                      slot_used if n % 4 == 3 else tile2_done)
            for m in range(NM):
                s = S5_OUT_AT + m // 4
                if m % 4 == 0:
                    slot2(s)
                if m == 0:
                    pe.wait_ge(gs_done.sem, NM)
                if m >= 4:
                    pe.wait_ge(bs_taken.sem, m - 3)
                tile2(s, m % 4, m % 4, lambda k: (ys_hi[:, k, :], ys_lo[:, k, :]), S5_TILES, 4 * (m % 4),
                      slot_used if m % 4 == 3 else tile2_done, ready=ys_done if m == 0 else None)
            for idx, m in enumerate(ORD):
                s = OUT_AT + idx // 2
                if idx % 2 == 0:
                    slot2(s)
                tile2(s, idx % 2, m, lambda k: (mix_hi[:, k, :], mix_lo[:, k, :]), NM, NM * (idx % 2),
                      (tile2_done, slot_used)[idx % 2], ready=merged if idx == 0 else None)
            sum_gathered(DEPTH, 2 * NM, 0)
            slot2(PLE_AT)
            pe.wait_ge(p_split.sem, 2 * PLE_TILES)
            for m in range(NM):
                mm_bank = PLE_BANKS[m]
                if m == NM - 1:
                    wait(pe, logged, DEPTH, 3)
                for k in range(PLE_TILES):
                    mm = three(ps[:, mm_bank, :], weights(PLE_AT % 2, 2 * m + k), (p_hi[:, k, :], p_lo[:, k, :]),
                               k == 0, k == 1)
                mm.then_inc((tile2_done if m < NM - 1 else slot_used).sem, 1)
            for m in range(NM):
                s = PLE_GATE_AT + m // 2
                if m % 2 == 0:
                    slot2(s)
                pe.wait_ge(ple_evac.sem, m + 1)
                for k in range(NM):
                    if m == 0:
                        pe.wait_ge(xs_done.sem, k + 1)
                    mm = three(ps[:, PLE_BANKS[m], :], weights(s % 2, NM * (m % 2) + k), hid(k), k == 0, k == NM - 1)
                mm.then_inc((tile2_done, slot_used)[m % 2].sem, 1)

        @block.scalar
        def _(act):
            def split(layer, s, more=0):
                buf = s % 2
                act.wait_ge(raw_in[buf].sem, (layer * (LAYER_SLOTS // 2) + s // 2 + 1) * 16 + more * 8)
                act.wait_ge(slot_used.sem, slot_used.at(layer, s - 1) + more)
                act.activation(w_hi[:, buf, :], raw[buf][:], ACT.Copy).then_inc(hi_split.sem, 1)

            def square(layer, before, idx, src, scale=1.0, sums=None, gather=None):
                if idx >= 2:
                    if gather is None:
                        wait(act, summed, layer, sums + idx - 1)
                    else:
                        wait(act, gathered, layer, gather * (GATHERED - 1) + max(idx - 2, 1))
                act.activation(sq[:, idx % 2, :], src, ACT.Square, scale=scale).then_inc(squared.sem, 1)

            def inverse_root(layer, sums, n):
                wait(act, summed, layer, sums)
                act.activation(rstd, ps[:, SS_BANK, :], ACT.Ln, bias=eps, scale=1.0 / D).then_inc(logged.sem, 1)
                wait(act, logged, layer, n + 1)
                act.activation(rstd, rstd, ACT.Exp, scale=-0.5).then_inc(inverted.sem, 1)

            def h_parts(layer, stage):
                for m in range(NM):
                    wait(act, h_scaled, layer, stage * NM + m + 1)
                    act.activation(h_hi[:, m, :], tmp[:, m % 2, :], ACT.Copy).then_inc(h_hi_done.sem, 1)

            def norm(layer, before, stage):
                for idx, m in enumerate(ORD):
                    wait(act, x_done, layer, (stage - 1) * NM + idx + 1)
                    square(layer, before, idx, x[:, m, :], gather=stage - 1)
                inverse_root(layer, 1 if stage == 1 else SUM_LAYER, stage)
                h_parts(layer, stage)

            def ffn(layer, f, at):
                with act.Fori(0, UP_SLOTS // 2) as j:
                    for i in range(2):
                        c = 2 * j + i
                        split(layer, at + i + 1, 2 * j)
                        act.wait_ge(slot_used.sem, slot_used.at(layer, at + 1) + c)
                        act.wait_ge(a_done.sem, a_done.at(layer, f * NF) + c)
                        act.activation(sil[:, i, :], ps[:, 2 * i, :], ACT.Silu).then_inc(silued.sem, 1)
                at += UP_SLOTS
                with act.Fori(0, DOWN_SLOTS // 2) as j:
                    for i in range(2):
                        split(layer, at + i + 1, 2 * j)
                split(layer, at + DOWN_SLOTS)
                norm(layer, NM if f == 0 else 3 * NM + 2, 2 * f + 1)

            def in_products(layer):
                for s in range(7):
                    split(layer, MIX_AT + s + 1)
                    t = 2 * s + 1
                    wait_tile(act, layer, MIX_AT + s, 1)
                    dst = c_raw[:, t - 1, :] if t < 6 else qk[:, t - 6, :]
                    act.activation(dst, ps[:, t % 4, :], ACT.Copy).then_inc(act_evac.sem, 1)
                    if s == 3:
                        wait(act, dve_evac, layer, 3)
                        wait(act, act_evac, layer, 3)
                        for i in range(5):
                            act.activation(c_sq[:, i, :], c_raw[:, i, :], ACT.Square).then_inc(c_squared.sem, 1)
                    if s == 5:
                        for i, width in enumerate((Q_LORA, KV_LORA)):
                            wait(act, c_summed, layer, i + 1)
                            act.activation(c_rstd[:, i, :], ps[:, 5 + i, :], ACT.Ln, bias=eps, scale=1.0 / width
                                           ).then_inc(c_logged.sem, 1)
                        wait(act, c_logged, layer, 2)
                        for i in range(2):
                            act.activation(c_rstd[:, i, :], c_rstd[:, i, :], ACT.Exp, scale=-0.5
                                           ).then_inc(c_inverted.sem, 1)
                split(layer, MIX_AT + 8)
                split(layer, MIX_AT + 9)
                for t in (1, 3):
                    wait_tile(act, layer, MIX_AT + 8, t)
                    act.activation(v_ac[:, t, :], ps[:, t, :], ACT.Copy).then_inc(act_evac.sem, 1)
                split(layer, MIX_AT + 10)
                wait(act, c_done, layer, 5)
                wait(act, k_turned, layer, 1)
                for half in range(2):
                    lo = 64 * (1 - half)
                    dst = k_b[lo:lo + 64, :, :].rearrange("p (h two) t -> p h two t", two=2)[:, :, half, :]
                    act.activation(dst, ps[lo:lo + 64, 7, :].unsqueeze(1).to_broadcast([64, HEADS_B // 2, T]), ACT.Copy
                                   ).then_inc(k_spread.sem, 1)
                split(layer, MIX_AT + 11)
                for i in range(4):
                    wait_tile(act, layer, MIX_AT + 11, i)
                    for half in range(2):
                        act.activation(k_b[64 * half:64 * half + 64, 2 * i + half, :],
                                       ps[64 * half:64 * half + 64, i, :], ACT.Copy).then_inc(act_evac.sem, 1)

            def exps(layer, u):
                kind = UNITS[u][0]
                wait(act, max_done, layer, u + 1)
                if u >= 4:
                    if u - 4 in TURNS:
                        wait(act, turned, layer, TURNS.index(u - 4) + 1)
                    else:
                        wait(act, p_done, layer, TURNS.index(u - 3) + 1)
                src = ps[:, u % 4, :] if kind == "b" else negs[:, u % 4, :]
                act.activation(probs[:, u % 4, :], src, ACT.Exp, bias=mneg[:, u % 4:u % 4 + 1], scale=-1.0,
                               accum_out=rsum[:, u % 4:u % 4 + 1]).then_inc(exp_done.sem, 1)

            def turned_out(layer, v):
                wait(act, turned, layer, v + 1)
                if v >= 2 * NT:
                    wait(act, pv_done, layer, v // NT - 1)
                q = v % NT
                act.activation(pt[:, 1 - (v // NT) % 2, :, q * P:(q + 1) * P],
                               ps[:, 4 + v % 2, :].rearrange("p (k n) -> p k n", k=NT), ACT.Copy
                               ).then_inc(pt_done.sem, 1)

            def attention(layer):
                for u in range(len(UNITS) + 7):
                    if u - 4 in TURNS:
                        turned_out(layer, TURNS.index(u - 4))
                    v = TURNS.index(u - 6) if u - 6 in TURNS else 0
                    if v % (2 * NT) == 2 * NT - 1 and v // (2 * NT) >= 2:
                        pair = v // (2 * NT)
                        wait(act, pv_done, layer, 2 * pair + 2)
                        act.activation(mix_hi[:, PAIR_TILE[pair], :], ps[:, 6 + pair % 2, :], ACT.Copy
                                       ).then_inc(pair_hi.sem, 1)
                    if u == len(UNITS) + 1:
                        wait(act, pv_done, layer, len(HEADS) - 1)
                        wait(act, exp_done, layer, len(UNITS))
                        split(layer, MIX_AT + 12)
                    if u < len(UNITS):
                        exps(layer, u)
                    if u == OC_NORM_AT:
                        for i in range(2):
                            wait(act, pv_taken, layer, i + 1)
                            square(layer, 2 * NM, i, tmp[:, i, :])
                    if u == OC_NORM_AT + 1:
                        for i in range(2):
                            wait(act, summed, layer, 2 + i)
                            act.activation(sq[:, i, :], ps[:, 6 + i, :], ACT.Ln, bias=eps, scale=1.0 / V_DIM
                                           ).then_inc(oc_logged.sem, 1)
                        wait(act, oc_logged, layer, 2)
                        for i in range(2):
                            act.activation(sq[:, i, :], sq[:, i, :], ACT.Exp, scale=-0.5).then_inc(oc_inverted.sem, 1)

            def out_products(layer):
                wait(act, pv_done, layer, len(HEADS))
                for s in range(12, 16):
                    split(layer, MIX_AT + s + 1)
                    for i in range(2):
                        idx = 2 * (s - 12) + i
                        wait(act, x_done, layer, NM + idx + 1)
                        square(layer, 2 * NM + 2, idx, x[:, ORD[idx], :], gather=1)
                inverse_root(layer, SUM_LAYER - 1, 2)
                h_parts(layer, 2)

            act.wait_ge(dve_pro.sem, 1)
            act.activation(lam_s[:, 4:6], lam_s[:, 0:2], ACT.Exp).then_inc(act_step.sem, 1)
            act.activation(lam_s[:, 6:8], lam_s[:, 2:4], ACT.Exp).then_inc(act_step.sem, 1)
            act.wait_ge(pos_done.sem, 1)
            for q in range(NT):
                act.activation(dist[:, q, :], pos_r[:], ACT.Abs, bias=pcol[:, q:q + 1], scale=-1.0
                               ).then_inc(dist_done.sem, 1)
            act.wait_ge(dve_pro.sem, 2)
            act.activation(rot[:, 0, :], rot[:, 2, :], ACT.Sin).then_inc(act_step.sem, 1)
            act.activation(rot[:, 3, :], rot[:, 2, :], ACT.Abs).then_inc(act_step.sem, 1)
            act.wait_ge(act_step.sem, 4)
            act.activation(rot[:, 1, :], rot[:, 3, :], ACT.Sin, bias=cols[:, 1:2], scale=-1.0).then_inc(act_step.sem, 1)
            for idx, m in enumerate(ORD):
                if idx == NM // 2:
                    act.wait_ge(raw_in[0].sem, 16)
                    act.activation(w_hi[:, 0, :], raw[0][:], ACT.Copy).then_inc(hi_split.sem, 1)
                act.wait_ge(x_in[idx // (NM // 2)].sem, 16)
                square(0, 0, idx, x[:, m, :], sums=-NM)
            act.wait_ge(cols_in.sem, 48)
            inverse_root(0, 0, 0)
            h_parts(0, 0)
            with act.Fori(0, DEPTH) as layer:
                ffn(layer, 0, 0)
                in_products(layer)
                attention(layer)
                out_products(layer)
                ffn(layer, 1, FFN2_AT)

            def split2(s):
                if s < SLOTS_2:
                    split(DEPTH, s)

            small = [0]

            def small_step(ins):
                small[0] += 1
                ins.then_inc(a_small.sem, 1)
                act.wait_ge(a_small.sem, small[0])

            for m in range(NM):
                act.wait_ge(x_again.sem, m + 1)
                square(DEPTH, NM, m, x[:, m, :], sums=0)
            inverse_root(DEPTH, NM, 1)
            h_parts(DEPTH, 1)
            split2(1)
            act.wait_ge(s5_in.sem, 64)
            small_step(act.activation(s5w[:, 0, :], s5p[:, 2, :], ACT.Exp))
            act.wait_ge(d_small.sem, D_DECAY)
            small_step(act.activation(s5w[:, 3, :], s5w[:, 2, :], ACT.Exp))
            act.wait_ge(d_small.sem, D_ANGLE)
            small_step(act.activation(s5w[:, 6, :], s5w[:, 5, :], ACT.Sin, scale=TURN))
            small_step(act.activation(s5w[:, 7, :], s5w[:, 5, :], ACT.Abs))
            small_step(act.activation(s5w[:, 7, :], s5w[:, 7, :], ACT.Sin, scale=-TURN, bias=cols[:, 1:2]))
            act.wait_ge(d_small.sem, D_LAM)
            small_step(act.activation(lru_s[:, 1, :], lru_s[:, 0, :], ACT.Exp, scale=-1.0))
            act.wait_ge(d_small.sem, D_LAM + 1)
            small_step(act.activation(lru_s[:, 1, :], lru_s[:, 1, :], ACT.Ln))

            def evac(n):
                src = ps[:, n % 4, :]
                wait_tile2(act, n // 2, n % 2, before=before2[n // 2])
                s = n // 2
                scale = 1.0
                if s < LRU_G_AT:
                    dst, func = u[:, n, :], ACT.Copy
                elif s < S5_G_AT:
                    dst, func = slg[:, n - 2 * LRU_G_AT, :], ACT.Silu
                elif s < LRU_X_AT:
                    dst, func = ssg[:, n - 2 * S5_G_AT, :], ACT.Silu
                elif s < GATE_L_AT:
                    dst, func = lrux[:, n - 2 * LRU_X_AT, PAD:PAD + T], ACT.Copy
                else:
                    dst, func, scale = gl[:, n - 2 * GATE_L_AT, :], ACT.Tanh, 0.5
                if n == 2 * GATE_L_AT:
                    act.wait_ge(s5_out.sem, S5_PAIRS)
                    act.wait_ge(scan_done.sem, 2 * S5_PAIRS)
                act.activation(dst, src, func, scale=scale).then_inc(evac2.sem, 1)

            def whole(p):
                if p < S5_PAIRS:
                    act.wait_ge(turned_by.sem, p + 1)
                    act.activation(turns, turns, ACT.Identity, bias=cols[:, 14:15]).then_inc(whole_turns.sem, 1)

            def tables(p):
                if p >= S5_PAIRS:
                    return
                cos, sin = (cos_sin[p % 2][:, n, :] for n in range(2))
                act.wait_ge(table_d.sem, p + 1)
                if p >= 2:
                    act.wait_ge(post_d.sem, 2 * (p - 1))
                    act.wait_ge(post_p.sem, 2 * (p - 1))
                act.activation(sin, tmp[:, 0, :], ACT.Sin, scale=TURN).then_inc(table_a.sem, 1)
                act.activation(cos, tmp[:, 0, :], ACT.Abs).then_inc(table_a.sem, 1)
                act.wait_ge(table_a.sem, 3 * p + 2)
                act.activation(cos, cos, ACT.Sin, scale=-TURN, bias=cols[:, 1:2]).then_inc(table_a.sem, 1)
                whole(p + 1)

            def lru_step(q):
                if 0 <= q - 1 < LRU_TILES:
                    act.wait_ge(lru_rest.sem, q)
                    act.activation(lru_r[q - 1], lru_r[q - 1], ACT.Ln, scale=0.25, bias=cols[:, 13:14]
                                   ).then_inc(lru_log.sem, 1)
                    act.wait_ge(lru_log.sem, q)
                    act.activation(lru_r[q - 1], lru_r[q - 1], ACT.Exp, scale=0.5).then_inc(lru_root.sem, 1)
                if q < LRU_TILES:
                    r = lru_r[q]
                    _, i_, a_ = lru_t[q % 3]
                    bank = 4 + 2 * (q % 2)
                    if q == 0:
                        act.wait_ge(d_small.sem, D_TABLES)
                    act.wait_ge(ri_done.sem, q + 1)
                    if q >= 3:
                        act.wait_ge(lru_scan.sem, q - 2)
                    act.activation(r, ps[:, bank, :], ACT.Tanh, bias=cols2[:, B_A + q:B_A + q + 1], scale=0.5
                                   ).then_inc(lru_a.sem, 1)
                    act.activation(i_, ps[:, bank + 1, :], ACT.Tanh, bias=cols2[:, B_X + q:B_X + q + 1], scale=0.5
                                   ).then_inc(lru_a.sem, 1)
                    act.wait_ge(lru_a.sem, 4 * q + 1)
                    half, minus = lru_s[:, 2, q:q + 1], lru_s[:, 3, q:q + 1]
                    act.activation(a_, r, ACT.Exp, scale=minus, bias=minus).then_inc(lru_a.sem, 1)
                    act.wait_ge(lru_a.sem, 4 * q + 3)
                    act.activation(r, r, ACT.Tanh, scale=half, bias=half).then_inc(lru_a.sem, 1)

            for n in range(2):
                evac(n)
            split2(2)
            for kind, n in first_products():
                if kind == "slot":
                    if n >= 2:
                        split2(n + 1)
                    if n == S5_FROM // 2 - 1:
                        whole(0)
                        tables(0)
                elif kind == "s5":
                    tables(n + 1)
                elif kind == "lru":
                    lru_step(n)
                elif n >= 2:
                    evac(n)
            for s in range(LRU_OUT_AT, GATE_S_AT):
                split2(s + 1)
            for n in range(S5_TILES):
                act.activation(u[:, n, :], u[:, n, :], ACT.Gelu_apprx_tanh).then_inc(gelued.sem, 1)
            for m in range(NM):
                if m % 2 == 0:
                    split2(GATE_S_AT + m // 2 + 1)
                wait_tile2(act, GATE_S_AT + m // 2, m % 2, before=before2[GATE_S_AT + m // 2])
                act.activation(gs[:, m, :], ps[:, m % 4, :], ACT.Tanh, scale=0.5).then_inc(gs_done.sem, 1)
            for n in range(S5_TILES):
                s = GLU_AT + n // 2
                if n % 2 == 0:
                    split2(s + 1)
                wait_tile2(act, s, 2 * (n % 2) + 1, n=4, before=before2[s])
                if n >= 2:
                    act.wait_ge(ys_done.sem, n - 1)
                act.activation(tmp[:, n % 2, :], ps[:, 5 + 2 * (n % 2), :], ACT.Sigmoid).then_inc(glu_sig.sem, 1)
            for m in range(NM):
                if m % 4 == 0:
                    split2(S5_OUT_AT + m // 4 + 1)
                act.wait_ge(gates_added.sem, m + 1)
                act.activation(mix_hi[:, m, :], gl[:, m, :], ACT.Copy).then_inc(merged_hi.sem, 1)
            for idx, m in enumerate(ORD):
                s = OUT_AT + idx // 2
                if idx % 2 == 0:
                    split2(s + 1)
                wait_tile2(act, s, idx % 2, before=before2[s])
                if idx == 0:
                    act.wait_ge(merged.sem, NM)
                act.activation(gs[:, m, :], ps[:, m, :], ACT.Copy, scale=0.5).then_inc(o_copied.sem, 1)
                square(DEPTH, 2 * NM, idx, ps[:, m, :], scale=0.5, gather=0)
            split2(PLE_AT + 1)
            inverse_root(DEPTH, NM + 1, 2)
            for m in range(NM):
                act.wait_ge(o_added.sem, m + 1)
                act.activation(h_hi[:, m, :], x[:, m, :], ACT.Copy).then_inc(xs_hi_done.sem, 1)
                wait_tile2(act, PLE_AT, m, n=NM, before=before2[PLE_AT])
                act.activation(gl[:, m, :], ps[:, PLE_BANKS[m], :], ACT.Copy).then_inc(ple_evac.sem, 1)
            for m in range(NM):
                s = PLE_GATE_AT + m // 2
                if m % 2 == 0:
                    split2(s + 1)
                wait_tile2(act, s, m % 2, before=before2[s])
                if m >= 2:
                    act.wait_ge(gate_step.sem, m - 1)
                act.activation(sq[:, m % 2, :], ps[:, PLE_BANKS[m], :], ACT.Sigmoid).then_inc(gate_sig.sem, 1)

        @block.vector
        def _(dve):
            steps = [0]

            def split(layer, s, more=0):
                buf = s % 2
                dve.wait_ge(hi_split.sem, hi_split.at(layer, s + 1) + more)
                dve.tensor_tensor(w_lo[:, buf, :], raw[buf][:], w_hi[:, buf, :].bitcast(F32), ALU.subtract
                                  ).then_inc(lo_split.sem, 1)

            def step(layer, ins):
                steps[0] += 1
                ins.then_inc(dve_step.sem, 1)
                wait(dve, dve_step, layer, steps[0])

            def scale_h(layer, stage):
                norm_no = 3 * layer + stage
                wait(dve, inverted, layer, stage + 1)
                for m in range(NM + 1):
                    if m < NM:
                        if m >= 2:
                            wait(dve, h_done, layer, stage * NM + m - 1)
                        dve.scalar_tensor_tensor(out=tmp[:, m % 2, :], in0=x[:, m, :],
                                                 scalar=gains[:, bass.ds(norm_no * NM + m, 1)], in1=rstd,
                                                 op0=ALU.mult, op1=ALU.mult).then_inc(h_scaled.sem, 1)
                    if m >= 1:
                        wait(dve, h_hi_done, layer, stage * NM + m)
                        dve.tensor_tensor(h_lo[:, m - 1, :], tmp[:, (m - 1) % 2, :], h_hi[:, m - 1, :].bitcast(F32),
                                          ALU.subtract).then_inc(h_done.sem, 1)

            def ffn(layer, f, at):
                with dve.Fori(0, UP_SLOTS // 2) as j:
                    for i in range(2):
                        c = 2 * j + i
                        split(layer, at + i + 1, 2 * j)
                        dve.wait_ge(silued.sem, silued.at(layer, f * NF + 1) + c)
                        dve.wait_ge(cs_out.sem, 16)
                        dve.wait_ge(bias_made.sem, 2 * c + 1)
                        dve.wait_ge(a_done.sem, a_done.at(layer, f * NF + 1) + c)
                        dve.tensor_tensor(atmp, sil[:, i, :], ps[:, 2 * i + 1, :], ALU.mult).then_inc(a_prod.sem, 1)
                        dve.wait_ge(a_prod.sem, a_prod.at(layer, f * NF + 1) + c)
                        dve.tensor_copy(a_hi[:, c, :], atmp).then_inc(a_hi_done.sem, 1)
                        dve.wait_ge(a_hi_done.sem, a_hi_done.at(layer, f * NF + 1) + c)
                        dve.tensor_tensor(a_lo[:, c, :], atmp, a_hi[:, c, :].bitcast(F32), ALU.subtract
                                          ).then_inc(a_done.sem, 1)
                at += UP_SLOTS
                with dve.Fori(0, DOWN_SLOTS // 2) as j:
                    for i in range(2):
                        split(layer, at + i + 1, 2 * j)
                for idx, m in enumerate(ORD):
                    wait_tile(dve, layer, at + DOWN_SLOTS - 1, idx)
                    dve.scalar_tensor_tensor(out=x[:, m, :], in0=ps[:, m, :], scalar=0.5, in1=x[:, m, :],
                                             op0=ALU.mult, op1=ALU.add).then_inc(x_done.sem, 1)
                split(layer, at + DOWN_SLOTS)
                scale_h(layer, 1 if f == 0 else 3)

            def in_products(layer):
                for s in range(7):
                    split(layer, MIX_AT + s + 1)
                    t = 2 * s
                    wait_tile(dve, layer, MIX_AT + s, 0)
                    bank = ps[:, t % 4, :]
                    if t == 0:
                        wait(dve, cs_in, layer, 16)
                        ins = dve.tensor_tensor(k_prod[0:64, :], bank[0:64, :], cs[0:64, 1, :], ALU.mult)
                    elif t < 6:
                        ins = dve.tensor_copy(c_raw[:, t - 1, :], bank)
                    else:
                        ins = dve.tensor_scalar(qk[:, t - 6, :], bank, -SCALE["a" if t < 10 else "c"], None, ALU.mult)
                    ins.then_inc(dve_evac.sem, 1)
                for i in range(2):
                    wait(dve, c_inverted, layer, i + 1)
                for i in range(5):
                    step(layer, dve.scalar_tensor_tensor(
                        out=tmp[:, i % 2, :], in0=c_raw[:, i, :],
                        scalar=gains[:, bass.ds(LOW_RANK_GAINS + 5 * layer + i, 1)],
                        in1=c_rstd[:, 0 if i < 3 else 1, :], op0=ALU.mult, op1=ALU.mult))
                    step(layer, dve.tensor_copy(cn_hi[:, i, :], tmp[:, i % 2, :]))
                    dve.tensor_tensor(cn_lo[:, i, :], tmp[:, i % 2, :], cn_hi[:, i, :].bitcast(F32), ALU.subtract
                                      ).then_inc(c_done.sem, 1)
                split(layer, MIX_AT + 8)
                split(layer, MIX_AT + 9)
                for t in (0, 2):
                    wait_tile(dve, layer, MIX_AT + 8, t)
                    dve.tensor_copy(v_ac[:, t, :], ps[:, t, :]).then_inc(dve_evac.sem, 1)
                for s in (9, 10):
                    split(layer, MIX_AT + s + 1)
                    for i in range(4):
                        wait_tile(dve, layer, MIX_AT + s, i)
                        head = 4 * (s - 9) + i
                        dve.scalar_tensor_tensor(out=q_b[:, head, :], in0=ps[:, i, :], scalar=-SCALE["b"],
                                                 in1=cs[:, head % 2, :], op0=ALU.mult, op1=ALU.mult
                                                 ).then_inc(dve_evac.sem, 1)
                for t in range(NT):
                    wait_tile(dve, layer, MIX_AT + 11, 4 + t)
                    dve.tensor_copy(v_b[:, t, :], ps[:, 4 + t, :]).then_inc(dve_evac.sem, 1)

            def maxes(layer, u):
                wait(dve, score_done, layer, u + 1)
                if u >= 4:
                    wait(dve, exp_done, layer, u - 3)
                if UNITS[u][0] == "b":
                    dve.tensor_reduce(mneg[:, u % 4:u % 4 + 1], ps[:, u % 4, :], AX.X, ALU.min
                                      ).then_inc(max_done.sem, 1)
                    return
                n = BIASED.index(u)
                wait(dve, bias_in[n % 4], layer, 16 * (n // 4 + 1))
                dve.sem_inc(dve_met.sem, 1)
                dve.tensor_tensor_reduce(out=negs[:, u % 4, :], in0=bias_ring[:, n % 4, :], in1=ps[:, u % 4, :],
                                         scale=1.0, scalar=3e38, op0=ALU.add, op1=ALU.min,
                                         accum_out=mneg[:, u % 4:u % 4 + 1]).then_inc(max_done.sem, 1)

            def normalise(layer, u):
                kind, _, c, _ = UNITS[u]
                wait(dve, exp_done, layer, u + 1)
                r = rinv[:, u % 4:u % 4 + 1]
                p = probs[:, u % 4, :]
                step(layer, dve.reciprocal(r, rsum[:, u % 4:u % 4 + 1]))
                if kind != "c":
                    dve.tensor_scalar(p, p, r, None, ALU.mult).then_inc(p_done.sem, 1)
                elif c == 0:
                    step(layer, dve.tensor_scalar(p, p, r, None, ALU.mult))
                else:
                    rl = rinv[:, 4 + u % 4:5 + u % 4]
                    step(layer, dve.tensor_scalar(rl, r, nlam[:, bass.ds(layer, 1)], None, ALU.mult))
                    dve.scalar_tensor_tensor(out=p, in0=p, scalar=rl, in1=probs[:, (u - 1) % 4, :],
                                             op0=ALU.mult, op1=ALU.add).then_inc(p_done.sem, 1)

            def pair_out(layer, pair):
                wait(dve, pv_done, layer, 2 * pair + 2)
                bank = ps[:, 6 + pair % 2, :]
                if pair < 2:
                    dve.tensor_copy(tmp[:, pair, :], bank).then_inc(pv_taken.sem, 1)
                    return
                tile = PAIR_TILE[pair]
                wait(dve, pair_hi, layer, pair - 1)
                dve.tensor_tensor(mix_lo[:, tile, :], bank, mix_hi[:, tile, :].bitcast(F32), ALU.subtract
                                  ).then_inc(pv_taken.sem, 1)

            def attention(layer):
                for u in range(len(UNITS) + 7):
                    if u == len(UNITS) + 3:
                        split(layer, MIX_AT + 12)
                    if u < len(UNITS):
                        maxes(layer, u)
                    if 1 <= u <= len(UNITS):
                        normalise(layer, u - 1)
                    v = TURNS.index(u - 6) if u - 6 in TURNS else 0
                    if v % (2 * NT) == 2 * NT - 1:
                        pair_out(layer, v // (2 * NT))
                    if u == OC_NORM_AT + 3:
                        for i in range(2):
                            wait(dve, oc_inverted, layer, i + 1)
                            step(layer, dve.scalar_tensor_tensor(
                                out=tmp[:, i, :], in0=tmp[:, i, :], scalar=gain_c[:, bass.ds(layer, 1)],
                                in1=sq[:, i, :], op0=ALU.mult, op1=ALU.mult))
                            step(layer, dve.tensor_copy(mix_hi[:, 6 + i, :], tmp[:, i, :]))
                            dve.tensor_tensor(mix_lo[:, 6 + i, :], tmp[:, i, :], mix_hi[:, 6 + i, :].bitcast(F32),
                                              ALU.subtract).then_inc(oc_mixed.sem, 1)

            def out_products(layer):
                for s in range(12, 16):
                    if s < 15:
                        split(layer, MIX_AT + s + 1)
                    for i in range(2):
                        m = ORD[2 * (s - 12) + i]
                        wait_tile(dve, layer, MIX_AT + s, i)
                        dve.tensor_tensor(x[:, m, :], ps[:, m, :], x[:, m, :], ALU.add).then_inc(x_done.sem, 1)
                split(layer, MIX_AT + 16)
                scale_h(layer, 2)

            n_pro = [0]

            def pro(ins):
                n_pro[0] += 1
                ins.then_inc(pro_step.sem, 1)
                dve.wait_ge(pro_step.sem, n_pro[0])

            dve.sem_inc(a_done.sem, 2)
            dve.wait_ge(pos_in.sem, 32)
            pro(dve.tensor_copy(pos_r[:], pos_i[:]))
            dve.tensor_copy(pcol[:], pcol_i[:]).then_inc(pos_done.sem, 1)
            dve.wait_ge(cols_in.sem, 48)
            for l in range(DEPTH):
                for i in range(2):
                    pro(dve.tensor_tensor(tmp[:, 0, 0:DIFF_QK], lamv[:, l, 2 * i, :], lamv[:, l, 2 * i + 1, :], ALU.mult))
                    pro(dve.tensor_reduce(lam_s[:, 2 * i + l:2 * i + l + 1], tmp[:, 0, 0:DIFF_QK], AX.X, ALU.add))
            dve.sem_inc(dve_pro.sem, 1)
            pro(dve.tensor_scalar(rot[:, 0, :], pos_r[:], cols[:, 2:3], None, ALU.mult))
            pro(dve.tensor_scalar(rot[:, 1, :], rot[:, 0, :], 1.0 / (2 * PI), MAGIC, ALU.mult, ALU.add))
            pro(dve.tensor_scalar(rot[:, 1, :], rot[:, 1, :], MAGIC, None, ALU.subtract))
            pro(dve.scalar_tensor_tensor(out=rot[:, 2, :], in0=rot[:, 1, :], scalar=-TURN_HI, in1=rot[:, 0, :],
                                         op0=ALU.mult, op1=ALU.add))
            pro(dve.scalar_tensor_tensor(out=rot[:, 2, :], in0=rot[:, 1, :], scalar=-TURN_LO, in1=rot[:, 2, :],
                                         op0=ALU.mult, op1=ALU.add))
            dve.tensor_scalar(rot[:, 2, :], rot[:, 2, :], PI_DOWN, -PI_DOWN, ALU.min, ALU.max).then_inc(dve_pro.sem, 1)
            dve.wait_ge(act_step.sem, 5)
            for i in range(2):
                mc, ms, mo = (cols[:, 3 + 3 * i + n:4 + 3 * i + n] for n in range(3))
                pro(dve.tensor_scalar(table2[:, i, :], rot[:, 1, :], mc, mo, ALU.mult, ALU.add))
                pro(dve.scalar_tensor_tensor(out=table2[:, i, :], in0=rot[:, 0, :], scalar=ms, in1=table2[:, i, :],
                                             op0=ALU.mult, op1=ALU.add))
            dve.sem_inc(cs_made.sem, 1)
            pro(dve.tensor_tensor(nlam[:], lam_s[:, 6:8], lam_s[:, 4:6], ALU.subtract))
            pro(dve.tensor_tensor(nlam[:], nlam[:], cols[:, 9:11], ALU.subtract))
            pro(dve.tensor_tensor(gain_c[:], gains[:, C_GAINS:C_GAINS + 2], cols[:, 11:13], ALU.mult))
            split(0, 0)
            scale_h(0, 0)
            with dve.Fori(0, DEPTH) as layer:
                ffn(layer, 0, 0)
                in_products(layer)
                attention(layer)
                out_products(layer)
                ffn(layer, 1, FFN2_AT)
            assert steps[0] == DVE_STEPS

            def split2(s):
                if s < SLOTS_2:
                    split(DEPTH, s)

            small = [0]

            def small_step(ins):
                small[0] += 1
                ins.then_inc(d_small.sem, 1)
                dve.wait_ge(d_small.sem, small[0])
                return small[0]

            dve.wait_ge(x_again.sem, NM)
            scale_h(DEPTH, 1)
            dve.memset(lrux[:, :, 0:PAD], 0.0).then_inc(pads_done.sem, 1)
            split2(1)
            sw = [s5w[:, n, :] for n in range(24)]
            re, im, dt, decay, turn, sin, cos = s5p[:, 0, :], s5p[:, 1, :], sw[0], sw[3], sw[5], sw[6], sw[7]
            dve.wait_ge(s5_in.sem, 64)
            dve.wait_ge(a_small.sem, 1)
            small_step(dve.tensor_tensor(sw[1], im, dt, ALU.mult))
            assert small_step(dve.tensor_tensor(sw[2], re, dt, ALU.mult)) == D_DECAY
            small_step(dve.tensor_scalar(sw[1], sw[1], 1.0 / (2 * PI), None, ALU.mult))
            small_step(dve.tensor_scalar(sw[4], sw[1], MAGIC, None, ALU.add))
            small_step(dve.tensor_scalar(sw[4], sw[4], MAGIC, None, ALU.subtract))
            assert small_step(dve.tensor_tensor(turn, sw[1], sw[4], ALU.subtract)) == D_ANGLE
            dve.wait_ge(cols2_in.sem, 16)
            lam = cols2[:, LAM:LAM + LRU_TILES]
            small_step(dve.tensor_scalar(lru_s[:, 2, :], lam, -1.0, None, ALU.mult))
            assert small_step(dve.tensor_tensor(lru_s[:, 0, :], lam, lru_s[:, 2, :], ALU.max)) == D_LAM
            dve.wait_ge(a_small.sem, 6)
            small_step(dve.tensor_scalar(lru_s[:, 1, :], lru_s[:, 1, :], 1.0, None, ALU.add))
            small_step(dve.tensor_tensor(sw[8], decay, cos, ALU.mult))
            small_step(dve.tensor_scalar(sw[8], sw[8], -1.0, None, ALU.add))
            small_step(dve.tensor_tensor(sw[9], decay, sin, ALU.mult))
            small_step(dve.tensor_tensor(sw[10], re, re, ALU.mult))
            small_step(dve.tensor_tensor(sw[11], im, im, ALU.mult))
            small_step(dve.tensor_tensor(sw[10], sw[10], sw[11], ALU.add))
            small_step(dve.reciprocal(sw[10], sw[10]))
            for dst, (x0, y0), (x1, y1), op in ((12, (8, re), (9, im), ALU.add), (13, (9, re), (8, im), ALU.subtract)):
                small_step(dve.tensor_tensor(sw[14], sw[x0], y0, ALU.mult))
                small_step(dve.tensor_tensor(sw[15], sw[x1], y1, ALU.mult))
                small_step(dve.tensor_tensor(sw[14], sw[14], sw[15], op))
                small_step(dve.tensor_tensor(sw[dst], sw[14], sw[10], ALU.mult))
            split2(2)
            z_re, z_im = (sw[n].unsqueeze(2).to_broadcast([P, S5_PAIRS, 32]) for n in (12, 13))
            c_re, c_im = (s5c_in[:, n, :].rearrange("p (g c) -> p g c", c=32) for n in range(2))
            t0, t1 = (s5t[:, n, :].rearrange("p (g c) -> p g c", c=32) for n in range(2))
            small_step(dve.tensor_tensor(t0, c_re, z_re, ALU.mult))
            small_step(dve.tensor_tensor(t1, c_im, z_im, ALU.mult))
            small_step(dve.tensor_tensor(s5c[:, 0, :], s5t[:, 0, :], s5t[:, 1, :], ALU.subtract))
            small_step(dve.tensor_tensor(t0, c_re, z_im, ALU.mult))
            small_step(dve.tensor_tensor(t1, c_im, z_re, ALU.mult))
            small_step(dve.scalar_tensor_tensor(out=s5c[:, 1, :], in0=s5t[:, 0, :], scalar=-1.0, in1=s5t[:, 1, :],
                                                op0=ALU.mult, op1=ALU.subtract))
            dve.wait_ge(a_small.sem, 7)
            small_step(dve.tensor_scalar(lru_s[:, 2, :], lru_s[:, 2, :], 0.0, None, ALU.max))
            small_step(dve.tensor_tensor(lru_s[:, 2, :], lru_s[:, 2, :], lru_s[:, 1, :], ALU.add))
            small_step(dve.tensor_scalar(lru_s[:, 2, :], lru_s[:, 2, :], 4.0, None, ALU.mult))
            small_step(dve.tensor_scalar(cols2[:, B_A:B_A + 2 * LRU_TILES], cols2[:, B_A:B_A + 2 * LRU_TILES], 0.5, None,
                                         ALU.mult))
            assert small_step(dve.tensor_scalar(lru_s[:, 3, :], lru_s[:, 2, :], -1.0, None, ALU.mult)) == D_TABLES
            dve.memset(rsum[:], 0.0).then_inc(s5_ready.sem, 1)

            def count_turns(p):
                if p < S5_PAIRS:
                    if p >= 1:
                        dve.wait_ge(table_d.sem, p)
                    dve.tensor_scalar(turns, tidx[:], turn[:, p:p + 1], MAGIC, ALU.mult, ALU.add
                                      ).then_inc(turned_by.sem, 1)

            def tables(p):
                if p >= S5_PAIRS:
                    return
                dve.wait_ge(whole_turns.sem, p + 1)
                if p >= 1:
                    dve.wait_ge(table_a.sem, 3 * p)
                dve.scalar_tensor_tensor(out=tmp[:, 0, :], in0=tidx[:], scalar=turn[:, p:p + 1], in1=turns,
                                         op0=ALU.mult, op1=ALU.subtract).then_inc(table_d.sem, 1)
                count_turns(p + 1)

            def scans(p):
                t = 4 * (p % 2)
                cos_, sin_ = (cos_sin[p % 2][:, n, :] for n in range(2))
                dve.wait_ge(pre_sum.sem, 2 * (p + 1))
                for n in range(2):
                    dve.tensor_tensor_scan(s5t[:, t + 2 * n + 1, :], decay[:, p:p + 1].to_broadcast([P, T]),
                                           s5t[:, t + 2 * n, :], 0.0, ALU.mult, ALU.add).then_inc(scan_done.sem, 1)
                dve.wait_ge(scan_done.sem, 2 * (p + 1))
                if p >= 1:
                    dve.wait_ge(h_re_done.sem, p)
                dve.tensor_tensor(s5h_re[p % 2], s5t[:, t + 1, :], cos_, ALU.mult).then_inc(post_d.sem, 1)
                dve.tensor_tensor(tmp[:, 1, :], s5t[:, t + 3, :], sin_, ALU.mult).then_inc(post_d.sem, 1)

            def s5_step(p):
                tables(p + 1)
                if 1 <= p <= S5_PAIRS:
                    scans(p - 1)
                if p % 4 == 2 and p >= 6:
                    s5_result(p // 4 - 1)
                if p < S5_PAIRS:
                    t = 4 * (p % 2)
                    cos_, sin_ = (cos_sin[p % 2][:, n, :] for n in range(2))
                    dve.wait_ge(bu_done.sem, p + 1)
                    dve.wait_ge(table_a.sem, 3 * (p + 1))
                    if p >= 2:
                        dve.wait_ge(s5_out.sem, p - 1)
                        dve.wait_ge(h_re_done.sem, p - 1)
                    for n, (bank, by) in enumerate(((4, cos_), (5, sin_), (5, cos_), (4, sin_))):
                        dve.tensor_tensor(s5t[:, t + n, :], ps[:, bank, :], by, ALU.mult).then_inc(pre_done.sem, 1)

            def s5_result(tile):
                dve.wait_ge(s5_out.sem, 4 * (tile + 1))
                dve.scalar_tensor_tensor(out=u[:, tile, :], in0=u[:, tile, :],
                                         scalar=cols2[:, D_SKIP + tile:D_SKIP + tile + 1],
                                         in1=ps[:, 6 + tile % 2, :], op0=ALU.mult, op1=ALU.add).then_inc(s5_y.sem, 1)

            def conv(q):
                c = lru_t[q % 3][0]
                if q == 0:
                    dve.wait_ge(pads_done.sem, 1)
                    dve.wait_ge(s5_out.sem, S5_PAIRS)
                    dve.wait_ge(post_d.sem, 2 * S5_PAIRS)
                if q >= 3:
                    dve.wait_ge(lru_b.sem, q - 2)
                dve.wait_ge(evac2.sem, 2 * LRU_X_AT + q + 1)
                w = [cols2[:, CONV_W + LRU_TILES * n + q:CONV_W + LRU_TILES * n + q + 1] for n in range(CONV)]
                dve.tensor_scalar(c, lrux[:, q, 0:T], w[0], cols2[:, CONV_B + q:CONV_B + q + 1], ALU.mult, ALU.add
                                  ).then_inc(conv_step.sem, 1)
                for n in range(1, CONV):
                    dve.wait_ge(conv_step.sem, 3 * q + n)
                    dve.scalar_tensor_tensor(out=c, in0=lrux[:, q, n:n + T], scalar=w[n], in1=c,
                                             op0=ALU.mult, op1=ALU.add
                                             ).then_inc((conv_step if n < CONV - 1 else conv_done).sem, 1)

            def lru_step(q):
                if 0 <= q - 1 < LRU_TILES:
                    a_, bank = lru_t[(q - 1) % 3][2], ps[:, 4 + 2 * ((q - 1) % 2), :]
                    dve.wait_ge(lru_a.sem, 4 * q)
                    dve.tensor_tensor(bank, a_, a_, ALU.mult).then_inc(lru_square.sem, 1)
                    dve.wait_ge(lru_square.sem, q)
                    dve.scalar_tensor_tensor(out=lru_r[q - 1], in0=bank, scalar=1.0, in1=lru_r[q - 1],
                                             op0=ALU.add, op1=ALU.mult).then_inc(lru_rest.sem, 1)
                if q == 0:
                    conv(0)
                if q + 1 < LRU_TILES:
                    conv(q + 1)
                if 0 <= q - 1 < LRU_TILES:
                    c, i_, a_ = lru_t[(q - 1) % 3]
                    dve.wait_ge(lru_rc.sem, q)
                    dve.scalar_tensor_tensor(out=i_, in0=i_, scalar=1.0, in1=c, op0=ALU.add, op1=ALU.mult
                                             ).then_inc(lru_b.sem, 1)
                    dve.wait_ge(lru_b.sem, q)
                    dve.tensor_tensor_scan(lru_r[q - 1], a_, i_, 0.0, ALU.mult, ALU.add).then_inc(lru_scan.sem, 1)

            def y_parts(k):
                dve.wait_ge(lru_y.sem, max(k + 1, 4))
                if k >= 2:
                    if k % 2 == 0:
                        dve.wait_ge(yl_used.sem, k // 2)
                    else:
                        wait(dve, slot_used, DEPTH, LRU_OUT_AT + k // 2)
                dve.tensor_copy(yl_hi[:, k % 2, :], slg[:, k, :]).then_inc(yl_hi_done.sem, 1)
                dve.wait_ge(yl_hi_done.sem, k + 1)
                dve.tensor_tensor(yl_lo[:, k % 2, :], slg[:, k, :], yl_hi[:, k % 2, :].bitcast(F32), ALU.subtract
                                  ).then_inc(yl_done.sem, 1)

            last = 2 * LRU_OUT_AT - 1
            for kind, n in first_products():
                if kind == "tile" and n == S5_FROM - 2:
                    count_turns(0)
                    tables(0)
                if kind == "tile" and n % 2 == 1 and 5 <= n < last:
                    split2(n // 2 + 1)
                if kind == "tile" and n == last - 1:
                    split2(LRU_OUT_AT)
                    for k in range(2):
                        y_parts(k)
                if kind == "s5":
                    s5_step(n)
                elif kind == "lru":
                    lru_step(n)
            for k in range(2, LRU_TILES):
                if k % 2 == 0:
                    split2(LRU_OUT_AT + k // 2)
                y_parts(k)
            split2(GATE_S_AT)
            for m in range(NM):
                wait_tile2(dve, GATE_S_AT - 1, m, n=NM, before=before2[GATE_S_AT - 1])
                dve.scalar_tensor_tensor(out=gl[:, m, :], in0=gl[:, m, :], scalar=1.0, in1=ps[:, m, :],
                                         op0=ALU.add, op1=ALU.mult).then_inc(z_taken.sem, 1)
            for s in range(GATE_S_AT, GLU_AT - 1):
                split2(s + 1)
                if s == GATE_S_AT:
                    for n in range(S5_TILES):
                        dve.wait_ge(gelued.sem, n + 1)
                        dve.tensor_copy(g_hi[:, n, :], u[:, n, :]).then_inc(g_hi_done.sem, 1)
                        dve.wait_ge(g_hi_done.sem, n + 1)
                        dve.tensor_tensor(g_lo[:, n, :], u[:, n, :], g_hi[:, n, :].bitcast(F32), ALU.subtract
                                          ).then_inc(g_done.sem, 1)
                if s == GATE_S_AT + 1:
                    dve.wait_ge(p_in.sem, 16)
                    dve.wait_ge(g_done.sem, S5_TILES)
                    for n in range(PLE_TILES):
                        dve.tensor_copy(p_hi[:, n, :], wide[:, n, :]).then_inc(p_split.sem, 1)
                        dve.wait_ge(p_split.sem, 2 * n + 1)
                        dve.tensor_tensor(p_lo[:, n, :], wide[:, n, :], p_hi[:, n, :].bitcast(F32), ALU.subtract
                                          ).then_inc(p_split.sem, 1)
            split2(GLU_AT)
            for n in range(S5_TILES):
                if n % 2 == 0:
                    split2(GLU_AT + n // 2 + 1)
                t = tmp[:, n % 2, :]
                dve.wait_ge(glu_sig.sem, n + 1)
                dve.tensor_tensor(t, ps[:, 4 + 2 * (n % 2), :], t, ALU.mult).then_inc(glu_prod.sem, 1)
                dve.wait_ge(glu_prod.sem, n + 1)
                dve.tensor_tensor(t, t, ssg[:, n, :], ALU.mult).then_inc(glu_step.sem, 1)
                dve.wait_ge(glu_step.sem, 2 * n + 1)
                dve.tensor_copy(ys_hi[:, n, :], t).then_inc(glu_step.sem, 1)
                dve.wait_ge(glu_step.sem, 2 * n + 2)
                dve.tensor_tensor(ys_lo[:, n, :], t, ys_hi[:, n, :].bitcast(F32), ALU.subtract).then_inc(ys_done.sem, 1)
            for m in range(NM + 1):
                if m < NM:
                    s = S5_OUT_AT + m // 4
                    if m % 4 == 0:
                        split2(s + 1)
                    wait_tile2(dve, s, m % 4, n=4, before=before2[s])
                    dve.scalar_tensor_tensor(out=gs[:, m, :], in0=gs[:, m, :], scalar=1.0, in1=ps[:, m % 4, :],
                                             op0=ALU.add, op1=ALU.mult).then_inc(bs_taken.sem, 1)
                    dve.wait_ge(bs_taken.sem, m + 1)
                    dve.tensor_tensor(gl[:, m, :], gl[:, m, :], gs[:, m, :], ALU.add).then_inc(gates_added.sem, 1)
                if m >= 1:
                    dve.wait_ge(merged_hi.sem, m)
                    dve.tensor_tensor(mix_lo[:, m - 1, :], gl[:, m - 1, :], mix_hi[:, m - 1, :].bitcast(F32),
                                      ALU.subtract).then_inc(merged.sem, 1)
            for s in range(OUT_AT, OUT_AT + 4):
                split2(s + 1)
            split2(PLE_AT + 1)
            wait(dve, inverted, DEPTH, 3)
            for m in range(NM + 1):
                if m < NM:
                    t = tmp[:, m % 2, :]
                    dve.scalar_tensor_tensor(out=t, in0=gs[:, m, :], scalar=cols2[:, G_POST + m:G_POST + m + 1],
                                             in1=rstd, op0=ALU.mult, op1=ALU.mult).then_inc(o_step.sem, 1)
                    dve.wait_ge(o_step.sem, m + 1)
                    dve.tensor_tensor(x[:, m, :], x[:, m, :], t, ALU.add).then_inc(o_added.sem, 1)
                if m >= 1:
                    dve.wait_ge(xs_hi_done.sem, m)
                    dve.tensor_tensor(h_lo[:, m - 1, :], x[:, m - 1, :], h_hi[:, m - 1, :].bitcast(F32), ALU.subtract
                                      ).then_inc(xs_done.sem, 1)
            for m in range(NM):
                s = PLE_GATE_AT + m // 2
                if m % 2 == 0:
                    split2(s + 1)
                dve.wait_ge(gate_sig.sem, m + 1)
                dve.wait_ge(ple_evac.sem, m + 1)
                dve.tensor_tensor(gl[:, m, :], gl[:, m, :], sq[:, m % 2, :], ALU.mult).then_inc(gate_step.sem, 1)
                dve.wait_ge(gate_step.sem, m + 1)
                dve.tensor_tensor(x[:, m, :], x[:, m, :], gl[:, m, :], ALU.add).then_inc(fin.sem, 1)


def _blocks(w):
    k, m = w.shape
    return w.reshape(k // P, P, m // P, P).transpose(0, 2, 1, 3)


def _slot(blocks):
    out = np.zeros((P, SLOT), np.float32)
    n = len(blocks)
    out[:, :n * P] = np.asarray(blocks).transpose(1, 0, 2).reshape(P, n * P)
    return out


def _ffn_slots(gate, up, down):
    g, u, d = _blocks(gate), _blocks(up), _blocks(down)
    for c in range(NF):
        yield _slot([w[k, c] for k in range(NM) for w in (g, u)])
    for j in range(DOWN_SLOTS):
        yield _slot([d[2 * j + n, m] for m in ORD for n in range(2)])


def _mixer_slots(w_in, w_uq, w_ukv, w_out):
    cols = np.arange(w_in.shape[1] + 1)
    a0, b0, c0 = 0, A_COLS, A_COLS + B_COLS
    kpe = b0 + Q_LORA + KV_LORA
    swap = list(range(16, 32)) + list(range(16))
    w_pad = np.concatenate([w_in, np.zeros((D, 1), np.float32)], axis=1)
    zero = [w_in.shape[1]] * 64
    tile = lambda at: list(range(at, at + P))
    tiles = [[kpe + i for i in range(32)] + [kpe + i for i in swap] + zero]
    tiles += [tile(b0 + P * i) for i in range(5)]
    for i in range(2):
        tiles += [tile(a0 + P * i), tile(a0 + 256 + P * i)]
    for i in range(2):
        tiles += [tile(c0 + P * i), tile(c0 + 256 + P * i)]
    b = [_blocks(w_pad[:, t])[:, 0] for t in tiles]
    for s in range(7):
        yield _slot(list(b[2 * s]) + list(b[2 * s + 1]))
    v = _blocks(w_in[:, list(range(a0 + 512, a0 + 768)) + list(range(c0 + 512, c0 + 768))])
    for s in range(2):
        yield _slot([v[4 * s + k, n] for k in range(4) for n in range(4)])
    heads = []
    for h in range(HEADS_B):
        q = h * (NOPE + ROPE)
        nope, rope = [q + i for i in range(NOPE)], [q + NOPE + i for i in range(ROPE)]
        swapped = [q + NOPE + i for i in swap]
        heads.append(_blocks(w_uq[:, nope + rope + swapped if h % 2 == 0 else rope + swapped + nope])[:, 0])
    for s in range(2):
        yield _slot([heads[4 * s + i][k] for i in range(4) for k in range(3)])
    keys = _blocks(w_ukv[:, [h * 128 + i for h in range(HEADS_B) for i in range(64)]])
    vals = _blocks(w_ukv[:, [h * 128 + 64 + i for h in range(HEADS_B) for i in range(64)]])
    yield _slot([keys[k, i] for i in range(4) for k in range(2)] + [vals[k, n] for k in range(2) for n in range(4)])
    o = _blocks(w_out)
    for j in range(4):
        yield _slot([o[k, ORD[2 * j + i]] for i in range(2) for k in range(NM)])


def _second_slots(g):
    w_in = _blocks(g["w_in_2"][0])
    x_s, g_s, x_l = range(0, 4), range(4, 8), range(8, 18)
    g_l, gate_s, gate_l = range(18, 28), range(28, 36), range(36, 44)

    def pairs(w, tiles):
        tiles = list(tiles)
        return [_slot([w[k, t] for t in tiles[i:i + 2] for k in range(NM)]) for i in range(0, len(tiles), 2)]

    out = []
    for tiles in (x_s, g_l, g_s, x_l, gate_l):
        out += pairs(w_in, tiles)
    w_bl, w_glu, w_bs = _blocks(g["w_bl_2"][0]), _blocks(g["w_glu_2"][0]), _blocks(g["w_bs_2"][0])
    out += [_slot([w_bl[2 * s + n, m] for n in range(2) for m in range(NM)]) for s in range(LRU_TILES // 2)]
    out += pairs(w_in, gate_s)
    out += [_slot([w_glu[k, t] for i in (0, 1) for t in (2 * s + i, 4 + 2 * s + i) for k in range(4)]) for s in range(2)]
    out += [_slot([w_bs[k, 4 * s + i] for i in range(4) for k in range(4)]) for s in range(2)]
    out += pairs(_blocks(g["w_out_2"][0]), ORD)
    w_ple = _blocks(g["w_ple_2"][0])
    out += [_slot([w_ple[k, m] for m in range(NM) for k in range(2)])]
    out += pairs(_blocks(g["w_ple_gate_2"][0]), range(NM))
    assert len(out) == SLOTS_2
    return out


def _s5_arrays(g):
    by_state = lambda v: v.reshape(S5_PAIRS, 2 * STATES).T
    log_dt = np.repeat(g["s5_log_dt_2"][0][:, None], STATES, axis=1)
    s5p = np.stack([by_state(v) for v in (g["s5_a_re_2"][0], g["s5_a_im_2"][0], log_dt)], axis=1)
    s5b = np.zeros((P, S5_TILES, 2, P), np.float32)
    s5c = np.zeros((P, 2, S5_PAIRS, 32), np.float32)
    for ri, part in enumerate(("re", "im")):
        b, c = g[f"s5_b_{part}_2"][0], g[f"s5_c_{part}_2"][0]
        for group in range(2 * S5_PAIRS):
            pair, n = divmod(group, 2)
            row = 32 * (pair % 4) + 16 * n
            s5b[row:row + 16, pair // 4, ri, 64 * n:64 * n + 64] = b[group].T
            s5c[64 * n:64 * n + 64, ri, pair, 16 * n:16 * n + 16] = c[group].T
    return s5p, s5b, s5c.reshape(P, 2, S5_PAIRS * 32)


def _columns(v):
    return v.reshape(-1, P).T


def _constants():
    cols = np.zeros((P, 16), np.float32)
    p = np.arange(P)
    cols[:, 0] = EPS
    cols[:, 1] = PI / 2
    half = ROPE // 2
    inv = (np.float32(10000.0) ** (-np.arange(half, dtype=np.float32) / np.float32(half))).astype(np.float32)
    cols[:, 2] = inv[p % half]
    sign = np.where(p % 32 < 16, -1.0, 1.0)
    for i, group in enumerate(((2, 2, 0, 1), (0, 1, 2, 2))):
        kind = np.array(group)[p // 32]
        cols[:, 3 + 3 * i] = kind == 0
        cols[:, 4 + 3 * i] = (kind == 1) * sign
        cols[:, 5 + 3 * i] = kind == 2
    cols[:, 9:11] = LAM_INIT
    cols[:, 13], cols[:, 14] = 1e-30, -MAGIC
    cols[:, 11:13] = 1.0 - np.array(LAM_INIT)
    mats = np.zeros((P, 4, P), np.float32)
    mats[:, 0] = np.eye(P)
    mats[:, 1] = 1.0
    mats[:, 2] = p[:, None] // 64 == p[None, :] // 64
    mats[:, 3] = p[:, None] % 32 == p[None, :] % 32
    d = np.abs(p[:, None] - np.arange(2 * T - P)[None, :] + (T - P))
    count = (d <= 64).astype(int) + ((d % 4 == 0) & (d <= 256)) + ((d % 16 == 0) & (d <= 1024))
    reach = np.where(count > 0, -np.log(np.maximum(count, 1)), FAR).astype(np.float32)
    return cols, mats, reach


def kernel(**inputs):
    import concourse.bacc as bacc
    from concourse.bass_utils import run_bass_kernel_spmd

    g = {k: np.ascontiguousarray(v) for k, v in inputs.items()}
    slots = []
    for l in range(DEPTH):
        slots += _ffn_slots(g["ffn1_w_gate"][l], g["ffn1_w_up"][l], g["ffn1_w_down"][l])
        slots += _mixer_slots(g["w_in"][l], g["mla_w_uq"][l], g["mla_w_ukv"][l], g["w_out"][l])
        slots += _ffn_slots(g["ffn2_w_gate"][l], g["ffn2_w_up"][l], g["ffn2_w_down"][l])
    slots += _second_slots(g)
    cols, mats, reach = _constants()
    gains = [_columns(v) for l in range(DEPTH) for v in (g["ffn1_norm"][l], g["mix_norm"][l], g["ffn2_norm"][l])]
    gains += [_columns(g["final_norm"]), _columns(g["g_pre_2"][0])]
    for l in range(DEPTH):
        gains += [_columns(g["mla_q_norm"][l]), _columns(g["mla_kv_norm"][l])]
    gains += [np.tile(g["diff_head_norm"][l], 2)[:, None] for l in range(DEPTH)]
    s5p, s5b, s5c = _s5_arrays(g)
    lam = np.stack([g["diff_lambda_" + n] for n in ("q1", "k1", "q2", "k2")], axis=1)
    arrays = {
        "x": g["x"][0].T.reshape(NM, P, T).transpose(1, 0, 2),
        "stream": np.stack(slots),
        "cols": cols, "mats": mats, "reach": reach,
        "gains": np.concatenate(gains, axis=1),
        "lamv": np.broadcast_to(lam[None], (P,) + lam.shape),
        "s5p": s5p, "s5b": s5b, "s5c": s5c,
        "tidx": np.broadcast_to(np.arange(T, dtype=np.float32) - T // 2, (P, T)),
        "w_lru": np.stack([g["lru_w_a_2"][0], g["lru_w_x_2"][0]], axis=1).reshape(2 * LRU_TILES, P, P).transpose(1, 0, 2),
        "p": g["p_2"][0, 0].T.reshape(PLE_TILES, P, T).transpose(1, 0, 2),
        "cols2": np.concatenate([_columns(v) for v in (
            g["s5_d_2"][0], *g["conv_w_2"][0], g["conv_b_2"][0], g["lru_b_a_2"][0], g["lru_b_x_2"][0],
            g["lru_lambda_2"][0], g["g_post_2"][0])], axis=1),
        "pos": g["positions"][0], "pos_col": g["positions"][0].reshape(NT, P).T,
    }
    arrays = {k: np.ascontiguousarray(v) for k, v in arrays.items()}
    nc = bacc.Bacc("TRN2", target_bir_lowering=False, num_devices=1)
    aps = {k: nc.dram_tensor("in_" + k, v.shape, mybir.dt.from_np(v.dtype), kind="ExternalInput").ap()
           for k, v in arrays.items()}
    aps["out"] = nc.dram_tensor("out", (P, NM, T), F32, kind="ExternalOutput").ap()
    build(nc, aps)
    r = run_bass_kernel_spmd(nc, [{"in_" + k: v for k, v in arrays.items()}], core_ids=[0])
    return r.results[0]["out"].transpose(1, 0, 2).reshape(1, D, T).transpose(0, 2, 1)
```
